# Optimizing a Trainium2 kernel written in Bass

```python
import math
import jax, jax.numpy as jnp
from jax import lax
import numpy as np

D_MODEL = 1024
BATCH = 1
SEQ = 256
DEPTH = 2

D_FF = 2816
HEAD_DIM = 64
N_Q_HEADS = 16
N_KV_HEADS = 2
Q_PER_KV = N_Q_HEADS // N_KV_HEADS
ATTN_WIDTH = N_Q_HEADS * HEAD_DIM
KV_WIDTH = N_KV_HEADS * HEAD_DIM
WINDOW = 128
ATTN_BLOCK = 128
SGU_CHUNK = 128
SGU_GROUPS = 8
SGU_GROUP_CH = 128
SGU_WIDTH = SGU_GROUPS * SGU_GROUP_CH
IN_SPLIT_SIZES = (ATTN_WIDTH, KV_WIDTH, KV_WIDTH, SGU_WIDTH, SGU_WIDTH, D_MODEL, D_MODEL)
IN_WIDTH = sum(IN_SPLIT_SIZES)
IN_SPLIT_POINTS = tuple(int(p) for p in np.cumsum(IN_SPLIT_SIZES)[:-1])

RMS_EPS = 1e-6
LN_EPS = 1e-5
MASK_VALUE = -1e30


def rms_norm(x, g):
    x32 = x.astype(jnp.float32)
    y = x32 * lax.rsqrt(jnp.mean(x32 * x32, axis=-1, keepdims=True) + RMS_EPS)
    return (y * g.astype(jnp.float32)).astype(x.dtype)

def layer_norm(x, g, b):
    x32 = x.astype(jnp.float32)
    mu = jnp.mean(x32, axis=-1, keepdims=True)
    xc = x32 - mu
    y = xc * lax.rsqrt(jnp.mean(xc * xc, axis=-1, keepdims=True) + LN_EPS)
    return (y * g.astype(jnp.float32) + b.astype(jnp.float32)).astype(x.dtype)

def swiglu(x, w1, w2):
    g, u = jnp.split(x @ w1, 2, axis=-1)
    return (jax.nn.silu(g) * u) @ w2

def sliding_window_attention(q, k, v, sinks):
    B, S, _ = q.shape
    nb = S // ATTN_BLOCK
    qb = q.reshape(B, nb, ATTN_BLOCK, N_KV_HEADS, Q_PER_KV, HEAD_DIM).astype(jnp.float32)
    kb = k.reshape(B, nb, ATTN_BLOCK, N_KV_HEADS, HEAD_DIM)
    vb = v.reshape(B, nb, ATTN_BLOCK, N_KV_HEADS, HEAD_DIM)
    kpad = jnp.zeros_like(kb[:, :1])
    vpad = jnp.zeros_like(vb[:, :1])
    k2 = jnp.concatenate([jnp.concatenate([kpad, kb[:, :-1]], axis=1), kb], axis=2).astype(jnp.float32)
    v2 = jnp.concatenate([jnp.concatenate([vpad, vb[:, :-1]], axis=1), vb], axis=2).astype(jnp.float32)
    scale = 1.0 / math.sqrt(HEAD_DIM)
    scores = jnp.einsum('bnqgrd,bnkgd->bngrqk', qb, k2) * scale
    qi = jnp.arange(ATTN_BLOCK)[:, None]
    kj = jnp.arange(2 * ATTN_BLOCK)[None, :]
    rel = qi + ATTN_BLOCK - kj
    band = (rel >= 0) & (rel < WINDOW)
    blk = jnp.arange(nb)[:, None, None]
    valid = band[None] & ((blk > 0) | (kj[None] >= ATTN_BLOCK))
    scores = jnp.where(valid[None, :, None, None], scores, MASK_VALUE)
    sink = sinks.astype(jnp.float32).reshape(1, 1, N_KV_HEADS, Q_PER_KV, 1)
    m = jnp.maximum(scores.max(axis=-1), sink)
    p = jnp.exp(scores - m[..., None])
    probs = p / (p.sum(axis=-1) + jnp.exp(sink - m))[..., None]
    out = jnp.einsum('bngrqk,bnkgd->bnqgrd', probs, v2)
    return out.reshape(B, S, ATTN_WIDTH).astype(q.dtype)

def spatial_gating(u, v, ln_g, ln_b, w_s, b_s):
    B, S, _ = u.shape
    nc = S // SGU_CHUNK
    vn = layer_norm(v, ln_g, ln_b).reshape(B, nc, SGU_CHUNK, SGU_GROUPS, SGU_GROUP_CH)
    causal = jnp.tril(jnp.ones((SGU_CHUNK, SGU_CHUNK), dtype=bool))
    w = jnp.where(causal[None], w_s, jnp.zeros_like(w_s))
    s = jnp.einsum('gts,bnsgc->bntgc', w, vn) + b_s.T[None, None, :, :, None]
    return u * s.reshape(B, S, SGU_WIDTH)

def first_inputs(seed: int = 0) -> dict:
    key = jax.random.key(seed)
    ks = iter(jax.random.split(key, 32))
    f32 = jnp.float32

    def nrm(shape, fan_in, scale=1.0):
        return jax.random.normal(next(ks), shape, f32) * (scale * fan_in ** -0.5)

    def gain(shape):
        return 1.0 + 0.05 * jax.random.normal(next(ks), shape, f32)

    L, D = DEPTH, D_MODEL
    return {
        "x": jax.random.normal(next(ks), (BATCH, SEQ, D), f32),
        "ffn1_pre_g": gain((L, D)),
        "ffn1_w1": nrm((L, D, 2 * D_FF), D),
        "ffn1_w2": nrm((L, D_FF, D), D_FF),
        "ffn1_post_g": gain((L, D)),
        "mix_pre_g": gain((L, D)),
        "w_in": nrm((L, D, IN_WIDTH), D),
        "attn_sinks": 0.5 * jax.random.normal(next(ks), (L, N_Q_HEADS), f32),
        "sgu_ln_g": gain((L, SGU_WIDTH)),
        "sgu_ln_b": 0.02 * jax.random.normal(next(ks), (L, SGU_WIDTH), f32),
        "sgu_w": nrm((L, SGU_GROUPS, SGU_CHUNK, SGU_CHUNK), SGU_CHUNK, 0.5),
        "sgu_b": gain((L, SGU_GROUPS, SGU_CHUNK)),
        "w_attn_branch": nrm((L, ATTN_WIDTH, D), ATTN_WIDTH),
        "w_sgu_branch": nrm((L, SGU_WIDTH, D), SGU_WIDTH),
        "w_out": nrm((L, D, D), D),
        "mix_post_g": gain((L, D)),
        "ffn2_pre_g": gain((L, D)),
        "ffn2_w1": nrm((L, D, 2 * D_FF), D),
        "ffn2_w2": nrm((L, D_FF, D), D_FF),
        "ffn2_post_g": gain((L, D)),
    }

def first_block(x, ffn1_pre_g, ffn1_w1, ffn1_w2, ffn1_post_g, mix_pre_g, w_in, attn_sinks,
              sgu_ln_g, sgu_ln_b, sgu_w, sgu_b, w_attn_branch, w_sgu_branch, w_out, mix_post_g,
              ffn2_pre_g, ffn2_w1, ffn2_w2, ffn2_post_g):
    for l in range(DEPTH):
        h = rms_norm(x, ffn1_pre_g[l])
        x = x + 0.5 * rms_norm(swiglu(h, ffn1_w1[l], ffn1_w2[l]), ffn1_post_g[l])

        h = rms_norm(x, mix_pre_g[l])
        z = h @ w_in[l]
        q, k, v, u_s, v_s, g_a, g_b = jnp.split(z, IN_SPLIT_POINTS, axis=-1)
        y_attn = sliding_window_attention(q, k, v, attn_sinks[l])
        y_sgu = spatial_gating(jax.nn.gelu(u_s, approximate=False), jax.nn.gelu(v_s, approximate=False),
                               sgu_ln_g[l], sgu_ln_b[l], sgu_w[l], sgu_b[l])
        merged = (jax.nn.sigmoid(g_a) * (y_attn @ w_attn_branch[l])
                  + jax.nn.sigmoid(g_b) * (y_sgu @ w_sgu_branch[l]))
        x = x + rms_norm(merged @ w_out[l], mix_post_g[l])

        h = rms_norm(x, ffn2_pre_g[l])
        x = x + 0.5 * rms_norm(swiglu(h, ffn2_w1[l], ffn2_w2[l]), ffn2_post_g[l])
    return x


N_MEM = 256
MIX_WIDTH = D_MODEL
N_GROUPS = 4
GROUP_WIDTH = MIX_WIDTH // N_GROUPS
CONF_WIDTH = 31
HG_HEADS = 4
HG_DK = GROUP_WIDTH // HG_HEADS
HG_DV = GROUP_WIDTH // HG_HEADS
HG_CHUNK = 64
SC_WIDTH = 3
MLA_HEADS = 4
MLA_NOPE = 64
MLA_ROPE = 32
MLA_V = GROUP_WIDTH // MLA_HEADS
MLA_Q_LORA = 256
MLA_KV_LORA = 128
ROPE_BASE = 10000.0
Q_BLOCK = 128
XA_HEADS = 4
XA_HEAD_DIM = 64
D_FF_2 = -(-8 * D_MODEL // (3 * 256)) * 256
EPS = 1e-6
A_COLS = 2 * GROUP_WIDTH
B_COLS = 5 * GROUP_WIDTH
C_COLS = 3 * GROUP_WIDTH
D_COLS = MLA_Q_LORA + MLA_KV_LORA + MLA_ROPE
IN_COLS = A_COLS + B_COLS + C_COLS + D_COLS
SPLITS = [A_COLS, A_COLS + B_COLS, A_COLS + B_COLS + C_COLS]


def rms_norm_2(x, g):
    xf = x.astype(jnp.float32)
    y = xf * lax.rsqrt(jnp.mean(xf * xf, axis=-1, keepdims=True) + EPS)
    return (y * g.astype(jnp.float32)).astype(x.dtype)

def layer_norm_2(x, g, b):
    xf = x.astype(jnp.float32)
    mu = jnp.mean(xf, axis=-1, keepdims=True)
    xc = xf - mu
    y = xc * lax.rsqrt(jnp.mean(xc * xc, axis=-1, keepdims=True) + EPS)
    return (y * g.astype(jnp.float32) + b.astype(jnp.float32)).astype(x.dtype)

def depthwise_conv(x, w, b):
    c = x.shape[-1]
    y = lax.conv_general_dilated(x, w[:, None, :].astype(x.dtype), window_strides=(1,),
                                 padding='SAME', dimension_numbers=('NWC', 'WIO', 'NWC'),
                                 feature_group_count=c)
    return y + b.astype(x.dtype)

def rope_tables(positions):
    inv = ROPE_BASE ** (-jnp.arange(0, MLA_ROPE, 2, dtype=jnp.float32) / MLA_ROPE)
    ang = positions.astype(jnp.float32)[..., None] * inv
    return jnp.cos(ang)[:, :, None, :], jnp.sin(ang)[:, :, None, :]

def apply_rope(x, cos, sin):
    x1, x2 = jnp.split(x, 2, axis=-1)
    return jnp.concatenate([x1 * cos - x2 * sin, x2 * cos + x1 * sin], axis=-1).astype(x.dtype)

def blocked_attention(q, k, v):
    b, s, h, d = q.shape
    scale = d ** -0.5
    qb = q.reshape(b, s // Q_BLOCK, Q_BLOCK, h, d).transpose(1, 0, 2, 3, 4)

    def one_block(qblk):
        sc = jnp.einsum('bqhd,bkhd->bhqk', qblk, k).astype(jnp.float32) * scale
        p = jax.nn.softmax(sc, axis=-1)
        return jnp.einsum('bhqk,bkhe->bqhe', p.astype(v.dtype), v)

    out = lax.map(one_block, qb)
    return out.transpose(1, 0, 2, 3, 4).reshape(b, s, h, v.shape[-1])

def conformer_conv(ua, dw_w, dw_b, ln_g, ln_b):
    a, gate = jnp.split(ua, 2, axis=-1)
    h = a * jax.nn.sigmoid(gate)
    h = depthwise_conv(h, dw_w, dw_b)
    h = layer_norm_2(h, ln_g, ln_b)
    return jax.nn.silu(h)

def hgrn2_bidir(ub, lb_fwd, lb_bwd, onorm_g):
    b, s, _ = ub.shape
    f32 = jnp.float32
    q, zf, zb, v, g = jnp.split(ub, 5, axis=-1)

    def log_forget(z, lb):
        zf32 = z.astype(f32)
        return jnp.log(jax.nn.sigmoid(zf32) + lb * jax.nn.sigmoid(-zf32))

    rev = lambda t: t[:, ::-1]
    logf = jnp.stack([log_forget(zf, lb_fwd), log_forget(rev(zb), lb_bwd)])
    qd = jnp.stack([q, rev(q)]).astype(f32)
    vd = jnp.stack([v, rev(v)]).astype(f32)
    n_chunks = s // HG_CHUNK

    def to_chunks(t, d):
        return t.reshape(2, b, n_chunks, HG_CHUNK, HG_HEADS, d).transpose(2, 0, 1, 4, 3, 5)

    mask = jnp.tril(jnp.ones((HG_CHUNK, HG_CHUNK), dtype=f32))[..., None]

    def step(state, inp):
        qc, lfc, vc = inp
        bcum = jnp.cumsum(lfc, axis=-2)
        kc = -jnp.expm1(lfc)
        o_inter = jnp.einsum('zbhcd,zbhde->zbhce', qc * jnp.exp(bcum), state)
        diff = bcum[..., :, None, :] - bcum[..., None, :, :]
        decay = jnp.exp(diff * mask) * mask
        attn = jnp.sum(qc[..., :, None, :] * kc[..., None, :, :] * decay, axis=-1)
        o_intra = jnp.einsum('zbhts,zbhse->zbhte', attn, vc)
        blast = bcum[..., -1:, :]
        new_state = jnp.exp(blast[..., 0, :])[..., :, None] * state + \
            jnp.einsum('zbhsd,zbhse->zbhde', kc * jnp.exp(blast - bcum), vc)
        return new_state, o_inter + o_intra

    init = jnp.zeros((2, b, HG_HEADS, HG_DK, HG_DV), f32)
    _, ys = lax.scan(step, init, (to_chunks(qd, HG_DK), to_chunks(logf, HG_DK), to_chunks(vd, HG_DV)))
    ys = ys.transpose(1, 2, 0, 4, 3, 5).reshape(2, b, s, HG_HEADS, HG_DV)
    o = ys[0] + ys[1][:, ::-1]
    o = rms_norm_2(o, onorm_g.reshape(HG_HEADS, HG_DV)) * \
        jax.nn.silu(g.astype(f32)).reshape(b, s, HG_HEADS, HG_DV)
    return o.reshape(b, s, GROUP_WIDTH).astype(ub.dtype)

def short_gated_conv(uc, dw_w, dw_b):
    gb, gc, xin = jnp.split(uc, 3, axis=-1)
    return gb * depthwise_conv(gc * xin, dw_w, dw_b)

def mla(ud, cos, sin, qa_g, wuq, kva_g, wukv, qn_g, kn_g):
    b, s, _ = ud.shape
    cq, ckv, kr = jnp.split(ud, [MLA_Q_LORA, MLA_Q_LORA + MLA_KV_LORA], axis=-1)
    q = (rms_norm_2(cq, qa_g) @ wuq).reshape(b, s, MLA_HEADS, MLA_NOPE + MLA_ROPE)
    kv = (rms_norm_2(ckv, kva_g) @ wukv).reshape(b, s, MLA_HEADS, MLA_NOPE + MLA_V)
    k_nope, v = jnp.split(kv, [MLA_NOPE], axis=-1)
    k = jnp.concatenate([k_nope, jnp.broadcast_to(kr[:, :, None, :], (b, s, MLA_HEADS, MLA_ROPE))], axis=-1)
    q = rms_norm_2(q, qn_g)
    k = rms_norm_2(k, kn_g)
    q = jnp.concatenate([q[..., :MLA_NOPE], apply_rope(q[..., MLA_NOPE:], cos, sin)], axis=-1)
    k = jnp.concatenate([k[..., :MLA_NOPE], apply_rope(k[..., MLA_NOPE:], cos, sin)], axis=-1)
    return blocked_attention(q, k, v).reshape(b, s, MLA_HEADS * MLA_V)

def second_inputs(seed: int = 0) -> dict:
    key = jax.random.key(seed)
    ks = iter(jax.random.split(key, 40))
    L = DEPTH
    f32 = jnp.float32

    def nrm(shape, fan_in):
        return jax.random.normal(next(ks), shape, f32) * fan_in ** -0.5

    def gain(shape):
        return 1.0 + 0.01 * jax.random.normal(next(ks), shape, f32)

    def bias(shape):
        return 0.01 * jax.random.normal(next(ks), shape, f32)

    x = jax.random.normal(next(ks), (BATCH, SEQ, D_MODEL), f32)
    mem = jax.random.normal(next(ks), (BATCH, N_MEM, D_MODEL), f32)
    positions = jnp.arange(SEQ, dtype=jnp.int32)[None, :] + \
        jax.random.randint(next(ks), (BATCH, 1), 0, 1024, dtype=jnp.int32)
    return {
        "x": x,
        "mem": mem,
        "positions": positions,
        "g_mix": gain((L, D_MODEL)),
        "w_in": nrm((L, D_MODEL, IN_COLS), D_MODEL),
        "a_dw_w": nrm((L, CONF_WIDTH, GROUP_WIDTH), CONF_WIDTH),
        "a_dw_b": bias((L, GROUP_WIDTH)),
        "a_ln_g": gain((L, GROUP_WIDTH)),
        "a_ln_b": bias((L, GROUP_WIDTH)),
        "h_gamma": 0.5 * jax.random.normal(next(ks), (2, L, GROUP_WIDTH), f32),
        "h_onorm_g": gain((L, GROUP_WIDTH)),
        "c_dw_w": nrm((L, SC_WIDTH, GROUP_WIDTH), SC_WIDTH),
        "c_dw_b": bias((L, GROUP_WIDTH)),
        "m_qa_g": gain((L, MLA_Q_LORA)),
        "m_wuq": nrm((L, MLA_Q_LORA, MLA_HEADS * (MLA_NOPE + MLA_ROPE)), MLA_Q_LORA),
        "m_kva_g": gain((L, MLA_KV_LORA)),
        "m_wukv": nrm((L, MLA_KV_LORA, MLA_HEADS * (MLA_NOPE + MLA_V)), MLA_KV_LORA),
        "m_qn_g": gain((L, MLA_NOPE + MLA_ROPE)),
        "m_kn_g": gain((L, MLA_NOPE + MLA_ROPE)),
        "g_branch": gain((L, MIX_WIDTH)),
        "w_out": nrm((L, MIX_WIDTH, D_MODEL), MIX_WIDTH),
        "g_xq": gain((L, D_MODEL)),
        "g_mem": gain((L, D_MODEL)),
        "x_wq": nrm((L, D_MODEL, XA_HEADS * XA_HEAD_DIM), D_MODEL),
        "x_wkv": nrm((L, D_MODEL, 2 * XA_HEADS * XA_HEAD_DIM), D_MODEL),
        "x_qn_g": gain((L, XA_HEAD_DIM)),
        "x_kn_g": gain((L, XA_HEAD_DIM)),
        "x_wo": nrm((L, XA_HEADS * XA_HEAD_DIM, D_MODEL), XA_HEADS * XA_HEAD_DIM),
        "g_ffn": gain((L, D_MODEL)),
        "f_w13": nrm((L, D_MODEL, 2 * D_FF_2), D_MODEL),
        "f_w2": nrm((L, D_FF_2, D_MODEL), D_FF_2),
    }

def second_block(x, mem, positions, g_mix, w_in, a_dw_w, a_dw_b, a_ln_g, a_ln_b, h_gamma, h_onorm_g,
              c_dw_w, c_dw_b, m_qa_g, m_wuq, m_kva_g, m_wukv, m_qn_g, m_kn_g, g_branch, w_out,
              g_xq, g_mem, x_wq, x_wkv, x_qn_g, x_kn_g, x_wo, g_ffn, f_w13, f_w2):
    b, s, _ = x.shape
    n_mem = mem.shape[1]
    cos, sin = rope_tables(positions)
    p = jax.nn.softmax(h_gamma.astype(jnp.float32), axis=1)
    lower = jnp.cumsum(p, axis=1) - p[:, :1]
    for l in range(DEPTH):
        n = rms_norm_2(x, g_mix[l])
        u = n @ w_in[l]
        ua, ub, uc, ud = jnp.split(u, SPLITS, axis=-1)
        y_a = conformer_conv(ua, a_dw_w[l], a_dw_b[l], a_ln_g[l], a_ln_b[l])
        y_b = hgrn2_bidir(ub, lower[0, l], lower[1, l], h_onorm_g[l])
        y_c = short_gated_conv(uc, c_dw_w[l], c_dw_b[l])
        y_d = mla(ud, cos, sin, m_qa_g[l], m_wuq[l], m_kva_g[l], m_wukv[l], m_qn_g[l], m_kn_g[l])
        cat = jnp.concatenate([y_a, y_b, y_c, y_d], axis=-1).reshape(b, s, N_GROUPS, GROUP_WIDTH)
        cat = rms_norm_2(cat, g_branch[l].reshape(N_GROUPS, GROUP_WIDTH)).reshape(b, s, MIX_WIDTH)
        x = x + cat @ w_out[l]
        hq = rms_norm_2(x, g_xq[l])
        mn = rms_norm_2(mem, g_mem[l])
        q = (hq @ x_wq[l]).reshape(b, s, XA_HEADS, XA_HEAD_DIM)
        kv = (mn @ x_wkv[l]).reshape(b, n_mem, XA_HEADS, 2 * XA_HEAD_DIM)
        k, v = jnp.split(kv, 2, axis=-1)
        q = rms_norm_2(q, x_qn_g[l])
        k = rms_norm_2(k, x_kn_g[l])
        o = blocked_attention(q, k, v).reshape(b, s, XA_HEADS * XA_HEAD_DIM)
        x = x + o @ x_wo[l]
        h = rms_norm_2(x, g_ffn[l])
        a1, a3 = jnp.split(h @ f_w13[l], 2, axis=-1)
        x = x + (jax.nn.silu(a1) * a3) @ f_w2[l]
    return x


def setup_inputs(seed=0):
    out = dict(first_inputs(seed))
    for name, value in second_inputs(seed + 1).items():
        if name != "x":
            out[name + "_2"] = value
    return out


def reference(
    x, ffn1_pre_g, ffn1_w1, ffn1_w2, ffn1_post_g, mix_pre_g, w_in, attn_sinks, sgu_ln_g,
    sgu_ln_b, sgu_w, sgu_b, w_attn_branch, w_sgu_branch, w_out, mix_post_g, ffn2_pre_g, ffn2_w1,
    ffn2_w2, ffn2_post_g, mem_2, positions_2, g_mix_2, w_in_2, a_dw_w_2, a_dw_b_2, a_ln_g_2,
    a_ln_b_2, h_gamma_2, h_onorm_g_2, c_dw_w_2, c_dw_b_2, m_qa_g_2, m_wuq_2, m_kva_g_2,
    m_wukv_2, m_qn_g_2, m_kn_g_2, g_branch_2, w_out_2, g_xq_2, g_mem_2, x_wq_2, x_wkv_2,
    x_qn_g_2, x_kn_g_2, x_wo_2, g_ffn_2, f_w13_2, f_w2_2,
):
    x = first_block(
        x, ffn1_pre_g, ffn1_w1, ffn1_w2, ffn1_post_g, mix_pre_g, w_in, attn_sinks, sgu_ln_g,
        sgu_ln_b, sgu_w, sgu_b, w_attn_branch, w_sgu_branch, w_out, mix_post_g, ffn2_pre_g,
        ffn2_w1, ffn2_w2, ffn2_post_g,
    )
    return second_block(
        x, mem_2, positions_2, g_mix_2, w_in_2, a_dw_w_2, a_dw_b_2, a_ln_g_2, a_ln_b_2,
        h_gamma_2, h_onorm_g_2, c_dw_w_2, c_dw_b_2, m_qa_g_2, m_wuq_2, m_kva_g_2, m_wukv_2,
        m_qn_g_2, m_kn_g_2, g_branch_2, w_out_2, g_xq_2, g_mem_2, x_wq_2, x_wkv_2, x_qn_g_2,
        x_kn_g_2, x_wo_2, g_ffn_2, f_w13_2, f_w2_2,
    )


_drawn_inputs = setup_inputs


def setup_inputs(seed=0):
    import zlib

    import numpy as np

    out = dict(_drawn_inputs(seed))
    spreads = {}
    factors = {'attn_sinks': 3.644,
     'sgu_ln_g': 2.894,
     'sgu_ln_b': 7.043,
     'g_mix_2': 4.994,
     'a_dw_b_2': 8.0,
     'a_ln_g_2': 8.0,
     'a_ln_b_2': 8.0,
     'h_onorm_g_2': 8.0,
     'c_dw_b_2': 8.0,
     'm_qa_g_2': 8.0,
     'm_kva_g_2': 8.0,
     'm_qn_g_2': 8.0,
     'm_kn_g_2': 8.0,
     'g_branch_2': 8.0,
     'g_xq_2': 8.0,
     'g_mem_2': 8.0,
     'x_qn_g_2': 8.0,
     'x_kn_g_2': 8.0,
     'g_ffn_2': 8.0}
    for name, (base, spread) in spreads.items():
        noise = np.random.default_rng([zlib.crc32(name.encode()), seed]).standard_normal(out[name].shape)
        drawn = base * np.exp(spread * noise) if base else spread * noise
        out[name] = __import__('jax').numpy.asarray(drawn.astype(out[name].dtype))
    for name, factor in factors.items():
        out[name] = (out[name] * factor).astype(out[name].dtype)
    return out
```

```python
from contextlib import ExitStack

import numpy as np
import concourse.bass as bass
from concourse import mybir

P = 128
F32 = mybir.dt.float32
F32R = mybir.dt.float32r
BF16 = mybir.dt.bfloat16
I32 = mybir.dt.int32
ACT = mybir.ActivationFunctionType
ALU = mybir.AluOpType
AX_X = mybir.AxisListType.X

DEPTH = 2
SEQ = 256
TT = SEQ // P
D = 1024
KT = D // P
D_FF = 2816
COLS = 256
FF_STEPS = D_FF // COLS
SLOTS = 3
BLOCK = KT * COLS
BANK = 512
RMS_EPS = 1e-6
LN_EPS = 1e-5


class Events:

    def __init__(self, known):
        self.known, self.table = known, {}

    def new_layer(self, layer):
        self.layer = layer
        self.count = dict.fromkeys(("pe", "act", "dve", "pool"), 0)

    def one(self, engine, name):
        self.count[engine] += 1
        assert (self.layer, name) not in self.table, name
        self.table[self.layer, name] = (engine, self.count[engine])
        return 1

    def at(self, name):
        return self.known[self.layer, name][1] if self.known else 1

    def last(self, engine):
        return self.count[engine]

    def when(self, c, name):
        engine, value = self.known[self.layer, name] if self.known else ("act", 1)
        return {"pe": c.pe_done, "act": c.act_done, "dve": c.dve_done, "pool": c.pool_done}[engine], value


class Core:
    pass


def allocate(nc, ctx, dram, known):
    c = Core()
    c.nc, c.dram = nc, dram

    def sb(name, shape, dt=F32):
        return ctx.enter_context(nc.sbuf_tensor(name, shape, dt))

    def sem(name):
        return ctx.enter_context(nc.semaphore(name))

    c.stage = [sb(f"stage{s}", [P, BLOCK]) for s in range(SLOTS)]
    c.w_hi = [sb(f"w_hi{s}", [P, BLOCK], F32R) for s in range(SLOTS)]
    c.w_lo = [sb(f"w_lo{s}", [P, BLOCK], F32R) for s in range(SLOTS)]
    c.x = sb("x", [P, TT, D])
    c.xn = sb("xn", [P, TT, D])
    c.aT_hi = sb("aT_hi", [P, KT, SEQ], F32R)
    c.aT_lo = sb("aT_lo", [P, KT, SEQ], F32R)
    c.gain_pre = sb("gain_pre", [P, D])
    c.gain_post = sb("gain_post", [P, D])
    c.squares = sb("squares", [P, D], BF16)
    c.ident = sb("ident", [P, P])
    c.zeros = sb("zeros", [P, BANK], BF16)
    c.half_power = sb("half_power", [P, 16])
    c.ss = sb("ss", [P, 16])
    c.rstd = sb("rstd", [P, 16])

    c.psum = ctx.enter_context(nc.psum_tensor("psum", [P, 8, BANK], F32))
    c.weight_loaded = [sem(f"weight_loaded{s}") for s in range(SLOTS)]
    c.w_hi_ready = [sem(f"w_hi_ready{s}") for s in range(SLOTS)]
    c.w_lo_ready = [sem(f"w_lo_ready{s}") for s in range(SLOTS)]
    c.w_used = [sem(f"w_used{s}") for s in range(SLOTS)]
    c.silu_done = sem("silu_done")
    c.hidden_ready = sem("hidden_ready")
    c.hidden_hi_ready = sem("hidden_hi_ready")
    c.hidden_lo_ready = sem("hidden_lo_ready")
    c.up_kv_loaded, c.mem_loaded = sem("up_kv_loaded"), sem("mem_loaded")
    c.pe_done, c.act_done, c.dve_done, c.pool_done = (sem(f"{e}_done") for e in ("pe", "act", "dve", "pool"))
    c.params = {}
    for name in ("gain_pre", "gain_post", "small"):
        c.params[name] = sem(f"{name}_loaded")
    c.loads = c.loads_before = dict.fromkeys(c.params, 0)
    c.ev = Events(known)
    c.per_layer_sems = [*c.weight_loaded, *c.w_hi_ready, *c.w_lo_ready, *c.w_used, c.silu_done, c.hidden_ready,
                        c.hidden_hi_ready, c.hidden_lo_ready, c.up_kv_loaded, c.mem_loaded,
                        c.pe_done, c.act_done, c.dve_done, c.pool_done]
    c.setup_done = sem("setup_done")
    c.x_loaded = sem("x_loaded")
    c.stored = sem("stored")
    return c


def start_layers(c, **loads):
    c.loads_before = {name: c.loads_before[name] + DEPTH * c.loads[name] for name in c.params}
    c.loads = loads


def wait_params(c, eng, name, count):
    eng.wait_ge(c.params[name], c.layer * (16 * c.loads[name]) + 16 * (c.loads_before[name] + count))


def clear_layer(c):
    with c.nc.Block() as block:
        @block.sync
        def _(sp):
            for s in c.per_layer_sems:
                sp.sem_clear(s)



def columns(c, name, layer, first, width=COLS):
    return c.dram[name].rearrange("l (kt p) n -> l p kt n", p=P)[layer][:, :, bass.ds(first, width)]


def rows(c, name, layer, pair):
    return c.dram[name].rearrange("l (b kt p) n -> l b p kt n", kt=2, p=P)[layer][bass.ds(pair, 1)].rearrange(
        "o p kt n -> p (o kt) n")


def as_columns(t):
    return t[:].rearrange("p (kt n) -> p kt n", kt=KT)


def as_rows(t):
    return t[:].rearrange("p (kt n) -> p kt n", kt=2)


def load_weights(c, sp, slot, use, first_use, source, tile=None):
    if not first_use:
        sp.wait_ge(c.w_lo_ready[slot], use)
    if tile is None:
        tile = as_columns(c.stage[slot]) if source.shape[1] == KT else as_rows(c.stage[slot])
    sp.dma_start(tile, source).then_inc(c.weight_loaded[slot], 16)


def split_hi(c, act, slot, use, first_use, size=BLOCK):
    act.wait_ge(c.weight_loaded[slot], 16 * use + 16)
    if not first_use:
        act.wait_ge(c.w_used[slot], use)
    act.activation(c.w_hi[slot][:, 0:size], c.stage[slot][:, 0:size], ACT.Copy).then_inc(c.w_hi_ready[slot], 1)


def split_lo(c, dve, slot, use, size=BLOCK):
    dve.wait_ge(c.w_hi_ready[slot], use + 1)
    dve.tensor_tensor(c.w_lo[slot][:, 0:size], c.stage[slot][:, 0:size], c.w_hi[slot][:, 0:size].bitcast(F32),
                      ALU.subtract).then_inc(c.w_lo_ready[slot], 1)


def hi(c, act, n, size=BLOCK):
    split_hi(c, act, n % SLOTS, n // SLOTS, n < SLOTS, size)


def lo(c, dve, n, size=BLOCK):
    split_lo(c, dve, n % SLOTS, n // SLOTS, size)



def features_by_tokens(pe, out, w_hi, w_lo, a_hi, a_lo, kts=KT):
    for f in range(2):
        cols = slice(f * P, (f + 1) * P)
        for kt in range(kts):
            pe.matmul(out[:, f, :], w_hi[:, kt, cols], a_hi[:, kt, :], start=(kt == 0), stop=False)
            pe.matmul(out[:, f, :], w_hi[:, kt, cols], a_lo[:, kt, :], start=False, stop=False)
            last = pe.matmul(out[:, f, :], w_lo[:, kt, cols], a_hi[:, kt, :], start=False, stop=(kt == kts - 1))
    return last


def tokens_by_features(pe, outs, w_hi, w_lo, a_hi, a_lo, kts, start=True, stop=True):
    for t in range(len(outs)):
        toks = slice(t * P, (t + 1) * P)
        for kt in range(kts):
            pe.matmul(outs[t], a_hi[:, kt, toks], w_hi[:, kt, :], start=start and kt == 0, stop=False,
                      skip_group_check=True)
            pe.matmul(outs[t], a_hi[:, kt, toks], w_lo[:, kt, :], start=False, stop=False, skip_group_check=True)
            last = pe.matmul(outs[t], a_lo[:, kt, toks], w_hi[:, kt, :], start=False,
                             stop=stop and kt == kts - 1, skip_group_check=True)
    return last


def row_block(c, pe, w_hi, w_lo, a_hi, a_lo, start=False, last_of=None):
    for t in range(TT):
        for half in range(2):
            cols = slice(half * BANK, (half + 1) * BANK)
            last = tokens_by_features(pe, [c.psum[:, 4 + 2 * t + half, :]], w_hi[:, :, cols], w_lo[:, :, cols],
                                      a_hi[:, :, t * P:(t + 1) * P], a_lo[:, :, t * P:(t + 1) * P], 2, start,
                                      last_of is not None)
        if last_of is not None and t == 0:
            last.then_inc(c.pe_done, c.ev.one("pe", f"{last_of}.acc0"))
    return last


def wait_weights(c, pe, n):
    pe.wait_ge(c.w_lo_ready[n % SLOTS], n // SLOTS + 1)



def rms_factors(c, pool, tag, cols, width, eps, quarter=1.0):
    ev = c.ev
    n = cols.stop - cols.start
    pool.tensor_scalar(c.rstd[:, cols], c.ss[:, cols], quarter / width, quarter * eps, ALU.mult, ALU.add)\
        .then_inc(c.pool_done, ev.one("pool", f"{tag}.meansq"))
    pool.wait_ge(c.pool_done, ev.at(f"{tag}.meansq"))
    pool.tensor_tensor(c.rstd[:, cols], c.rstd[:, cols], c.half_power[:, 0:n], ALU.pow)\
        .then_inc(c.pool_done, ev.one("pool", f"{tag}.rstd"))


def transpose_split(c, block, tag, source, tiles, after_pe, banks, dst_hi=None, dst_lo=None, kt0=0, after_out=()):
    ev = c.ev
    dst_hi = c.aT_hi if dst_hi is None else dst_hi
    dst_lo = c.aT_lo if dst_lo is None else dst_lo
    groups = [(t, k, min(4, tiles - k)) for t in range(TT) for k in range(0, tiles, 4)]

    @block.tensor
    def _(pe):
        for i, (t, k, m) in enumerate(groups):
            for name in after_pe[t]:
                pe.wait_ge(*ev.when(c, name))
            if i >= len(banks):
                pe.wait_ge(c.dve_done, ev.at(f"{tag}.lo{i - len(banks)}"))
            for j in range(m):
                last = pe.transpose(c.psum[:, banks[i % len(banks)], j * P:(j + 1) * P],
                                    source[:, t, (k + j) * P:(k + j + 1) * P], c.ident[:])
            last.then_inc(c.pe_done, ev.one("pe", f"{tag}.turned{i}"))

    def places(i):
        t, k, m = groups[i]
        src = c.psum[:, banks[i % len(banks)], 0:m * P].rearrange("p (k t) -> p k t", k=m)
        return src, slice(kt0 + k, kt0 + k + m), slice(t * P, (t + 1) * P)

    @block.scalar
    def _(act):
        for i in range(len(groups)):
            src, ks, ts = places(i)
            act.wait_ge(c.pe_done, ev.at(f"{tag}.turned{i}"))
            for name in after_out:
                act.wait_ge(*ev.when(c, name))
            act.activation(dst_hi[:, ks, ts], src, ACT.Copy).then_inc(c.act_done, ev.one("act", f"{tag}.hi{i}"))

    @block.vector
    def _(dve):
        for i in range(len(groups)):
            src, ks, ts = places(i)
            dve.wait_ge(c.act_done, ev.at(f"{tag}.hi{i}"))
            dve.tensor_tensor(dst_lo[:, ks, ts], src, dst_hi[:, ks, ts].bitcast(F32), ALU.subtract)\
                .then_inc(c.dve_done, ev.one("dve", f"{tag}.lo{i}"))
    return f"{tag}.lo{len(groups) - 1}"


def pre_norm(c, block, tag, x_ready, gain_count, x=None, gain=None, dst=None, banks=(0, 1, 2, 3)):
    ev = c.ev
    x = c.x if x is None else x
    which, gain = ("gain_pre", c.gain_pre) if gain is None else gain
    dst = (c.aT_hi, c.aT_lo) if dst is None else dst
    xn = c.xn

    @block.scalar
    def _(act):
        for t in range(TT):
            for name in x_ready[t]:
                act.wait_ge(*ev.when(c, name))
            if ev.last("act"):
                act.wait_ge(c.act_done, ev.last("act"))
            act.activation(c.squares[:], x[:, t, :], ACT.Square, accum_out=c.ss[:, t:t + 1])\
                .then_inc(c.act_done, ev.one("act", f"{tag}.ss{t}"))

    @block.gpsimd
    def _(pool):
        for t in range(TT):
            pool.wait_ge(c.act_done, ev.at(f"{tag}.ss{t}"))
            rms_factors(c, pool, f"{tag}.{t}", slice(t, t + 1), D, RMS_EPS)

    @block.vector
    def _(dve):
        wait_params(c, dve, which, gain_count)
        for t in range(TT):
            for name in x_ready[t]:
                dve.wait_ge(*ev.when(c, name))
            dve.wait_ge(c.pool_done, ev.at(f"{tag}.{t}.rstd"))
            dve.scalar_tensor_tensor(xn[:, t, :], x[:, t, :], c.rstd[:, t:t + 1], gain[:],
                                     ALU.mult, ALU.mult).then_inc(c.dve_done, ev.one("dve", f"{tag}.xn{t}"))

    return transpose_split(c, block, tag, xn, KT, [[f"{tag}.xn{t}"] for t in range(TT)], banks, *dst)


def post_norm(c, block, tag, uses, gain_count, half, slot=2):
    ev = c.ev

    def acc(t):
        return c.psum[:, 4 + 2 * t:6 + 2 * t, :].rearrange("p b n -> p (b n)")

    @block.scalar
    def _(act):
        for t in range(TT):
            if t == 0:
                act.wait_ge(c.pe_done, ev.at(f"{tag}.acc0"))
            else:
                act.wait_ge(c.w_used[slot], uses)
            if ev.last("act"):
                act.wait_ge(c.act_done, ev.last("act"))
            act.activation(c.squares[:], acc(t), ACT.Square, accum_out=c.ss[:, t:t + 1])\
                .then_inc(c.act_done, ev.one("act", f"{tag}.post_ss{t}"))

    @block.gpsimd
    def _(pool):
        for t in range(TT):
            pool.wait_ge(c.act_done, ev.at(f"{tag}.post_ss{t}"))
            rms_factors(c, pool, f"{tag}.post{t}", slice(t, t + 1), D, RMS_EPS, 4.0 if half else 1.0)

    @block.vector
    def _(dve):
        wait_params(c, dve, "gain_post", gain_count)
        for t in range(TT):
            dve.wait_ge(c.act_done, ev.at(f"{tag}.post_ss{t}"))
            dve.tensor_tensor(c.xn[:, t, :], acc(t), c.gain_post[:], ALU.mult)\
                .then_inc(c.dve_done, ev.one("dve", f"{tag}.step{t}"))
            dve.wait_ge(c.dve_done, ev.at(f"{tag}.step{t}"))
            dve.wait_ge(c.pool_done, ev.at(f"{tag}.post{t}.rstd"))
            dve.scalar_tensor_tensor(c.x[:, t, :], c.xn[:, t, :], c.rstd[:, t:t + 1], c.x[:, t, :],
                                     ALU.mult, ALU.add).then_inc(c.dve_done, ev.one("dve", f"{tag}.x{t}"))


def add_to_x(c, block, tag, uses, slot=2):
    ev = c.ev

    @block.vector
    def _(dve):
        for t in range(TT):
            if t == 0:
                dve.wait_ge(c.pe_done, ev.at(f"{tag}.acc0"))
            else:
                dve.wait_ge(c.w_used[slot], uses)
            acc = c.psum[:, 4 + 2 * t:6 + 2 * t, :].rearrange("p b n -> p (b n)")
            dve.tensor_tensor(c.x[:, t, :], c.x[:, t, :], acc, ALU.add)\
                .then_inc(c.dve_done, ev.one("dve", f"{tag}.x{t}"))


def split_next(c, block, n):
    @block.scalar
    def _(act):
        hi(c, act, n)

    @block.vector
    def _(dve):
        lo(c, dve, n)


def ffn(c, block, tag, w1, w2, layer, use0, hidden0, aT_ready, last_stage, acc_free):
    nc, ev = c.nc, c.ev
    first = use0 == 0
    with ExitStack() as tiles:
        def sb(name, shape, dt=F32):
            return tiles.enter_context(nc.sbuf_tensor(f"{tag}_{name}", shape, dt))
        silu = sb("silu", [P, 2, SEQ])
        hidden = sb("hidden", [P, 2, SEQ])
        h_hi = [sb(f"h_hi{p}", [P, 2, SEQ], F32R) for p in range(2)]
        h_lo = [sb(f"h_lo{p}", [P, 2, SEQ], F32R) for p in range(2)]

    def bank(p, which):
        return c.psum[:, 2 * p + which, :].rearrange("p (f t) -> p f t", f=2)

    pairs = (FF_STEPS - 3) // 2

    @block.sync
    def _(sp):
        def up(j, first_use=False):
            load_weights(c, sp, 0, use0 + j, first_use, columns(c, w1, layer, COLS * j))
            load_weights(c, sp, 1, use0 + j, first_use, columns(c, w1, layer, COLS * j + D_FF))

        def down(j, first_use=False):
            load_weights(c, sp, 2, use0 + j, first_use, rows(c, w2, layer, j))
        up(0, first)
        down(0, first)
        up(1)
        with sp.Fori(0, FF_STEPS - 2) as i:
            up(i + 2)
            down(i + 1)
        down(FF_STEPS - 1)

    @block.scalar
    def _(act):
        def step(j, p, split_down, split_up, j_is_first=False):
            if split_up:
                split_hi(c, act, 0, use0 + j + 1, False)
            act.wait_ge(c.w_used[0], use0 + j + 1)
            if not j_is_first:
                act.wait_ge(c.hidden_ready, hidden0 + j)
            act.activation(silu[:], bank(p, 0), ACT.Silu).then_inc(c.silu_done, 1)
            if split_up:
                split_hi(c, act, 1, use0 + j + 1, False)
            act.wait_ge(c.hidden_ready, hidden0 + j + 1)
            act.activation(h_hi[p][:], hidden[:], ACT.Copy).then_inc(c.hidden_hi_ready, 1)
            if split_down:
                split_hi(c, act, 2, use0 + j, False)
        if first:
            for n in range(SLOTS):
                split_hi(c, act, n, 0, True)
        step(0, 0, False, True, True)
        with act.Fori(0, pairs) as i:
            step(2 * i + 1, 1, True, True)
            step(2 * i + 2, 0, True, True)
        step(FF_STEPS - 2, 1, True, True)
        j = FF_STEPS - 1
        act.wait_ge(c.w_used[0], use0 + j + 1)
        act.wait_ge(c.hidden_ready, hidden0 + j)
        act.activation(silu[:], bank(0, 0), ACT.Silu).then_inc(c.silu_done, 1)
        split_hi(c, act, 2, use0 + j, False)
        act.wait_ge(c.hidden_ready, hidden0 + j + 1)
        act.activation(h_hi[0][:], hidden[:], ACT.Copy).then_inc(c.hidden_hi_ready, 1)
        if not last_stage:
            split_hi(c, act, 0, use0 + j + 1, False)
            split_hi(c, act, 1, use0 + j + 1, False)

    @block.vector
    def _(dve):
        def step(j, p, split_down, split_up, j_is_first=False):
            if split_up:
                split_lo(c, dve, 0, use0 + j + 1)
            dve.wait_ge(c.silu_done, hidden0 + j + 1)
            if not j_is_first:
                dve.wait_ge(c.hidden_lo_ready, hidden0 + j)
            dve.wait_ge(c.w_used[1], use0 + j + 1)
            dve.tensor_tensor(hidden[:], silu[:], bank(p, 1), ALU.mult).then_inc(c.hidden_ready, 1)
            if split_up:
                split_lo(c, dve, 1, use0 + j + 1)
            dve.wait_ge(c.hidden_hi_ready, hidden0 + j + 1)
            dve.tensor_tensor(h_lo[p][:], hidden[:], h_hi[p][:].bitcast(F32), ALU.subtract)\
               .then_inc(c.hidden_lo_ready, 1)
            if split_down:
                split_lo(c, dve, 2, use0 + j)
        if first:
            for n in range(SLOTS):
                split_lo(c, dve, n, 0)
        step(0, 0, False, True, True)
        with dve.Fori(0, pairs) as i:
            step(2 * i + 1, 1, True, True)
            step(2 * i + 2, 0, True, True)
        step(FF_STEPS - 2, 1, True, True)
        j = FF_STEPS - 1
        split_lo(c, dve, 2, use0 + j)
        dve.wait_ge(c.silu_done, hidden0 + j + 1)
        dve.wait_ge(c.hidden_lo_ready, hidden0 + j)
        dve.wait_ge(c.w_used[1], use0 + j + 1)
        dve.tensor_tensor(hidden[:], silu[:], bank(0, 1), ALU.mult).then_inc(c.hidden_ready, 1)
        dve.wait_ge(c.hidden_hi_ready, hidden0 + j + 1)
        dve.tensor_tensor(h_lo[0][:], hidden[:], h_hi[0][:].bitcast(F32), ALU.subtract)           .then_inc(c.hidden_lo_ready, 1)
        if not last_stage:
            split_lo(c, dve, 0, use0 + j + 1)
            split_lo(c, dve, 1, use0 + j + 1)

    @block.tensor
    def _(pe):
        def up(j, p, reused=True):
            if reused:
                pe.wait_ge(c.hidden_lo_ready, hidden0 + j - 1)
            for slot in range(2):
                project(j, p, slot)

        def project(j, p, slot):
            pe.wait_ge(c.w_lo_ready[slot], use0 + j + 1)
            features_by_tokens(pe, bank(p, slot), as_columns(c.w_hi[slot]), as_columns(c.w_lo[slot]),
                               c.aT_hi, c.aT_lo).then_inc(c.w_used[slot], 1)

        def down(j, p, last_of=None):
            pe.wait_ge(c.hidden_lo_ready, hidden0 + j + 1)
            pe.wait_ge(c.w_lo_ready[2], use0 + j + 1)
            row_block(c, pe, as_rows(c.w_hi[2]), as_rows(c.w_lo[2]), h_hi[p], h_lo[p], False, last_of)\
                .then_inc(c.w_used[2], 1)

        for name in acc_free:
            pe.wait_ge(*ev.when(c, name))
        for b in range(4):
            pe.matmul(c.psum[:, 4 + b, :], c.zeros[:, 0:P], c.zeros[:], start=True, stop=False,
                      skip_group_check=True)
        pe.wait_ge(c.dve_done, ev.at(aT_ready))
        up(0, 0, False)
        up(1, 1, False)
        down(0, 0)
        with pe.Fori(0, (FF_STEPS - 3) // 2) as i:
            up(2 * i + 2, 0)
            down(2 * i + 1, 1)
            up(2 * i + 3, 1)
            down(2 * i + 2, 0)
        j = FF_STEPS - 1
        pe.wait_ge(c.hidden_lo_ready, hidden0 + j - 1)
        project(j, 0, 0)
        down(j - 1, 1)
        project(j, 0, 1)
        down(j, 0, tag)



HEADS = 16
KV_HEADS = 2
HEAD_DIM = 64
GROUPS = 8
MASKED = -1e30
MIX1_BLOCKS = 21 + 12


def load_gain(c, pool, which, source, after):
    for name in after:
        pool.wait_ge(*c.ev.when(c, name))
    tile = c.gain_pre if which == "gain_pre" else c.gain_post
    pool.dma_start(tile[:], source.partition_broadcast(P)).then_inc(c.params[which], 16)


def first_block_layer(c, layer, masks):
    nc, ev = c.nc, c.ev
    ev.new_layer("first")
    c.layer = layer
    with nc.Block() as block:
        @block.gpsimd
        def _(pool):
            load_gain(c, pool, "gain_pre", c.dram["ffn1_pre_g"][layer], [])
            load_gain(c, pool, "gain_post", c.dram["ffn1_post_g"][layer], [])
        pre_norm(c, block, "f1", [[], []], 1)

        @block.gpsimd
        def _(pool):
            load_gain(c, pool, "gain_pre", c.dram["mix_pre_g"][layer], ["f1.xn1"])
        ffn(c, block, "f1", "ffn1_w1", "ffn1_w2", layer, 0, 0, "f1.lo3", False, [])
        post_norm(c, block, "f1", FF_STEPS, 1, True)
        pre_norm(c, block, "mix", [["f1.x0"], ["f1.x1"]], 2)

        @block.gpsimd
        def _(pool):
            load_gain(c, pool, "gain_post", c.dram["mix_post_g"][layer], ["f1.step1"])
        split_next(c, block, SLOTS * FF_STEPS + 2)

        @block.gpsimd
        def _(pool):
            load_gain(c, pool, "gain_pre", c.dram["ffn2_pre_g"][layer], ["mix.xn1"])
        mixer_one(c, block, layer, SLOTS * FF_STEPS, masks)
        post_norm(c, block, "mix", FF_STEPS + MIX1_BLOCKS // SLOTS, 2, False)
        pre_norm(c, block, "f2", [["mix.x0"], ["mix.x1"]], 3)

        @block.gpsimd
        def _(pool):
            load_gain(c, pool, "gain_post", c.dram["ffn2_post_g"][layer], ["mix.step1"])
        split_next(c, block, SLOTS * FF_STEPS + MIX1_BLOCKS + 2)
        ffn(c, block, "f2", "ffn2_w1", "ffn2_w2", layer, FF_STEPS + MIX1_BLOCKS // SLOTS, FF_STEPS, "f2.lo3", True,
            ["mix.step1"])
        post_norm(c, block, "f2", 2 * FF_STEPS + MIX1_BLOCKS // SLOTS, 3, True)


def mixer_one(c, block, layer, n0, masks):
    nc, ev, dram = c.nc, c.ev, c.dram
    window_mask, causal_T = masks
    with ExitStack() as tiles:
        def sb(name, shape, dt=F32):
            return tiles.enter_context(nc.sbuf_tensor(f"m_{name}", shape, dt))
        qT = sb("qT", [P, KT, SEQ])
        k_twice = [sb(f"k{g}", [P, SEQ]) for g in range(KV_HEADS)]
        vT = sb("vT", [P, SEQ])
        v = sb("v", [P, TT, P])
        uT = sb("uT", [P, GROUPS, SEQ])
        gateA = sb("gateA", [P, KT, SEQ])
        gateB = sb("gateB", [P, KT, SEQ])
        ysT_hi = sb("ysT_hi", [P, GROUPS, SEQ], F32R)
        ysT_lo = sb("ysT_lo", [P, GROUPS, SEQ], F32R)
        scores = sb("scores", [P, 2, 3 * P])
        probs = sb("probs", [P, 2, 3 * P])
        probsT = sb("probsT", [P, 2, 3 * P])
        neg_max = sb("neg_max", [P, TT, HEADS])
        row_max = sb("row_max", [P, TT, HEADS])
        row_sum = sb("row_sum", [P, TT, HEADS])
        sinks = sb("sinks", [P, HEADS])
        stats = sb("stats", [P, TT, 2, 6])
        mean_var = sb("mean_var", [P, TT, 2])
        sgu_wT = sb("sgu_wT", [P, GROUPS, P])
        sgu_b = sb("sgu_b", [P, GROUPS, P])
    vt = c.xn
    merged = qT
    sgu_w = gateB
    ln_g = gateA[:].rearrange("p k t -> p (k t)")[:, 0:D]
    ln_b = gateA[:].rearrange("p k t -> p (k t)")[:, D:2 * D]
    sgu_w = gateB[:].rearrange("p k t -> p (k t)")[:, 0:GROUPS * P].rearrange("p (g s) -> p g s", g=GROUPS)
    Q0, KV, V0, U0, GA0, GB0, SB0, AB0, WO0 = 0, 4, 5, 9, 13, 17, 21, 25, 29
    first_col = {}
    for i in range(4):
        first_col[Q0 + i] = COLS * i
        first_col[V0 + i] = 2304 + COLS * i
        first_col[U0 + i] = 1280 + COLS * i
        first_col[GA0 + i] = 3328 + COLS * i
        first_col[GB0 + i] = 4352 + COLS * i
    first_col[KV] = 1024

    def bank(b):
        return c.psum[:, b, :]

    def two(b):
        return c.psum[:, b, :].rearrange("p (f t) -> p f t", f=2)

    @block.gpsimd
    def _(pool):
        pool.wait_ge(c.dve_done, ev.at("f1.x1"))
        small = c.params["small"]
        pool.dma_start(sinks[:], dram["attn_sinks"][layer].partition_broadcast(P)).then_inc(small, 16)
        pool.dma_start(ln_g, dram["sgu_ln_g"][layer].partition_broadcast(P)).then_inc(small, 16)
        pool.dma_start(ln_b, dram["sgu_ln_b"][layer].partition_broadcast(P)).then_inc(small, 16)
        pool.dma_start(sgu_b[:], dram["sgu_b"][layer].partition_broadcast(P)).then_inc(small, 16)
        pool.dma_start(sgu_w, dram["sgu_w"].rearrange("l g t s -> l t g s")[layer]).then_inc(small, 16)

    @block.sync
    def _(sp):
        for i in range(21):
            load_weights(c, sp, (n0 + i) % SLOTS, (n0 + i) // SLOTS, False, columns(c, "w_in", layer, first_col[i]))
        for base, name in ((SB0, "w_sgu_branch"), (AB0, "w_attn_branch")):
            for i in range(4):
                n = n0 + base + i
                load_weights(c, sp, n % SLOTS, n // SLOTS, False, columns(c, name, layer, COLS * i))
        for i in range(4):
            n = n0 + WO0 + i
            load_weights(c, sp, n % SLOTS, n // SLOTS, False, rows(c, "w_out", layer, i))

    def scores_bank(h):
        return c.psum[:, 2 + h % 2, 0:3 * P]

    def probsT_bank(h):
        return c.psum[:, 4 + h % 2, 0:3 * P]

    def out_bank(q):
        return c.psum[:, 6 + q % 2, :].rearrange("p (t h e) -> p t h e", t=TT, h=4)

    @block.tensor
    def _(pe):
        pe.wait_ge(c.dve_done, ev.at("mix.lo3"))

        def project(i):
            n = n0 + i
            if i >= 2:
                pe.wait_ge(c.act_done, ev.at(f"blk{i - 2}.out"))
            wait_weights(c, pe, n)
            w_hi, w_lo = as_columns(c.w_hi[n % SLOTS]), as_columns(c.w_lo[n % SLOTS])
            a_hi, a_lo = c.aT_hi, c.aT_lo
            if V0 <= i < U0:
                last = tokens_by_features(pe, [two(i % 2)[:, t, :] for t in range(TT)], w_hi, w_lo, a_hi, a_lo, KT)
            else:
                last = features_by_tokens(pe, two(i % 2), w_hi, w_lo, a_hi, a_lo)
            last.then_inc(c.w_used[n % SLOTS], 1)

        def attend(step):
            for h in range(2 * step, 2 * step + 2):
                if 0 <= h < HEADS:
                    hp = slice((h % 2) * HEAD_DIM, (h % 2 + 1) * HEAD_DIM)
                    if h >= 2:
                        pe.wait_ge(c.dve_done, ev.at(f"masked{h - 2}"))
                    else:
                        pe.wait_ge(c.dve_done, ev.at(f"blk{KV}.k"))
                        pe.wait_ge(c.act_done, ev.at(f"blk{KV}.v"))
                        pe.wait_ge(c.dve_done, ev.at("v.out"))
                    s = scores_bank(h)
                    k = k_twice[h * KV_HEADS // HEADS]
                    pe.matmul(s[:, 0:P], qT[hp, h // 2, 0:P], k[hp, 0:P], start=True, stop=True)
                    pe.matmul(s[:, P:3 * P], qT[hp, h // 2, P:2 * P], k[hp, :], start=True, stop=True)\
                        .then_inc(c.pe_done, ev.one("pe", f"scores{h}"))
            for h in range(2 * step - 2, 2 * step):
                if 0 <= h < HEADS:
                    pe.wait_ge(c.act_done, ev.at(f"probs{h}"))
                    pe.wait_ge(*ev.when(c, f"probsT{h - 2}" if h >= 2 else "sgu.u3"))
                    for j in range(3):
                        last = pe.transpose(probsT_bank(h)[:, j * P:(j + 1) * P], probs[:, h % 2, j * P:(j + 1) * P],
                                            c.ident[:])
                    last.then_inc(c.pe_done, ev.one("pe", f"turned{h}"))
            for h in range(2 * step - 4, 2 * step - 2):
                if 0 <= h < HEADS:
                    pe.wait_ge(c.act_done, ev.at(f"probsT{h}"))
                    q, kv = h // 4, h * KV_HEADS // HEADS
                    if h % 4 == 0:
                        pe.wait_ge(c.dve_done, ev.at(f"y{q - 2}" if q >= 2 else "sgu.u3"))
                    e = slice(kv * HEAD_DIM, (kv + 1) * HEAD_DIM)
                    y = out_bank(q)
                    pT = probsT[:, h % 2, :]
                    pe.matmul(y[:, 0, h % 4, :], pT[:, 0:P], v[:, 0, e], start=True, stop=True)
                    pe.matmul(y[:, 1, h % 4, :], pT[:, P:2 * P], v[:, 0, e], start=True, stop=False)
                    pe.matmul(y[:, 1, h % 4, :], pT[:, 2 * P:3 * P], v[:, 1, e], start=False, stop=True)\
                        .then_inc(c.pe_done, ev.one("pe", f"weighted{h}"))

        for i in range(21):
            project(i)
            if i == KV:
                wait_params(c, pe, "small", 5)
                pe.wait_ge(c.dve_done, ev.at("f1.step1"))
                for g in range(GROUPS):
                    last = pe.transpose(c.psum[:, 4 + g // 4, (g % 4) * P:(g % 4 + 1) * P], sgu_w[:, g, :], c.ident[:])
                last.then_inc(c.pe_done, ev.one("pe", "sgu_w.turned"))
            if i == KV + 1:
                pe.wait_ge(c.act_done, ev.at(f"blk{KV}.v"))
                for t in range(TT):
                    last = pe.transpose(c.psum[:, 2, t * P:(t + 1) * P], vT[:, t * P:(t + 1) * P], c.ident[:])
                last.then_inc(c.pe_done, ev.one("pe", "v.turned"))
            if i >= U0 + 3:
                if i == U0 + 3:
                    pe.wait_ge(c.dve_done, ev.at("sgu.vn1"))
                    pe.wait_ge(c.dve_done, ev.at("sgu_wT"))
                    for t in range(TT):
                        for g in range(GROUPS):
                            last = pe.matmul(c.psum[:, 4 + 2 * t + g // 4, (g % 4) * P:(g % 4 + 1) * P],
                                             vt[:, t, g * P:(g + 1) * P], sgu_wT[:, g, :], start=True, stop=True)
                        last.then_inc(c.pe_done, ev.one("pe", f"sgu.s{t}"))
                attend(i - U0 - 3)
        attend(9)

    @block.scalar
    def _(act):
        def evacuate(i):
            n = n0 + i
            act.wait_ge(c.w_used[n % SLOTS], n // SLOTS + 1)
            src = two(i % 2)
            if i < KV:
                act.activation(qT[:, 2 * i:2 * i + 2, :], src, ACT.Copy)\
                    .then_inc(c.act_done, ev.one("act", f"blk{i}.out"))
            elif i == KV:
                act.wait_ge(c.dve_done, ev.at(f"blk{i}.k"))
                act.activation(vT[:], src[:, 1, :], ACT.Copy).then_inc(c.act_done, ev.one("act", f"blk{i}.v"))
                act.activation(k_twice[1][0:64, :], src[64:128, 0, :], ACT.Copy)\
                    .then_inc(c.act_done, ev.one("act", f"blk{i}.out"))
            elif i < U0:
                j = i - V0
                act.activation(vt[:, :, COLS * j:COLS * (j + 1)], src, ACT.Gelu)\
                    .then_inc(c.act_done, ev.one("act", f"blk{i}.out"))
            elif i < GA0:
                j = i - U0
                act.activation(uT[:, 2 * j:2 * j + 2, :], src, ACT.Gelu)\
                    .then_inc(c.act_done, ev.one("act", f"blk{i}.out"))
            elif i < GB0:
                j = i - GA0
                act.wait_ge(c.dve_done, ev.at("sgu.vn1"))
                act.activation(gateA[:, 2 * j:2 * j + 2, :], src, ACT.Tanh, scale=0.5)\
                    .then_inc(c.act_done, ev.one("act", f"blk{i}.out"))
            else:
                j = i - GB0
                act.activation(gateB[:, 2 * j:2 * j + 2, :], src, ACT.Tanh, scale=0.5)\
                    .then_inc(c.act_done, ev.one("act", f"blk{i}.out"))

        def attend(step):
            for h in range(2 * step, 2 * step + 2):
                if 0 <= h < HEADS:
                    act.wait_ge(c.dve_done, ev.at(f"neg_max{h}"))
                    if h >= 2:
                        act.wait_ge(c.pe_done, ev.at(f"turned{h - 2}"))
                    for t, ks in ((0, slice(0, P)), (1, slice(P, 3 * P))):
                        last = act.activation(probs[:, h % 2, ks], scores[:, h % 2, ks], ACT.Exp,
                                              bias=neg_max[:, t, h:h + 1], accum_out=row_sum[:, t, h:h + 1])
                    last.then_inc(c.act_done, ev.one("act", f"probs{h}"))
            for h in range(2 * step - 2, 2 * step):
                if 0 <= h < HEADS:
                    act.wait_ge(c.pe_done, ev.at(f"turned{h}"))
                    if h >= 2:
                        act.wait_ge(c.pe_done, ev.at(f"weighted{h - 2}"))
                    act.activation(probsT[:, h % 2, :], probsT_bank(h), ACT.Copy)\
                        .then_inc(c.act_done, ev.one("act", f"probsT{h}"))
            if step >= 3 and step % 2 == 1:
                q = (step - 3) // 2
                act.wait_ge(c.dve_done, ev.at(f"sink{q}"))
                hs = slice(4 * q, 4 * q + 4)
                act.activation(neg_max[:, :, hs], neg_max[:, :, hs], ACT.Exp)\
                    .then_inc(c.act_done, ev.one("act", f"sink_exp{q}"))

        for i in range(21):
            evacuate(i)
            hi(c, act, n0 + i + SLOTS)
            if i == GA0:
                for b in range(2):
                    gs = slice(4 * b, 4 * b + 4)
                    act.wait_ge(c.dve_done, ev.at(f"sgu.u{2 + b}"))
                    act.activation(ysT_hi[:, gs, :], uT[:, gs, :], ACT.Copy)\
                        .then_inc(c.act_done, ev.one("act", f"ysT_hi{b}"))
            if i >= U0 + 3:
                attend(i - U0 - 3)
        attend(9)

    @block.vector
    def _(dve):

        def attend(step):
            for h in range(2 * step, 2 * step + 2):
                if 0 <= h < HEADS:
                    dve.wait_ge(c.pe_done, ev.at(f"scores{h}"))
                    if h >= 2:
                        dve.wait_ge(c.act_done, ev.at(f"probs{h - 2}"))
                    s = scores[:, h % 2, :]
                    dve.scalar_tensor_tensor(s, scores_bank(h), HEAD_DIM ** -0.5, window_mask[:],
                                             ALU.mult, ALU.add).then_inc(c.dve_done, ev.one("dve", f"masked{h}"))
                    dve.wait_ge(c.dve_done, ev.at(f"masked{h}"))
                    dve.tensor_reduce(row_max[:, 0, h:h + 1], s[:, 0:P], AX_X, ALU.max)
                    dve.tensor_reduce(row_max[:, 1, h:h + 1], s[:, P:3 * P], AX_X, ALU.max)\
                        .then_inc(c.dve_done, ev.one("dve", f"row_max{h}"))
                    dve.wait_ge(c.dve_done, ev.at(f"row_max{h}"))
                    dve.tensor_scalar(neg_max[:, :, h:h + 1], row_max[:, :, h:h + 1],
                                      sinks[:, h:h + 1], -1.0, ALU.max, ALU.mult)\
                        .then_inc(c.dve_done, ev.one("dve", f"neg_max{h}"))
            if step >= 3 and step % 2 == 1:
                q = (step - 3) // 2
                hs = slice(4 * q, 4 * q + 4)
                dve.wait_ge(c.act_done, ev.at(f"probs{4 * q + 3}"))
                dve.tensor_tensor(neg_max[:, :, hs], neg_max[:, :, hs],
                                  sinks[:, hs].unsqueeze(1).broadcast_to([P, TT, 4]), ALU.add)\
                    .then_inc(c.dve_done, ev.one("dve", f"sink{q}"))
                dve.wait_ge(c.act_done, ev.at(f"sink_exp{q}"))
                dve.tensor_tensor(row_sum[:, :, hs], row_sum[:, :, hs], neg_max[:, :, hs], ALU.add)\
                    .then_inc(c.dve_done, ev.one("dve", f"den{q}"))
                dve.wait_ge(c.dve_done, ev.at(f"den{q}"))
                dve.reciprocal(row_sum[:, :, hs], row_sum[:, :, hs]).then_inc(c.dve_done, ev.one("dve", f"rden{q}"))
                dve.wait_ge(c.dve_done, ev.at(f"rden{q}"))
                dve.wait_ge(c.pe_done, ev.at(f"weighted{4 * q + 3}"))
                dve.wait_ge(c.pe_done, ev.at("sgu.s1"))
                y = vt[:, :, 4 * q * HEAD_DIM:4 * (q + 1) * HEAD_DIM].rearrange("p t (h e) -> p t h e", h=4)
                dve.tensor_tensor(y, out_bank(q), row_sum[:, :, hs].unsqueeze(3).broadcast_to(
     [P, TT, 4, HEAD_DIM]), ALU.mult).then_inc(c.dve_done, ev.one("dve", f"y{q}"))

        for i in range(21):
            if i == KV:
                n = n0 + i
                dve.wait_ge(c.w_used[n % SLOTS], n // SLOTS + 1)
                src = two(i % 2)
                dve.tensor_copy(k_twice[0][0:64, :], src[0:64, 0, :])
                dve.tensor_copy(k_twice[0][64:128, :], src[0:64, 0, :])
                dve.tensor_copy(k_twice[1][64:128, :], src[64:128, 0, :])\
                    .then_inc(c.dve_done, ev.one("dve", f"blk{i}.k"))
            lo(c, dve, n0 + i + SLOTS)
            if i == KV:
                dve.wait_ge(c.pe_done, ev.at("sgu_w.turned"))
                for b in range(2):
                    gs = slice(4 * b, 4 * b + 4)
                    last = dve.tensor_tensor(sgu_wT[:, gs, :], bank(4 + b).rearrange("p (g t) -> p g t", g=4),
                                             causal_T[:].unsqueeze(1).broadcast_to([P, 4, P]), ALU.mult)
                last.then_inc(c.dve_done, ev.one("dve", "sgu_wT"))
            if i == GA0:
                for b in range(2):
                    gs = slice(4 * b, 4 * b + 4)
                    dve.wait_ge(c.act_done, ev.at(f"ysT_hi{b}"))
                    dve.tensor_tensor(ysT_lo[:, gs, :], uT[:, gs, :], ysT_hi[:, gs, :].bitcast(F32),
                                      ALU.subtract).then_inc(c.dve_done, ev.one("dve", f"ysT_lo{b}"))
            if i == KV + 2:
                dve.wait_ge(c.pe_done, ev.at("v.turned"))
                dve.tensor_copy(v[:].rearrange("p t e -> p (t e)"), c.psum[:, 2, 0:TT * P])\
                    .then_inc(c.dve_done, ev.one("dve", "v.out"))
            if i == U0:
                dve.wait_ge(c.act_done, ev.at(f"blk{U0 - 1}.out"))
                for t in range(TT):
                    for half in range(2):
                        last = dve.bn_stats(stats[:, t, half, :], vt[:, t, half * BANK:(half + 1) * BANK])
                last.then_inc(c.dve_done, ev.one("dve", "sgu.stats"))
                dve.wait_ge(c.dve_done, ev.at("sgu.stats"))
                for t in range(TT):
                    last = dve.bn_aggr(mean_var[:, t, :], stats[:, t, :, :].rearrange("p a s -> p (a s)"))
                last.then_inc(c.dve_done, ev.one("dve", "sgu.mean_var"))
            if i == U0 + 1:
                for t in range(TT):
                    dve.wait_ge(c.pool_done, ev.at("sgu.rstd"))
                    dve.tensor_scalar(vt[:, t, :], vt[:, t, :], mean_var[:, t, 0:1],
                                      c.rstd[:, 4 + t:5 + t], ALU.subtract, ALU.mult)\
                        .then_inc(c.dve_done, ev.one("dve", f"sgu.xc{t}"))
                    dve.wait_ge(c.dve_done, ev.at(f"sgu.xc{t}"))
                    wait_params(c, dve, "small", 5)
                    dve.tensor_tensor(vt[:, t, :], vt[:, t, :], ln_g, ALU.mult)\
                        .then_inc(c.dve_done, ev.one("dve", f"sgu.xg{t}"))
                    dve.wait_ge(c.dve_done, ev.at(f"sgu.xg{t}"))
                    dve.tensor_tensor(vt[:, t, :], vt[:, t, :], ln_b, ALU.add)\
                        .then_inc(c.dve_done, ev.one("dve", f"sgu.vn{t}"))
            if i == U0 + 3:
                dve.wait_ge(c.act_done, ev.at(f"blk{U0 + 3}.out"))
                for t in range(TT):
                    dve.wait_ge(c.pe_done, ev.at(f"sgu.s{t}"))
                    for b in range(2):
                        gs, ts = slice(4 * b, 4 * b + 4), slice(t * P, (t + 1) * P)
                        s = bank(4 + 2 * t + b).rearrange("p (g t) -> p g t", g=4)
                        dve.tensor_tensor(s, s, sgu_b[:, gs, :], ALU.add)\
                            .then_inc(c.dve_done, ev.one("dve", f"sgu.b{2 * t + b}"))
                        dve.wait_ge(c.dve_done, ev.at(f"sgu.b{2 * t + b}"))
                        dve.tensor_tensor(uT[:, gs, ts], uT[:, gs, ts], s, ALU.mult)\
                            .then_inc(c.dve_done, ev.one("dve", f"sgu.u{2 * t + b}"))
            if i >= U0 + 3:
                attend(i - U0 - 3)
        attend(9)

    @block.gpsimd
    def _(pool):
        pool.wait_ge(c.dve_done, ev.at("sgu.mean_var"))
        pool.tensor_scalar(c.rstd[:, 4:4 + TT], mean_var[:, :, 1], LN_EPS, None, ALU.add)\
            .then_inc(c.pool_done, ev.one("pool", "sgu.var"))
        pool.wait_ge(c.pool_done, ev.at("sgu.var"))
        pool.tensor_tensor(c.rstd[:, 4:4 + TT], c.rstd[:, 4:4 + TT], c.half_power[:, 0:TT], ALU.pow)\
            .then_inc(c.pool_done, ev.one("pool", "sgu.rstd"))
        for gate, base, name in ((gateA, GA0, "ga"), (gateB, GB0, "gb")):
            for j in range(4):
                ks = slice(2 * j, 2 * j + 2)
                pool.wait_ge(c.act_done, ev.at(f"blk{base + j}.out"))
                pool.tensor_scalar(gate[:, ks, :], gate[:, ks, :], 0.5, 0.5, ALU.mult, ALU.add)\
                    .then_inc(c.pool_done, ev.one("pool", f"{name}{j}"))

    def branch(first, a_hi, a_lo, ready):
        @block.tensor
        def _(pe):
            pe.wait_ge(c.dve_done, ev.at(ready))
            for i in range(first, first + 4):
                n = n0 + i
                pe.wait_ge(*ev.when(c, f"blk{i - 2}.out"))
                wait_weights(c, pe, n)
                features_by_tokens(pe, two(i % 2), as_columns(c.w_hi[n % SLOTS]), as_columns(c.w_lo[n % SLOTS]),
                                   a_hi, a_lo).then_inc(c.w_used[n % SLOTS], 1)

    branch(SB0, ysT_hi, ysT_lo, "ysT_lo1")

    @block.scalar
    def _(act):
        for i in range(SB0, AB0):
            hi(c, act, n0 + i + SLOTS)

    @block.vector
    def _(dve):
        for i in range(SB0, AB0):
            n, j = n0 + i, i - SB0
            ks = slice(2 * j, 2 * j + 2)
            dve.wait_ge(c.w_used[n % SLOTS], n // SLOTS + 1)
            dve.wait_ge(c.pool_done, ev.at(f"gb{j}"))
            dve.tensor_tensor(merged[:, ks, :], two(i % 2), gateB[:, ks, :], ALU.mult)\
                .then_inc(c.dve_done, ev.one("dve", f"blk{i}.out"))
            lo(c, dve, n + SLOTS)

    transpose_split(c, block, "ya", vt, KT, [["y3"], ["y3"]], [2, 3, 4, 5])
    branch(AB0, c.aT_hi, c.aT_lo, "ya.lo3")

    @block.tensor
    def _(pe):
        for i in range(4):
            n = n0 + WO0 + i
            pe.wait_ge(c.dve_done, ev.at(f"merged_lo{i}"))
            wait_weights(c, pe, n)
            row_block(c, pe, as_rows(c.w_hi[n % SLOTS]), as_rows(c.w_lo[n % SLOTS]), ysT_hi[:, 2 * i:2 * i + 2, :],
                      ysT_lo[:, 2 * i:2 * i + 2, :], i == 0, "mix" if i == 3 else None).then_inc(c.w_used[n % SLOTS], 1)

    @block.scalar
    def _(act):
        for i in range(AB0, WO0 + 4):
            if i < WO0 + 3:
                hi(c, act, n0 + i + SLOTS)
            if i < WO0:
                j = i - AB0
                ks = slice(2 * j, 2 * j + 2)
                act.wait_ge(c.dve_done, ev.at(f"merged{j}"))
                act.activation(ysT_hi[:, ks, :], merged[:, ks, :], ACT.Copy)\
                    .then_inc(c.act_done, ev.one("act", f"merged_hi{j}"))

    @block.vector
    def _(dve):
        for i in range(AB0, WO0 + 4):
            n, j = n0 + i, i - AB0
            if i < WO0:
                ks = slice(2 * j, 2 * j + 2)
                dve.wait_ge(c.w_used[n % SLOTS], n // SLOTS + 1)
                dve.wait_ge(c.pool_done, ev.at(f"ga{j}"))
                dve.tensor_tensor(gateA[:, ks, :], two(i % 2), gateA[:, ks, :], ALU.mult)\
                    .then_inc(c.dve_done, ev.one("dve", f"blk{i}.out"))
                dve.wait_ge(c.dve_done, ev.at(f"blk{i}.out"))
                dve.tensor_tensor(merged[:, ks, :], merged[:, ks, :], gateA[:, ks, :], ALU.add)\
                    .then_inc(c.dve_done, ev.one("dve", f"merged{j}"))
            if i < WO0 + 3:
                lo(c, dve, n + SLOTS)
            if i < WO0:
                dve.wait_ge(c.act_done, ev.at(f"merged_hi{j}"))
                dve.tensor_tensor(ysT_lo[:, ks, :], merged[:, ks, :],
                                  ysT_hi[:, ks, :].bitcast(F32), ALU.subtract)\
                    .then_inc(c.dve_done, ev.one("dve", f"merged_lo{j}"))



GROUP = 256
CONF_TAPS = 31
SHORT_TAPS = 3
HG_HEADS = 4
HG_D = 64
MLA_HEADS = 4
NOPE, ROPE = 64, 32
QK = NOPE + ROPE
ROPE_BASE = 10000.0
XA_HEADS = 4
XA_D = 64
LEVELS = [128, 64, 32, 16, 8, 4, 2, 1, 0]
HG_CHUNK = 64
TINY = 2.0 ** -60

KV0, KV1, HQ, ZF, ZB, CQ, CKV, CA, CG, UP, HV, HG, SC, SX, SB, WO = range(16)
XQ, XO = WO + 4, WO + 5
FFN_USE = 7
SMALL = 13


class Second:
    pass


def second_tiles(c, ctx):
    s = Second()

    def sb(name, shape, dt=F32):
        return ctx.enter_context(c.nc.sbuf_tensor(f"s_{name}", shape, dt))

    s.cos = sb("cos", [P, TT, ROPE // 2])
    s.sin = sb("sin", [P, TT, ROPE // 2])
    s.lower = sb("lower", [P, DEPTH, HG_HEADS])
    s.block_mask = sb("block_mask", [P, len(LEVELS) - 2, P], I32)
    s.again = sb("again", [P, HG_HEADS * SEQ], BF16)
    return s


def second_setup(c, s):
    nc, dram = c.nc, c.dram
    half = ROPE // 2
    with ExitStack() as tiles:
        def sb(name, shape, dt=F32):
            return tiles.enter_context(nc.sbuf_tensor(f"t_{name}", shape, dt))
        pos_i, pos = sb("pos_i", [P, TT], I32), sb("pos", [P, TT])
        inv = sb("inv", [P, half])
        ang, turns = sb("ang", [P, TT, half]), sb("turns", [P, TT, half])
        shifted, over = sb("shifted", [P, TT, half]), sb("over", [P, TT, half])
        gamma = sb("gamma", [P, DEPTH, HG_HEADS])
        top, total = sb("top", [P, HG_HEADS]), sb("total", [P, HG_HEADS])
        t_index, s_xor_t, shift = sb("t_index", [P, P], I32), sb("s_xor_t", [P, P], I32), sb("shift", [P, P], I32)
        p_index = sb("p_index", [P, P], I32)
        loaded = tiles.enter_context(nc.semaphore("setup_loaded"))
        made = tiles.enter_context(nc.semaphore("setup_made"))
        d = tiles.enter_context(nc.semaphore("setup_dve"))
        a = tiles.enter_context(nc.semaphore("setup_act"))
        with nc.Block() as block:
            @block.sync
            def _(sp):
                with nc.allow_non_contiguous_dma(reason="1 KB of positions and 4 KB of gammas"):
                    sp.dma_start(pos_i[:], dram["positions_2"].rearrange("o (t p) -> p (o t)", p=P))\
                        .then_inc(loaded, 16)
                    for direction in range(2):
                        ps = slice(direction * HG_D, (direction + 1) * HG_D)
                        sp.dma_start(gamma[ps], dram["h_gamma_2"][direction].rearrange("l (h d) -> d l h", d=HG_D))\
                            .then_inc(loaded, 16)
                sp.wait_ge(loaded, 48)

            @block.gpsimd
            def _(pool):
                pool.iota(t_index[:], pattern=[[1, P]], base=0, channel_multiplier=0)
                pool.iota(p_index[:], pattern=[[0, P]], base=0, channel_multiplier=1)
                for j in range(half):
                    last = pool.memset(inv[:, j:j + 1], float(np.float32(ROPE_BASE) ** np.float32(-2 * j / ROPE)))
                last.then_inc(made, 1)

            @block.vector
            def _(dve):
                count = [0]

                def link(instruction):
                    count[0] += 1
                    instruction.then_inc(d, 1)
                    dve.wait_ge(d, count[0])

                dve.wait_ge(made, 1)
                dve.wait_ge(loaded, 48)
                link(dve.tensor_tensor(s_xor_t[:], p_index[:], t_index[:], ALU.bitwise_xor))
                for i, h in enumerate(LEVELS[2:]):
                    bits = (2 * h).bit_length() - 1 if h else 0
                    link(dve.tensor_scalar(shift[:], s_xor_t[:], bits, None, ALU.logical_shift_right))
                    link(dve.tensor_scalar(s.block_mask[:, i, :], shift[:], 0, None, ALU.is_equal))
                link(dve.tensor_copy(pos[:], pos_i[:]))
                link(dve.tensor_tensor(ang[:], pos[:].unsqueeze(2).broadcast_to([P, TT, half]),
                                       inv[:].unsqueeze(1).broadcast_to([P, TT, half]), ALU.mult))
                link(dve.tensor_scalar(turns[:], ang[:], float(1 / (2 * np.pi)), None, ALU.mult))
                link(dve.tensor_scalar(turns[:], turns[:], 1.5 * 2.0 ** 23, None, ALU.add))
                link(dve.tensor_scalar(turns[:], turns[:], 1.5 * 2.0 ** 23, None, ALU.subtract))
                rest, full = 2 * np.pi, 2 * np.pi
                parts = []
                for bits in (6, 17):
                    part = np.floor(rest * 2.0 ** bits) / 2.0 ** bits
                    parts.append(part)
                    rest -= part
                parts.append(rest)
                for part in parts:
                    link(dve.scalar_tensor_tensor(ang[:], turns[:], -float(part), ang[:], ALU.mult, ALU.add))
                pi = float(np.nextafter(np.float32(np.pi), np.float32(0)))
                link(dve.tensor_scalar(shifted[:], ang[:], float(np.pi / 2), None, ALU.add))
                link(dve.tensor_scalar(over[:], shifted[:], pi, -float(full), ALU.is_gt, ALU.mult))
                link(dve.tensor_tensor(shifted[:], shifted[:], over[:], ALU.add))
                link(dve.tensor_scalar(shifted[:], shifted[:], pi, -pi, ALU.min, ALU.max))
                link(dve.tensor_scalar(ang[:], ang[:], pi, -pi, ALU.min, ALU.max))
                link(dve.tensor_copy(top[:], gamma[:, 0, :]))
                for l in range(1, DEPTH):
                    link(dve.tensor_tensor(top[:], top[:], gamma[:, l, :], ALU.max))
                link(dve.tensor_tensor(gamma[:], gamma[:], top[:].unsqueeze(1).broadcast_to([P, DEPTH, HG_HEADS]),
                                       ALU.subtract))
                dve.wait_ge(a, 3)
                link(dve.tensor_copy(total[:], gamma[:, 0, :]))
                for l in range(1, DEPTH):
                    link(dve.tensor_tensor(total[:], total[:], gamma[:, l, :], ALU.add))
                link(dve.reciprocal(total[:], total[:]))
                link(dve.tensor_tensor(gamma[:], gamma[:], total[:].unsqueeze(1).broadcast_to([P, DEPTH, HG_HEADS]),
                                       ALU.mult))
                link(dve.tensor_copy(top[:], gamma[:, 0, :]))
                for l in range(DEPTH):
                    if l:
                        link(dve.tensor_tensor(top[:], top[:], gamma[:, l, :], ALU.add))
                    link(dve.tensor_tensor(s.lower[:, l, :], top[:], gamma[:, 0, :], ALU.subtract))

            before = 1 + 2 * len(LEVELS[2:]) + 5 + 3 + 5

            @block.scalar
            def _(act):
                act.wait_ge(d, before)
                act.activation(s.sin[:], ang[:], ACT.Sin).then_inc(a, 1)
                act.activation(s.cos[:], shifted[:], ACT.Sin).then_inc(a, 1)
                act.wait_ge(d, before + DEPTH + 1)
                act.activation(gamma[:], gamma[:], ACT.Exp).then_inc(a, 1)


def second_block_layer(c, s, layer):
    nc, ev, dram = c.nc, c.ev, c.dram
    ev.new_layer("second")
    c.layer = layer
    with ExitStack() as tiles:
        def sb(name, shape, dt=F32):
            return tiles.enter_context(nc.sbuf_tensor(f"u_{name}", shape, dt))

        low_hi, low_lo = sb("low_hi", [P, 3, SEQ], F32R), sb("low_lo", [P, 3, SEQ], F32R)
        kv_mem = sb("kv_mem", [P, TT, 2 * XA_HEADS * XA_D])
        q2, lf, kk = (sb(n, [P, HG_HEADS, SEQ]) for n in ("q2", "lf", "kk"))
        GH = sb("GH", [P, 2, HG_HEADS, SEQ])
        hv, hg = sb("hv", [P, TT, GROUP]), sb("hg", [P, TT, GROUP])
        qk = sb("qk", [P, 2, TT * MLA_HEADS, QK])
        kv_up = sb("kv_up", [P, TT, 2 * GROUP])
        conf, conf_out = sb("conf", [P, 2, SEQ + CONF_TAPS - 1]), sb("conf_out", [P, 2, SEQ])
        short, short_out = sb("short", [P, 2, SEQ + SHORT_TAPS - 1]), sb("short_out", [P, 2, SEQ])
        row_max, row_sum = sb("row_max", [P, 2 * TT, 4]), sb("row_sum", [P, 2 * TT, 4])
        taps_rows, taps = sb("taps_rows", [36, GROUP]), sb("taps", [P, 2, 36])
        bc = {name: sb(name, [P, n]) for name, n in (("qa_g", GROUP), ("kva_g", P), ("qn_g", QK), ("kn_g", QK),
                                                     ("ln_g", GROUP), ("ln_b", GROUP), ("onorm_g", GROUP),
                                                     ("xqn_g", XA_D), ("xkn_g", XA_D))}
        sq_sum, factor = sb("sq_sum", [P, 16]), sb("factor", [P, 16])
        lower = sb("lower_now", [P, HG_HEADS])
        stats, mean_var = sb("stats", [P, TT, 6]), sb("mean_var", [P, TT, 2])
        with ExitStack() as early:
            def sb_early(name, shape, dt=F32):
                return early.enter_context(nc.sbuf_tensor(f"u_{name}", shape, dt))
            bT_hi, bT_lo = sb_early("bT_hi", [P, KT, SEQ], F32R), sb_early("bT_lo", [P, KT, SEQ], F32R)
        near, far = (sb(n, [P, HG_HEADS * TT, P]) for n in ("near", "far"))
        Q = [sb(f"Q{i}", [P, HG_HEADS, SEQ]) for i in range(2)]
        K = [sb(f"K{i}", [P, HG_HEADS, SEQ]) for i in range(2)]

    G, H = GH[:, 0], GH[:, 1]
    mem = GH.rearrange("p t h n -> p t (h n)")
    probs, probsT = lf[:, 0:2, :], lf[:, 2:4, :]
    cat = c.xn
    cqkv = c.xn[:, 0, :].rearrange("p (t n) -> p t n", t=TT)
    scratch = c.xn[:, 1, :]
    f, clamp = (t[:].rearrange("p i t -> p (i t)").rearrange("p (h t) -> p h t", h=HG_HEADS) for t in (near, far))
    mla_T = (Q[0], K[0])
    mem_T = (G, H)
    squares = Q[1][:].rearrange("p h t -> p (h t)")
    CKV_AT = COLS - P - ROPE
    UP_Q = 2 * MLA_HEADS * QK
    first_col = {KV0: 0, KV1: 256, HQ: 512, ZF: 768, ZB: 1024, HV: 1280, HG: 1536, CA: 0, CG: 256, SB: 1792,
                 SC: 2048, SX: 2304, CQ: 2560, CKV: 2976 - COLS}
    by_tokens = (KV0, KV1, CQ, CKV, HV, HG)

    def two(b):
        return c.psum[:, b, :].rearrange("p (f t) -> p f t", f=2)

    def load(sp, n, source):
        load_weights(c, sp, n % SLOTS, n // SLOTS, n < SLOTS, source)

    def used(eng, n):
        eng.wait_ge(c.w_used[n % SLOTS], n // SLOTS + 1)


    def rms_sum(dve, tag, view, sq, n, dims):
        dve.tensor_tensor(sq, view, view, ALU.mult).then_inc(c.dve_done, ev.one("dve", f"{tag}.sq"))
        dve.wait_ge(c.dve_done, ev.at(f"{tag}.sq"))
        dve.tensor_reduce(sq_sum[:, 0:n].rearrange(dims[0], **dims[1]), sq, AX_X, ALU.add)\
            .then_inc(c.dve_done, ev.one("dve", f"{tag}.sum"))

    def rms_power(pool, tag, n, width):
        pool.wait_ge(c.dve_done, ev.at(f"{tag}.sum"))
        pool.tensor_scalar(factor[:, 0:n], sq_sum[:, 0:n], 1.0 / width, RMS_EPS, ALU.mult,
                           ALU.add).then_inc(c.pool_done, ev.one("pool", f"{tag}.meansq"))
        pool.wait_ge(c.pool_done, ev.at(f"{tag}.meansq"))
        pool.tensor_tensor(factor[:, 0:n], factor[:, 0:n], c.half_power[:, 0:n], ALU.pow)\
            .then_inc(c.pool_done, ev.one("pool", f"{tag}.factor"))


    def halves(tile, direction, h):
        part = tile[direction * HG_D:(direction + 1) * HG_D].rearrange("p h t -> p (h t)")
        return part.rearrange("p (b two t) -> p b two t", two=2, t=h)[:, :, 1 - direction, :]

    def other_halves(tile, direction, h):
        part = tile[direction * HG_D:(direction + 1) * HG_D].rearrange("p h t -> p (h t)")
        return part.rearrange("p (b two t) -> p b two t", two=2, t=h)[:, :, direction, :]

    def head_side(tile, direction, side):
        return tile[direction * HG_D:(direction + 1) * HG_D, side:side + 3:2, :]

    def gates_dve(dve):
        dve.wait_ge(c.act_done, ev.at(f"blk{ZB}.out"))
        dve.wait_ge(c.dve_done, ev.at("lower"))
        lower_b = lower[:].unsqueeze(2).broadcast_to([P, HG_HEADS, SEQ])
        dve.tensor_tensor(clamp, kk[:], lower_b, ALU.mult).then_inc(c.dve_done, ev.one("dve", "hg.lower"))
        dve.wait_ge(c.dve_done, ev.at("hg.lower"))
        dve.tensor_tensor(f, f, clamp, ALU.add).then_inc(c.dve_done, ev.one("dve", "hg.f"))
        dve.wait_ge(c.dve_done, ev.at("hg.f"))
        dve.tensor_tensor(kk[:], kk[:], clamp, ALU.subtract).then_inc(c.dve_done, ev.one("dve", "hg.k"))
        dve.wait_ge(c.dve_done, ev.at("hg.k"))
        dve.tensor_scalar(lf[:], f, TINY, None, ALU.max).then_inc(c.dve_done, ev.one("dve", "hg.big"))
        dve.tensor_scalar(clamp, f, 1 / TINY, 1.0, ALU.mult, ALU.min).then_inc(c.dve_done, ev.one("dve", "hg.small"))
        dve.wait_ge(c.act_done, ev.at("hg.ln"))
        dve.tensor_tensor(lf[:], lf[:], clamp, ALU.add).then_inc(c.dve_done, ev.one("dve", "lf"))

    def gates_act(act):
        act.wait_ge(c.dve_done, ev.at("hg.small"))
        act.activation(lf[:], lf[:], ACT.Ln)
        act.activation(clamp, clamp, ACT.Ln).then_inc(c.act_done, ev.one("act", "hg.ln"))

    def again_pool(pool, h):
        starts = s.again[:].rearrange("p (b t) -> p b t", t=h)[:, :, 0:1]
        pool.memset(starts, 0.0).then_inc(c.pool_done, ev.one("pool", f"again{h}"))

    def sums_dve(dve):
        flat = lf[:].rearrange("p h t -> p (h t)")
        for tile, h in ((G, SEQ), (H, HG_CHUNK)):
            dve.wait_ge(c.dve_done, ev.at("lf"))
            dve.wait_ge(c.pool_done, ev.at(f"again{h}"))
            dve.tensor_tensor_scan(tile.rearrange("p h t -> p (h t)"), s.again[:], flat, 0.0, ALU.mult, ALU.add)\
                .then_inc(c.dve_done, ev.one("dve", f"prefix{h}"))

    def sums_pool(pool, h):
        tile = G if h == SEQ else H
        back = slice(HG_D, P)
        pool.wait_ge(c.dve_done, ev.at(f"prefix{h}"))
        pool.wait_ge(c.pool_done, ev.last("pool"))
        pool.tensor_tensor(tile[back], tile[back], lf[back], ALU.subtract)\
            .then_inc(c.pool_done, ev.one("pool", f"sums{h}"))
        pool.wait_ge(c.pool_done, ev.last("pool"))

    def border_dve(dve, j):
        p, h = j % 2, LEVELS[j]
        tile = (G if h >= HG_CHUNK else H).rearrange("p h t -> p (h t)").rearrange("p (b t) -> p b t", t=2 * h)
        dve.wait_ge(c.pool_done, ev.at(f"sums{SEQ if h >= HG_CHUNK else HG_CHUNK}"))
        if j >= 2:
            dve.wait_ge(c.pe_done, ev.at(f"level{j - 2}.product"))
        dve.tensor_tensor(K[p][:].rearrange("p h t -> p (h t)").rearrange("p (b t) -> p b t", t=2 * h), tile,
                          tile[:, :, h - 1:h].broadcast_to([P, HG_HEADS * SEQ // (2 * h), 2 * h]), ALU.subtract)\
            .then_inc(c.dve_done, ev.one("dve", f"border{j}"))

    def exp_act(act, j):
        p, h = j % 2, LEVELS[j]
        act.wait_ge(c.dve_done, ev.at(f"border{j}"))
        both = K[p][:].rearrange("p h t -> p (h t)").rearrange("p (b two t) -> p b two t", two=2, t=h)
        for side, sign in ((0, -1.0), (1, 1.0)):
            last = act.activation(both[:, :, side, :], both[:, :, side, :], ACT.Exp, scale=sign)
        last.then_inc(c.act_done, ev.one("act", f"exp{j}"))

    def query_pool(pool, j):
        p, h = j % 2, LEVELS[j]
        if j >= 2:
            pool.wait_ge(c.pe_done, ev.at(f"level{j - 2}.product"))
        else:
            pool.wait_ge(c.act_done, ev.at(f"blk{ZF}.out"))
        pool.wait_ge(c.pool_done, ev.last("pool"))
        for direction in range(2):
            pool.memset(other_halves(Q[p], direction, h), 0.0)
        pool.wait_ge(c.act_done, ev.at(f"exp{j}"))
        for direction in range(2):
            last = pool.tensor_tensor(halves(Q[p], direction, h), halves(K[p], direction, h),
                                      halves(q2, direction, h), ALU.mult)
        last.then_inc(c.pool_done, ev.one("pool", f"query{j}"))
        pool.wait_ge(c.pool_done, ev.last("pool"))

    def scale_dve(dve, j):
        p = j % 2
        dve.wait_ge(c.pool_done, ev.at(f"query{j}"))
        dve.tensor_tensor(K[p][:], K[p][:], kk[:], ALU.mult).then_inc(c.dve_done, ev.one("dve", f"scaled{j}"))

    def product_pe(pe, j):
        p, h = j % 2, LEVELS[j]
        if h:
            pe.wait_ge(c.dve_done, ev.at(f"scaled{j}"))
        else:
            pe.wait_ge(c.dve_done, ev.at("hg.k"))
            pe.wait_ge(c.act_done, ev.at(f"blk{HQ}.out"))
        if j:
            pe.wait_ge(c.dve_done, ev.at(f"level{j - 1}"))
        Kj, Qj = (K[p], Q[p]) if h else (kk, q2)
        for head in range(HG_HEADS):
            for t in range(TT):
                i, tq = 2 * head + t, (1 - t if h == P else t)
                last = pe.matmul(c.psum[:, 2 + i // 4, (i % 4) * P:(i % 4 + 1) * P],
                                 Kj[:, head, t * P:(t + 1) * P], Qj[:, head, tq * P:(tq + 1) * P],
                                 start=True, stop=True)
        last.then_inc(c.pe_done, ev.one("pe", f"level{j}.product"))

    def keep_dve(dve, j):
        product = c.psum[:, 2:4, :].rearrange("p b (i t) -> p (b i) t", t=P)
        dve.wait_ge(c.pe_done, ev.at(f"level{j}.product"))
        if j >= 2:
            dve.wait_ge(c.dve_done, ev.at(f"level{j - 1}"))
            ins = dve.copy_predicated(near[:], s.block_mask[:, j - 2:j - 1, :].broadcast_to([P, HG_HEADS * TT, P]),
                                      product)
        else:
            ins = dve.tensor_copy((near if j else far)[:], product)
        ins.then_inc(c.dve_done, ev.one("dve", f"level{j}"))

    def weigh_pe(pe):
        pe.wait_ge(c.dve_done, ev.at(f"level{len(LEVELS) - 1}"))
        pe.wait_ge(c.act_done, ev.at(f"blk{HV}.out"))
        out = c.psum[:, 2, :].rearrange("p (t n) -> p t n", t=TT)
        for head in range(HG_HEADS):
            e = slice(head * HG_D, (head + 1) * HG_D)
            for t in range(TT):
                pe.matmul(out[:, t, e], near[:, 2 * head + t, :], hv[:, t, e], start=True, stop=False)
                last = pe.matmul(out[:, t, e], far[:, 2 * head + 1 - t, :], hv[:, 1 - t, e], start=False, stop=True)
        last.then_inc(c.pe_done, ev.one("pe", "hg.o"))

    by_head = ("p (t h) -> p t h", dict(t=TT))
    mem_heads = kv_mem[:].rearrange("p t (h e) -> p t h e", h=XA_HEADS)
    xq = conf_out[:].rearrange("p t (h e) -> p t h e", h=XA_HEADS)

    def cat_part(group):
        return cat[:, :, group * GROUP:(group + 1) * GROUP]

    def heads_of(view):
        return view.rearrange("p t (h e) -> p t h e", e=HG_D)

    def head_norm_dve(dve, tag, view, gain, after):
        sq = squares[:, 0:TT * GROUP].rearrange("p (t h e) -> p t h e", t=TT, e=HG_D)
        for name in after:
            dve.wait_ge(*ev.when(c, name))
        rms_sum(dve, tag, view, sq, 8, by_head)
        dve.wait_ge(c.pool_done, ev.at(f"{tag}.factor"))
        fb = factor[:, 0:8].rearrange("p (t h) -> p t h", t=TT).unsqueeze(3).broadcast_to([P, TT, 4, HG_D])
        dve.tensor_tensor(view, view, fb, ALU.mult).then_inc(c.dve_done, ev.one("dve", f"{tag}.scaled"))
        dve.wait_ge(c.dve_done, ev.at(f"{tag}.scaled"))
        gb = bc[gain][:].unsqueeze(1).unsqueeze(1).broadcast_to([P, TT, 4, HG_D])
        dve.tensor_tensor(view, view, gb, ALU.mult).then_inc(c.dve_done, ev.one("dve", f"{tag}.normed"))

    def hg_norm_dve(dve):
        o = heads_of(cat_part(1))
        sq = squares[:, 0:TT * GROUP].rearrange("p (t h e) -> p t h e", t=TT, e=HG_D)
        dve.wait_ge(c.act_done, ev.at("hg.copied"))
        dve.wait_ge(c.pe_done, ev.at(f"level{len(LEVELS) - 2}.product"))
        rms_sum(dve, "hgn", o, sq, 8, by_head)
        dve.wait_ge(c.pool_done, ev.at("hgn.factor"))
        fb = factor[:, 0:8].rearrange("p (t h) -> p t h", t=TT).unsqueeze(3).broadcast_to([P, TT, HG_HEADS, HG_D])
        dve.tensor_tensor(o, o, fb, ALU.mult).then_inc(c.dve_done, ev.one("dve", "hgn.scaled"))
        dve.wait_ge(c.dve_done, ev.at("hgn.scaled"))
        dve.tensor_tensor(cat_part(1), cat_part(1), bc["onorm_g"][:].unsqueeze(1).broadcast_to(
[P, TT, GROUP]), ALU.mult).then_inc(c.dve_done, ev.one("dve", "hgn.gained"))
        dve.wait_ge(c.dve_done, ev.at("hgn.gained"))
        dve.tensor_tensor(cat_part(1), cat_part(1), hg[:], ALU.mult).then_inc(c.dve_done, ev.one("dve", "cat1"))


    def low_act(act):
        act.wait_ge(c.act_done, ev.at(f"blk{CKV}.out"))
        for n in range(4):
            t, at, width = n % 2, COLS * (n // 2), (COLS, P)[n // 2]
            if n:
                act.wait_ge(c.act_done, ev.at(f"low.ss{n - 1}"))
            act.activation(scratch[:, 0:width], cqkv[:, t, at:at + width], ACT.Square,
                           accum_out=c.ss[:, 8 + n:9 + n]).then_inc(c.act_done, ev.one("act", f"low.ss{n}"))

    def low_pool(pool):
        pool.wait_ge(c.act_done, ev.at("low.ss3"))
        rms_factors(c, pool, "lowq", slice(8, 10), GROUP, RMS_EPS)
        rms_factors(c, pool, "lowkv", slice(10, 12), P, RMS_EPS)

    def low_dve(dve):
        dve.wait_ge(c.pool_done, ev.at("lowkv.rstd"))
        wait_params(c, dve, "small", SMALL)
        for n in range(4):
            t, at, width = n % 2, COLS * (n // 2), (COLS, P)[n // 2]
            v = cqkv[:, t, at:at + width]
            dve.scalar_tensor_tensor(v, v, c.rstd[:, 8 + n:9 + n], bc[("qa_g", "kva_g")[n // 2]][:],
                                     ALU.mult, ALU.mult).then_inc(c.dve_done, ev.one("dve", f"low.n{n}"))

    def low_pe(pe):
        pe.wait_ge(c.dve_done, ev.at("low.n3"))
        pe.wait_ge(c.dve_done, ev.at("taps.out"))
        for t in range(TT):
            for k in range(3):
                last = pe.transpose(c.psum[:, 6 + t, k * P:(k + 1) * P], cqkv[:, t, k * P:(k + 1) * P], c.ident[:])
            last.then_inc(c.pe_done, ev.one("pe", f"low.turned{t}"))

    def low_split(eng, name, t):
        src = c.psum[:, 6 + t, 0:3 * P].rearrange("p (k t) -> p k t", k=3)
        ts = slice(t * P, (t + 1) * P)
        if name == "act":
            eng.wait_ge(c.pe_done, ev.at(f"low.turned{t}"))
            eng.activation(low_hi[:, :, ts], src, ACT.Copy).then_inc(c.act_done, ev.one("act", f"low.hi{t}"))
        else:
            eng.wait_ge(c.act_done, ev.at(f"low.hi{t}"))
            eng.tensor_tensor(low_lo[:, :, ts], src, low_hi[:, :, ts].bitcast(F32), ALU.subtract)\
                .then_inc(c.dve_done, ev.one("dve", f"low.lo{t}"))

    def up_pe(pe):
        slot = UP % SLOTS
        pe.wait_ge(c.act_done, ev.at(f"blk{UP - 1}.out"))
        pe.wait_ge(c.dve_done, ev.at("low.lo1"))
        q_hi, q_lo = (w[slot][:, 0:UP_Q].rearrange("p (kt n) -> p kt n", kt=2) for w in (c.w_hi, c.w_lo))
        k_hi, k_lo = (w[slot][:, UP_Q:UP_Q + 512].rearrange("p (kt n) -> p kt n", kt=1) for w in (c.w_hi, c.w_lo))
        tokens_by_features(pe, [c.psum[:, t, 0:MLA_HEADS * QK] for t in range(TT)], q_hi, q_lo, low_hi, low_lo, 2)
        tokens_by_features(pe, [c.psum[:, 6 + t, :] for t in range(TT)], k_hi, k_lo, low_hi[:, 2:3, :],
                           low_lo[:, 2:3, :], 1).then_inc(c.w_used[slot], 1)

    def keys_pool(pool):
        pool.wait_ge(c.act_done, ev.at(f"blk{UP}.out"))
        pool.wait_ge(c.act_done, ev.at(f"blk{CKV}.out"))
        for t in range(TT):
            hs = slice(t * MLA_HEADS, (t + 1) * MLA_HEADS)
            pool.tensor_copy(qk[:, 1, hs, 0:NOPE],
                             kv_up[:, t, :].rearrange("p (h n) -> p h n", h=MLA_HEADS)[:, :, 0:NOPE])
            last = pool.tensor_copy(qk[:, 1, hs, NOPE:QK], cqkv[:, t, COLS + P:COLS + P + ROPE].unsqueeze(1)
                                    .broadcast_to([P, MLA_HEADS, ROPE]))
        last.then_inc(c.pool_done, ev.one("pool", "keys"))

    def qk_norm_dve(dve, w):
        v = qk[:, w, :, :]
        tag = f"qk{w}"
        dve.wait_ge(c.pool_done, ev.at("keys"))
        dve.wait_ge(c.dve_done, ev.at("low.n3"))
        dve.wait_ge(c.pe_done, ev.at("low.turned1"))
        if w:
            dve.wait_ge(c.dve_done, ev.at("qk0.sum"))
            dve.wait_ge(c.pool_done, ev.at("qk0.factor"))
            dve.wait_ge(c.dve_done, ev.at("qk0.scaled"))
        rms_sum(dve, tag, v, scratch[:, 0:8 * QK].rearrange("p (n e) -> p n e", e=QK), 8, ("p (n o) -> p n o", dict(o=1)))
        dve.wait_ge(c.pool_done, ev.at(f"{tag}.factor"))
        dve.tensor_tensor(v, v, factor[:, 0:8].unsqueeze(2).broadcast_to([P, 8, QK]), ALU.mult)\
            .then_inc(c.dve_done, ev.one("dve", f"{tag}.scaled"))
        dve.wait_ge(c.dve_done, ev.at(f"{tag}.scaled"))
        dve.tensor_tensor(v, v, bc[("qn_g", "kn_g")[w]][:].unsqueeze(1).broadcast_to([P, 8, QK]),
                          ALU.mult).then_inc(c.dve_done, ev.one("dve", f"{tag}.normed"))

    def rope_pool(pool, w):
        n = ROPE // 2
        v = qk[:, w, :, :].rearrange("p (t h) e -> p t h e", t=TT)
        x1, x2 = v[:, :, :, NOPE:NOPE + n], v[:, :, :, NOPE + n:QK]
        cos, sin = (t[:].unsqueeze(2).broadcast_to([P, TT, MLA_HEADS, n]) for t in (s.cos, s.sin))
        tmp = [scratch[:, i * 128:(i + 1) * 128].rearrange("p (t h e) -> p t h e", t=TT, h=MLA_HEADS)
               for i in range(4)]
        pool.wait_ge(c.dve_done, ev.at(f"qk{w}.normed"))
        pool.wait_ge(c.dve_done, ev.at("qk1.sum"))
        if w:
            pool.wait_ge(c.pool_done, ev.at("rotated0"))
        for i, (x, cs) in enumerate(((x1, cos), (x2, sin), (x2, cos), (x1, sin))):
            pool.tensor_tensor(tmp[i], x, cs, ALU.mult).then_inc(c.pool_done, ev.one("pool", f"rope{w}.{i}"))
        pool.wait_ge(c.pool_done, ev.at(f"rope{w}.3"))
        pool.tensor_tensor(x1, tmp[0], tmp[1], ALU.subtract)
        pool.tensor_tensor(x2, tmp[2], tmp[3], ALU.add).then_inc(c.pool_done, ev.one("pool", f"rotated{w}"))

    def turn_heads_pe(pe, tag, view, width, after, banks):
        for name in after:
            pe.wait_ge(*ev.when(c, name))
        for g in range(2):
            for j in range(2):
                for t in range(TT):
                    at = (2 * j + t) * P
                    last = pe.transpose(c.psum[0:width, banks[g], at:at + P], view(t, 2 * g + j), c.ident[:])
            last.then_inc(c.pe_done, ev.one("pe", f"{tag}.turned{g}"))

    def turn_heads_out(eng, tag, dst, width, banks, g, after=()):
        eng.wait_ge(c.pe_done, ev.at(f"{tag}.turned{g}"))
        for name in after:
            eng.wait_ge(*ev.when(c, name))
        eng.activation(dst[0:width, 2 * g:2 * g + 2, :].rearrange("p h t -> p (h t)"),
                       c.psum[0:width, banks[g], :], ACT.Copy).then_inc(c.act_done, ev.one("act", f"{tag}.T{g}"))

    def attention(tag, qT, kT, width, value, out, ready):
        scale = width ** -0.5

        @block.tensor
        def _(pe):
            for name in ready:
                pe.wait_ge(*ev.when(c, name))
            for step in range(XA_HEADS + 2):
                h = step
                if h < XA_HEADS:
                    if h >= 2:
                        pe.wait_ge(c.act_done, ev.at(f"{tag}.p{h - 2}"))
                    for t in range(TT):
                        last = pe.matmul(two(4 + h % 2)[:, t, :], qT[0:width, h, t * P:(t + 1) * P],
                                         kT[0:width, h, :], start=True, stop=True)
                    last.then_inc(c.pe_done, ev.one("pe", f"{tag}.s{h}"))
                h = step - 1
                if 0 <= h < XA_HEADS:
                    pe.wait_ge(c.act_done, ev.at(f"{tag}.p{h}"))
                    if h:
                        pe.wait_ge(c.dve_done, ev.at(f"{tag}.pT{h - 1}"))
                    for k in range(TT):
                        for t in range(TT):
                            at = (2 * k + t) * P
                            last = pe.transpose(c.psum[:, 6, at:at + P], probs[:, t, k * P:(k + 1) * P], c.ident[:])
                    last.then_inc(c.pe_done, ev.one("pe", f"{tag}.turned{h}"))
                h = step - 2
                if 0 <= h < XA_HEADS:
                    pe.wait_ge(c.dve_done, ev.at(f"{tag}.pT{h}"))
                    for t in range(TT):
                        for k in range(TT):
                            last = pe.matmul(two(7)[:, t, h * HG_D:(h + 1) * HG_D],
                                             probsT[:, k, t * P:(t + 1) * P], value(h, k),
                                             start=(k == 0), stop=(k == TT - 1))
                    last.then_inc(c.pe_done, ev.one("pe", f"{tag}.o{h}"))

        @block.scalar
        def _(act):
            for h in range(XA_HEADS):
                act.wait_ge(c.dve_done, ev.at(f"{tag}.neg{h}"))
                if h:
                    act.wait_ge(c.pe_done, ev.at(f"{tag}.turned{h - 1}"))
                for t in range(TT):
                    last = act.activation(probs[:, t, :], two(4 + h % 2)[:, t, :], ACT.Exp, scale=scale,
                                          bias=row_max[:, t, h:h + 1], accum_out=row_sum[:, t, h:h + 1])
                last.then_inc(c.act_done, ev.one("act", f"{tag}.p{h}"))

        @block.vector
        def _(dve):
            for h in range(XA_HEADS + 1):
                if h < XA_HEADS:
                    dve.wait_ge(c.pe_done, ev.at(f"{tag}.s{h}"))
                    m = row_max[:, 0:TT, h:h + 1]
                    dve.tensor_reduce(m, two(4 + h % 2), AX_X, ALU.max)\
                        .then_inc(c.dve_done, ev.one("dve", f"{tag}.max{h}"))
                    dve.wait_ge(c.dve_done, ev.at(f"{tag}.max{h}"))
                    dve.tensor_scalar(m, m, -scale, None, ALU.mult)\
                        .then_inc(c.dve_done, ev.one("dve", f"{tag}.neg{h}"))
                if h:
                    dve.wait_ge(c.pe_done, ev.at(f"{tag}.turned{h - 1}"))
                    if h > 1:
                        dve.wait_ge(c.pe_done, ev.at(f"{tag}.o{h - 2}"))
                    dve.tensor_copy(probsT.rearrange("p k t -> p (k t)"), c.psum[:, 6, :])\
                        .then_inc(c.dve_done, ev.one("dve", f"{tag}.pT{h - 1}"))
            dve.wait_ge(c.act_done, ev.at(f"{tag}.p{XA_HEADS - 1}"))
            dve.reciprocal(row_sum[:, 0:TT, :], row_sum[:, 0:TT, :]).then_inc(c.dve_done, ev.one("dve", f"{tag}.rden"))
            dve.wait_ge(c.dve_done, ev.at(f"{tag}.rden"))
            dve.wait_ge(c.pe_done, ev.at(f"{tag}.o{XA_HEADS - 1}"))
            dve.tensor_tensor(
 heads_of(out), two(7).rearrange("p t (h e) -> p t h e", e=HG_D),
 row_sum[:, 0:TT, :].unsqueeze(3).broadcast_to([P, TT, XA_HEADS, HG_D]), ALU.mult)\
                .then_inc(c.dve_done, ev.one("dve", f"{tag}.out"))


    def conv_dve(dve, tag, padded, out, tap0, count, part):
        for k in part:
            for ct in range(2):
                src, w = padded[:, ct, k:k + SEQ], taps[:, ct, tap0 + k:tap0 + k + 1]
                if k == 0:
                    bias = taps[:, ct, tap0 + count:tap0 + count + 1]
                    ins = dve.tensor_scalar(out[:, ct, :], src, w, bias, ALU.mult, ALU.add)
                else:
                    dve.wait_ge(c.dve_done, ev.at(f"{tag}.{k - 1}.{ct}"))
                    ins = dve.scalar_tensor_tensor(out[:, ct, :], src, w, out[:, ct, :], ALU.mult, ALU.add)
                ins.then_inc(c.dve_done, ev.one("dve", f"{tag}.{k}.{ct}"))

    def turn_tiles_pe(pe, tag, source, b, after):
        for name in after:
            pe.wait_ge(*ev.when(c, name))
        for t in range(TT):
            for ct in range(2):
                last = pe.transpose(c.psum[:, b, (2 * t + ct) * P:(2 * t + ct + 1) * P],
                                    source[:, ct, t * P:(t + 1) * P], c.ident[:])
        last.then_inc(c.pe_done, ev.one("pe", f"{tag}.turned"))

    def conf_norm_dve(dve):
        dve.wait_ge(c.pe_done, ev.at("conf.turned"))
        for t in range(TT):
            last = dve.bn_stats(stats[:, t, :], two(4)[:, t, :])
        last.then_inc(c.dve_done, ev.one("dve", "conf.stats"))
        dve.wait_ge(c.dve_done, ev.at("conf.stats"))
        for t in range(TT):
            last = dve.bn_aggr(mean_var[:, t, :], stats[:, t, :])
        last.then_inc(c.dve_done, ev.one("dve", "conf.mean_var"))
        dve.wait_ge(c.pool_done, ev.at("conf.rstd"))
        dve.wait_ge(c.pool_done, ev.at("rotated1"))
        for t in range(TT):
            dve.tensor_scalar(cat_part(0)[:, t, :], two(4)[:, t, :], mean_var[:, t, 0:1],
                              c.rstd[:, 4 + t:5 + t], ALU.subtract, ALU.mult)\
                .then_inc(c.dve_done, ev.one("dve", f"conf.n{t}"))
        dve.wait_ge(c.dve_done, ev.at("conf.n1"))
        dve.tensor_tensor(cat_part(0), cat_part(0), bc["ln_g"][:].unsqueeze(1).broadcast_to(
[P, TT, GROUP]), ALU.mult).then_inc(c.dve_done, ev.one("dve", "conf.g"))
        dve.wait_ge(c.dve_done, ev.at("conf.g"))
        dve.tensor_tensor(cat_part(0), cat_part(0), bc["ln_b"][:].unsqueeze(1).broadcast_to(
[P, TT, GROUP]), ALU.add).then_inc(c.dve_done, ev.one("dve", "conf.b"))

    def conf_pool(pool):
        pool.wait_ge(c.dve_done, ev.at("conf.mean_var"))
        pool.tensor_scalar(c.rstd[:, 4:4 + TT], mean_var[:, :, 1], RMS_EPS, None, ALU.add)\
            .then_inc(c.pool_done, ev.one("pool", "conf.var"))
        pool.wait_ge(c.pool_done, ev.at("conf.var"))
        pool.tensor_tensor(c.rstd[:, 4:4 + TT], c.rstd[:, 4:4 + TT], c.half_power[:, 0:TT],
                           ALU.pow).then_inc(c.pool_done, ev.one("pool", "conf.rstd"))

    with nc.Block() as block:
        @block.gpsimd
        def _(pool):
            load_gain(c, pool, "gain_post", dram["g_mem_2"][layer], [])
            load_gain(c, pool, "gain_pre", dram["g_mix_2"][layer], [])
            small = c.params["small"]
            for name, source in (("qa_g", "m_qa_g_2"), ("kva_g", "m_kva_g_2"), ("qn_g", "m_qn_g_2"),
                                 ("kn_g", "m_kn_g_2"), ("ln_g", "a_ln_g_2"), ("ln_b", "a_ln_b_2"),
                                 ("onorm_g", "h_onorm_g_2"), ("xqn_g", "x_qn_g_2"), ("xkn_g", "x_kn_g_2")):
                pool.dma_start(bc[name][:], dram[source][layer].partition_broadcast(P)).then_inc(small, 16)
            pool.dma_start(taps_rows[0:31, :], dram["a_dw_w_2"][layer]).then_inc(small, 16)
            pool.dma_start(taps_rows[31:32, :], dram["a_dw_b_2"][layer].unsqueeze(0)).then_inc(small, 16)
            pool.dma_start(taps_rows[32:35, :], dram["c_dw_w_2"][layer]).then_inc(small, 16)
            pool.dma_start(taps_rows[35:36, :], dram["c_dw_b_2"][layer].unsqueeze(0)).then_inc(small, 16)

        @block.sync
        def _(sp):
            sp.dma_start(mem, dram["mem_2"].rearrange("o (t p) n -> p (o t) n", p=P)).then_inc(c.mem_loaded, 16)
            for i in range(WO):
                slot = i % SLOTS
                if i == UP:
                    load_weights(c, sp, slot, i // SLOTS, False, dram["m_wuq_2"].rearrange(
                        "l (kt p) n -> l p kt n", p=P)[layer], c.stage[slot][:, 0:UP_Q].rearrange(
                        "p (kt n) -> p kt n", kt=2))
                    sp.dma_start(c.stage[slot][:, UP_Q:UP_Q + 512], dram["m_wukv_2"][layer])\
                      .then_inc(c.up_kv_loaded, 16)
                else:
                    load(sp, i, columns(c, "x_wkv_2" if i <= KV1 else "w_in_2", layer, first_col[i]))
            for i in range(4):
                load(sp, WO + i, rows(c, "w_out_2", layer, i))
            load(sp, XQ, columns(c, "x_wq_2", layer, 0))
            load(sp, XO, rows(c, "x_wo_2", layer, 0))

        @block.scalar
        def _(act):
            for n in range(SLOTS):
                hi(c, act, n)
            act.wait_ge(c.mem_loaded, 16)

        @block.vector
        def _(dve):
            for n in range(SLOTS):
                lo(c, dve, n)
            dve.wait_ge(c.mem_loaded, 16)

        pre_norm(c, block, "mem", [[], []], 1, mem, ("gain_post", c.gain_post), (bT_hi, bT_lo))
        pre_norm(c, block, "mix", [["mem.turned1"], ["mem.turned3"]], 1)

        TAPS = -(-CONF_TAPS // (WO - CG))

        def part_of_block(i):
            return UP_Q + 512 if i == UP else BLOCK

        @block.tensor
        def _(pe):
            pe.wait_ge(c.dve_done, ev.at("lower"))
            for ct in range(2):
                last = pe.transpose(c.psum[:, 6, ct * 36:(ct + 1) * 36], taps_rows[:, ct * P:(ct + 1) * P],
                                    c.ident[0:36, 0:36])
            last.then_inc(c.pe_done, ev.one("pe", "taps.turned"))
            for i in range(WO):
                if i == KV0:
                    pe.wait_ge(c.dve_done, ev.at("mem.lo3"))
                    pe.wait_ge(c.dve_done, ev.at("mix.lo3"))
                if i >= 2:
                    pe.wait_ge(c.act_done, ev.at(f"blk{i - 2}.out"))
                if i == UP + 1:
                    pe.wait_ge(c.act_done, ev.at(f"blk{UP}.out"))
                wait_weights(c, pe, i)
                w_hi, w_lo = as_columns(c.w_hi[i % SLOTS]), as_columns(c.w_lo[i % SLOTS])
                a = (bT_hi, bT_lo) if i <= KV1 else (c.aT_hi, c.aT_lo)
                if i == UP:
                    up_pe(pe)
                elif i in by_tokens:
                    tokens_by_features(pe, [two(i % 2)[:, t, :] for t in range(TT)], w_hi, w_lo, *a, KT)\
                        .then_inc(c.w_used[i % SLOTS], 1)
                else:
                    features_by_tokens(pe, two(i % 2), w_hi, w_lo, *a).then_inc(c.w_used[i % SLOTS], 1)
                if i == CA:
                    low_pe(pe)
                if i >= CKV:
                    product_pe(pe, i - CKV)
                if i == SX:
                    turn_heads_pe(pe, "q", lambda t, h: qk[:, 0, t * MLA_HEADS + h, :], QK,
                                  ["rotated0", f"blk{UP}.out"], (6, 7))
                if i == SB:
                    turn_heads_pe(pe, "k", lambda t, h: qk[:, 1, t * MLA_HEADS + h, :], QK, ["rotated1", "q.T1"],
                                  (6, 7))
            weigh_pe(pe)
            for tag, tile, b, last in (("conf", conf_out, 4, [f"conf.{CONF_TAPS - 1}.{ct}" for ct in range(2)]),
                                       ("short", short_out, 5, ["short.y"])):
                turn_tiles_pe(pe, tag, tile, b, last)

        @block.scalar
        def _(act):
            for i in range(WO):
                used(act, i)
                src = two(i % 2)
                if i <= KV1:
                    ins = act.activation(kv_mem[:, :, COLS * i:COLS * (i + 1)], src, ACT.Copy)
                elif i == HQ:
                    for side in range(2):
                        for direction in range(2):
                            ins = act.activation(head_side(q2, direction, side),
                                                 src[side * HG_D:(side + 1) * HG_D, :, :], ACT.Copy)
                elif i in (ZF, ZB):
                    for side in range(2):
                        for tile, sign in ((f, 1.0), (kk, -1.0)):
                            ins = act.activation(head_side(tile, i - ZF, side),
                                                 src[side * HG_D:(side + 1) * HG_D, :, :], ACT.Sigmoid, scale=sign)
                elif i == CQ:
                    act.wait_ge(c.pe_done, ev.at("mix.turned3"))
                    ins = act.activation(cqkv[:, :, 0:COLS], src, ACT.Copy)
                elif i == CKV:
                    ins = act.activation(cqkv[:, :, COLS:COLS + P + ROPE], src[:, :, CKV_AT:COLS], ACT.Copy)
                elif i == HV:
                    ins = act.activation(hv[:], src, ACT.Copy)
                elif i == HG:
                    ins = act.activation(hg[:], src, ACT.Silu)
                elif i == UP:
                    for t in range(TT):
                        act.activation(qk[:, 0, t * MLA_HEADS:(t + 1) * MLA_HEADS, :], c.psum[:, t, 0:MLA_HEADS * QK]
                                       .rearrange("p (h e) -> p h e", h=MLA_HEADS), ACT.Copy)
                        ins = act.activation(kv_up[:, t, :], c.psum[:, 6 + t, :], ACT.Copy)
                elif i == CA:
                    ins = act.activation(conf_out[:], src, ACT.Copy)
                elif i == CG:
                    act.wait_ge(c.pool_done, ev.at("padding"))
                    ins = act.activation(conf[:, :, 15:15 + SEQ], src, ACT.Sigmoid)
                elif i == SC:
                    ins = act.activation(short_out[:], src, ACT.Copy)
                elif i == SX:
                    ins = act.activation(short[:, :, 1:1 + SEQ], src, ACT.Copy)
                if i != SB:
                    ins.then_inc(c.act_done, ev.one("act", f"blk{i}.out"))
                if i + SLOTS == UP:
                    act.wait_ge(c.up_kv_loaded, 16)
                hi(c, act, i + SLOTS, part_of_block(i + SLOTS))
                if i == ZB:
                    gates_act(act)
                    exp_act(act, 0)
                if i == CKV:
                    low_act(act)
                if i == CA:
                    for t in range(TT):
                        low_split(act, "act", t)
                if 1 <= i - ZB < len(LEVELS) - 1:
                    exp_act(act, i - ZB)
                if i == SB:
                    for g in range(2):
                        turn_heads_out(act, "q", mla_T[0], QK, (6, 7), g, [f"level{len(LEVELS) - 3}.product"])
                    for g in range(2):
                        turn_heads_out(act, "k", mla_T[1], QK, (6, 7), g)
            act.wait_ge(c.pe_done, ev.at("hg.o"))
            act.wait_ge(c.pool_done, ev.at("rotated1"))
            act.activation(cat_part(1), two(2), ACT.Copy).then_inc(c.act_done, ev.one("act", "hg.copied"))
            act.wait_ge(c.dve_done, ev.at("conf.b"))
            act.activation(cat_part(0), cat_part(0), ACT.Silu).then_inc(c.act_done, ev.one("act", "cat0"))
            act.wait_ge(c.pe_done, ev.at("short.turned"))
            act.activation(cat_part(2), two(5), ACT.Copy).then_inc(c.act_done, ev.one("act", "cat2"))

        @block.vector
        def _(dve):
            wait_params(c, dve, "small", SMALL)
            dve.tensor_copy(lower[:], s.lower[:, bass.ds(layer, 1), :].rearrange("p o h -> p (o h)"))\
                .then_inc(c.dve_done, ev.one("dve", "lower"))
            dve.wait_ge(c.pe_done, ev.at("taps.turned"))
            dve.tensor_copy(taps[:].rearrange("p c k -> p (c k)"), c.psum[:, 6, 0:72])\
                .then_inc(c.dve_done, ev.one("dve", "taps.out"))
            for i in range(WO):
                lo(c, dve, i + SLOTS, part_of_block(i + SLOTS))
                j = i - ZB
                if j == 0:
                    gates_dve(dve)
                    sums_dve(dve)
                if 1 <= j < len(LEVELS):
                    scale_dve(dve, j - 1)
                if 0 <= j < len(LEVELS) - 1:
                    border_dve(dve, j)
                if 2 <= j < len(LEVELS) + 2:
                    keep_dve(dve, j - 2)
                if i == CKV:
                    low_dve(dve)
                if i == CA:
                    for t in range(TT):
                        low_split(dve, "dve", t)
                if i == UP + 1:
                    qk_norm_dve(dve, 0)
                    qk_norm_dve(dve, 1)
                if i == CG:
                    dve.wait_ge(c.act_done, ev.at(f"blk{CG}.out"))
                    dve.wait_ge(c.dve_done, ev.at("taps.out"))
                    dve.tensor_tensor(conf[:, :, 15:15 + SEQ], conf[:, :, 15:15 + SEQ],
                                      conf_out[:], ALU.mult).then_inc(c.dve_done, ev.one("dve", "conf.h"))
                    dve.wait_ge(c.dve_done, ev.at("conf.h"))
                if i >= CG:
                    conv_dve(dve, "conf", conf, conf_out, 0, CONF_TAPS, range(TAPS * (i - CG), min(TAPS * (i - CG + 1), CONF_TAPS)))
                if i == SX:
                    dve.wait_ge(c.act_done, ev.at(f"blk{SX}.out"))
                    dve.tensor_tensor(short[:, :, 1:1 + SEQ], short[:, :, 1:1 + SEQ],
                                      short_out[:], ALU.mult).then_inc(c.dve_done, ev.one("dve", "short.h"))
                    dve.wait_ge(c.dve_done, ev.at("short.h"))
                    conv_dve(dve, "short", short, short_out, 32, SHORT_TAPS, range(SHORT_TAPS))
                if i == SB:
                    used(dve, SB)
                    dve.wait_ge(c.dve_done, ev.at(f"short.{SHORT_TAPS - 1}.0"))
                    dve.wait_ge(c.dve_done, ev.at(f"short.{SHORT_TAPS - 1}.1"))
                    dve.tensor_tensor(short_out[:], short_out[:], two(SB % 2), ALU.mult)\
                        .then_inc(c.dve_done, ev.one("dve", "short.y"))
            conf_norm_dve(dve)
            hg_norm_dve(dve)

        @block.gpsimd
        def _(pool):
            load_gain(c, pool, "gain_post", dram["g_branch_2"][layer], ["mem.xn1"])
            load_gain(c, pool, "gain_pre", dram["g_xq_2"][layer], ["mix.xn1"])
            pool.memset(conf[:], 0.0)
            pool.memset(short[:], 0.0).then_inc(c.pool_done, ev.one("pool", "padding"))
            pool.memset(s.again[:], 1.0).then_inc(c.pool_done, ev.one("pool", "ones"))
            pool.wait_ge(c.pool_done, ev.at("ones"))
            again_pool(pool, SEQ)
            pool.wait_ge(c.dve_done, ev.at(f"prefix{SEQ}"))
            again_pool(pool, HG_CHUNK)
            sums_pool(pool, SEQ)
            sums_pool(pool, HG_CHUNK)
            for j in range(len(LEVELS) - 1):
                query_pool(pool, j)
                if j == CKV - ZB - 1:
                    low_pool(pool)
                if j == UP - ZB:
                    keys_pool(pool)
                    rms_power(pool, "qk0", 8, QK)
                    rms_power(pool, "qk1", 8, QK)
                    rope_pool(pool, 0)
                    rope_pool(pool, 1)
            conf_pool(pool)
            rms_power(pool, "hgn", 8, HG_D)

        attention("mla", mla_T[0], mla_T[1], QK,
                  lambda h, k: kv_up[:, k, 2 * NOPE * h + NOPE:2 * NOPE * (h + 1)], cat_part(3),
                  ["q.T1", "k.T1", "conf.b", "cat2"])

        @block.vector
        def _(dve):
            dve.wait_ge(c.act_done, ev.at("cat0"))
            dve.wait_ge(c.dve_done, ev.at("cat1"))
            dve.wait_ge(c.act_done, ev.at("cat2"))
            dve.wait_ge(c.dve_done, ev.at("mla.out"))
            for t in range(TT):
                v = cat[:, t, :].rearrange("p (g n) -> p g n", g=4)
                if t:
                    dve.wait_ge(c.dve_done, ev.at("group0"))
                dve.tensor_tensor(squares.rearrange("p (g n) -> p g n", g=4), v, v, ALU.mult)\
                    .then_inc(c.dve_done, ev.one("dve", f"group_sq{t}"))
                dve.wait_ge(c.dve_done, ev.at(f"group_sq{t}"))
                dve.tensor_reduce(sq_sum[:, 4 * t:4 * t + 4].unsqueeze(2), squares.rearrange(
     "p (g n) -> p g n", g=4), AX_X, ALU.add).then_inc(c.dve_done, ev.one("dve", f"group{t}"))
            wait_params(c, dve, "gain_post", 2)
            dve.wait_ge(c.pool_done, ev.at("groups.factor"))
            for t in range(TT):
                v = cat[:, t, :].rearrange("p (g n) -> p g n", g=4)
                dve.tensor_tensor(v, v, factor[:, 4 * t:4 * t + 4].unsqueeze(2).broadcast_to(
     [P, 4, GROUP]), ALU.mult).then_inc(c.dve_done, ev.one("dve", f"group_scaled{t}"))
            for t in range(TT):
                dve.wait_ge(c.dve_done, ev.at(f"group_scaled{t}"))
                dve.tensor_tensor(cat[:, t, :], cat[:, t, :], c.gain_post[:], ALU.mult)\
                    .then_inc(c.dve_done, ev.one("dve", f"cat.n{t}"))

        @block.gpsimd
        def _(pool):
            pool.wait_ge(c.dve_done, ev.at("group0"))
            pool.wait_ge(c.dve_done, ev.at("group1"))
            pool.tensor_scalar(factor[:, 0:8], sq_sum[:, 0:8], 1.0 / GROUP, RMS_EPS, ALU.mult,
                               ALU.add).then_inc(c.pool_done, ev.one("pool", "groups.meansq"))
            pool.wait_ge(c.pool_done, ev.at("groups.meansq"))
            pool.tensor_tensor(factor[:, 0:8], factor[:, 0:8], c.half_power[:, 0:8], ALU.pow)\
                .then_inc(c.pool_done, ev.one("pool", "groups.factor"))

        transpose_split(c, block, "cat", cat, KT, [["cat.n0", "hg.copied", "short.y"], ["cat.n1"]], [0, 1, 2, 3])

        @block.tensor
        def _(pe):
            pe.wait_ge(c.dve_done, ev.at("cat.lo3"))
            pe.wait_ge(c.dve_done, ev.at("mla.out"))
            for i in range(4):
                n = WO + i
                wait_weights(c, pe, n)
                row_block(c, pe, as_rows(c.w_hi[n % SLOTS]), as_rows(c.w_lo[n % SLOTS]),
                          c.aT_hi[:, 2 * i:2 * i + 2, :], c.aT_lo[:, 2 * i:2 * i + 2, :], i == 0, "wo" if i == 3 else None)\
                    .then_inc(c.w_used[n % SLOTS], 1)

        @block.scalar
        def _(act):
            for n in range(WO, XQ - 1):
                hi(c, act, n + SLOTS)

        @block.vector
        def _(dve):
            for n in range(WO, XQ - 1):
                lo(c, dve, n + SLOTS)
                if n == WO:
                    head_norm_dve(dve, "xk", mem_heads[:, :, :, 0:XA_D], "xkn_g", [f"blk{KV1}.out", "group1"])

        @block.gpsimd
        def _(pool):
            rms_power(pool, "xk", 8, XA_D)
        add_to_x(c, block, "wo", WO // SLOTS + 2, 0)

        @block.tensor
        def _(pe):
            turn_heads_pe(pe, "xk", lambda t, h: mem_heads[:, t, h, :], 2 * XA_D, ["xk.normed", "cat.lo3"], (2, 3))

        @block.scalar
        def _(act):
            for g in range(2):
                turn_heads_out(act, "xk", mem_T[1], XA_D, (2, 3), g)
        pre_norm(c, block, "xq", [["wo.x0"], ["wo.x1", "xk.T1"]], 2)
        split_next(c, block, XQ - 1 + SLOTS)

        @block.gpsimd
        def _(pool):
            load_gain(c, pool, "gain_pre", dram["g_ffn_2"][layer], ["xq.xn1"])
            rms_power(pool, "xqh", 8, XA_D)

        @block.tensor
        def _(pe):
            pe.wait_ge(c.dve_done, ev.at("xq.lo3"))
            wait_weights(c, pe, XQ)
            slot = XQ % SLOTS
            tokens_by_features(pe, [two(0)[:, t, :] for t in range(TT)], as_columns(c.w_hi[slot]),
                               as_columns(c.w_lo[slot]), c.aT_hi, c.aT_lo, KT).then_inc(c.w_used[slot], 1)
            turn_tiles_pe(pe, "xq_h", conf_out, 2, ["xqh.normed"])

        @block.scalar
        def _(act):
            used(act, XQ)
            act.activation(conf_out[:], two(0), ACT.Copy).then_inc(c.act_done, ev.one("act", "xq.out"))
            hi(c, act, XQ + SLOTS)
            act.wait_ge(c.pe_done, ev.at("xq_h.turned"))
            for side in range(2):
                last = act.activation(mem_T[0][0:XA_D, side:side + 3:2, :], two(2)[side * XA_D:(side + 1) * XA_D],
                                      ACT.Copy)
            last.then_inc(c.act_done, ev.one("act", "xq_h.T"))

        @block.vector
        def _(dve):
            head_norm_dve(dve, "xqh", xq, "xqn_g", ["xq.out"])
            lo(c, dve, XQ + SLOTS)
        attention("xa", mem_T[0], mem_T[1], XA_D,
                  lambda h, k: kv_mem[:, k, 2 * XA_D * h + XA_D:2 * XA_D * (h + 1)], short_out[:],
                  ["xq_h.T", "xk.T1", "wo.x1"])
        transpose_split(c, block, "xo", short_out, 2, [["xa.out"], ["xa.out"]], [2, 3], low_hi, low_lo)

        @block.tensor
        def _(pe):
            pe.wait_ge(c.dve_done, ev.at("xo.lo1"))
            wait_weights(c, pe, XO)
            slot = XO % SLOTS
            row_block(c, pe, as_rows(c.w_hi[slot]), as_rows(c.w_lo[slot]), low_hi[:, 0:2, :], low_lo[:, 0:2, :],
                      True, "xo_x").then_inc(c.w_used[slot], 1)

        add_to_x(c, block, "xo_x", XO // SLOTS + 1, XO % SLOTS)

        pre_norm(c, block, "ffn", [["xo_x.x0"], ["xo_x.x1"]], 3)
        split_next(c, block, XO + SLOTS)
        ffn(c, block, "ffn", "f_w13_2", "f_w2_2", layer, FFN_USE, 0, "ffn.lo3", True, ["xo_x.x1"])
        add_to_x(c, block, "ffn", FFN_USE + FF_STEPS)


def constants(c, block, window_mask, causal_T):
    @block.gpsimd
    def _(pool):
        done = c.setup_done
        pool.memset(c.ident[:], 0.0)
        pool.memset(c.zeros[:], 0.0)
        pool.memset(c.half_power[:], -0.5)
        pool.memset(window_mask[:], 0.0)
        pool.memset(causal_T[:], 1.0).then_inc(done, 1)
        pool.wait_ge(done, 1)
        pool.affine_select(out=c.ident[:], in_=c.ident[:], compare_op=ALU.not_equal, fill=1.0, base=0,
                           pattern=[[-1, P]], channel_multiplier=1)
        for part, base, step, sign in ((0, 0, -1, 1), (1, -1, 1, -1), (2, 0, -1, 1)):
            own = window_mask[:, part * P:(part + 1) * P]
            pool.affine_select(out=own, in_=own, compare_op=ALU.is_ge, fill=MASKED, base=base,
                               pattern=[[step, P]], channel_multiplier=sign)
        pool.affine_select(out=causal_T[:], in_=causal_T[:], compare_op=ALU.is_ge, fill=0.0, base=0,
                           pattern=[[1, P]], channel_multiplier=-1).then_inc(done, 1)
        pool.wait_ge(done, 2)


def program(nc, dram, out, known):
    with ExitStack() as ctx:
        c = allocate(nc, ctx, dram, known)
        token_major = dram["x"].rearrange("o (t p) n -> p (o t) n", p=P)
        with ExitStack() as first:
            window_mask = first.enter_context(nc.sbuf_tensor("window_mask", [P, 3 * P], F32))
            causal_T = first.enter_context(nc.sbuf_tensor("causal_T", [P, P], F32))
            with nc.Block() as block:
                @block.sync
                def _(sp):
                    sp.dma_start(c.x[:], token_major).then_inc(c.x_loaded, 16)
                    sp.wait_ge(c.x_loaded, 16)
                constants(c, block, window_mask, causal_T)
            start_layers(c, gain_pre=3, gain_post=3, small=5)
            with nc.Fori(0, DEPTH) as layer:
                first_block_layer(c, layer, (window_mask, causal_T))
                clear_layer(c)
        with ExitStack() as second:
            s = second_tiles(c, second)
            second_setup(c, s)
            start_layers(c, gain_pre=3, gain_post=2, small=SMALL)
            with nc.Fori(0, DEPTH) as layer:
                second_block_layer(c, s, layer)
                clear_layer(c)
        with nc.Block() as block:
            @block.sync
            def _(sp):
                sp.dma_start(out.rearrange("o (t p) n -> p (o t) n", p=P), c.x[:]).then_inc(c.stored, 16)
                sp.wait_ge(c.stored, 16)
        return c.ev.table


_SHAPE = (1, SEQ, D)


def kernel(**inputs):
    from concourse.bacc import Bacc
    from concourse.bass_utils import run_bass_kernel_spmd

    inputs = {name: np.ascontiguousarray(a) for name, a in inputs.items()}

    def build(known):
        nc = Bacc("TRN2", target_bir_lowering=False, num_devices=1)
        dram = {name: nc.dram_tensor(f"in_{name}", a.shape, mybir.dt.from_np(a.dtype), kind="ExternalInput").ap()
                for name, a in inputs.items()}
        out = nc.dram_tensor("y", _SHAPE, F32, kind="ExternalOutput").ap()
        return nc, program(nc, dram, out, known)

    _, counts = build(None)
    nc, _ = build(counts)
    result = run_bass_kernel_spmd(nc, [{f"in_{name}": a for name, a in inputs.items()}], core_ids=[0])
    return result.results[0]["y"]
```

```python
from contextlib import ExitStack

import numpy as np
import concourse.bass as bass
from concourse import mybir

P = 128
F32 = mybir.dt.float32
F32R = mybir.dt.float32r
BF16 = mybir.dt.bfloat16
I32 = mybir.dt.int32
ACT = mybir.ActivationFunctionType
ALU = mybir.AluOpType
AX_X = mybir.AxisListType.X

DEPTH = 2
SEQ = 256
TT = SEQ // P
D = 1024
KT = D // P
D_FF = 2816
COLS = 256
FF_STEPS = D_FF // COLS
SLOTS = 3
BLOCK = KT * COLS
BANK = 512
RMS_EPS = 1e-6
LN_EPS = 1e-5
WARM = 20
START_WARM = 38
HEAD_WARM = 3


class Events:

    def __init__(self, known):
        self.known, self.table = known, {}

    def new_layer(self, layer):
        self.layer = layer
        self.count = dict.fromkeys(("pe", "act", "dve", "pool"), 0)

    def one(self, engine, name):
        self.count[engine] += 1
        assert (self.layer, name) not in self.table, name
        self.table[self.layer, name] = (engine, self.count[engine])
        return 1

    def at(self, name):
        return self.known[self.layer, name][1] if self.known else 1

    def last(self, engine):
        return self.count[engine]

    def when(self, c, name):
        engine, value = self.known[self.layer, name] if self.known else ("act", 1)
        return {"pe": c.pe_done, "act": c.act_done, "dve": c.dve_done, "pool": c.pool_done}[engine], value


class Core:
    pass


def allocate(nc, ctx, dram, known):
    c = Core()
    c.nc, c.dram = nc, dram

    def sb(name, shape, dt=F32):
        return ctx.enter_context(nc.sbuf_tensor(name, shape, dt))

    def sem(name):
        return ctx.enter_context(nc.semaphore(name))

    c.stage = [sb(f"stage{s}", [P, BLOCK]) for s in range(SLOTS)]
    c.w_hi = [sb(f"w_hi{s}", [P, BLOCK], F32R) for s in range(SLOTS)]
    c.w_lo = [sb(f"w_lo{s}", [P, BLOCK], F32R) for s in range(SLOTS)]
    c.x = sb("x", [P, TT, D])
    c.xn = sb("xn", [P, TT, D])
    c.aT_hi = sb("aT_hi", [P, KT, SEQ], F32R)
    c.aT_lo = sb("aT_lo", [P, KT, SEQ], F32R)
    c.gain_pre = sb("gain_pre", [P, D])
    c.gain_post = sb("gain_post", [P, D])
    c.squares = sb("squares", [P, D], BF16)
    c.ident = sb("ident", [P, P])
    c.zeros = sb("zeros", [P, BANK], BF16)
    c.half_power = sb("half_power", [P, 16])
    c.ss = sb("ss", [P, 16])
    c.rstd = sb("rstd", [P, 16])

    c.psum = ctx.enter_context(nc.psum_tensor("psum", [P, 8, BANK], F32))
    c.weight_loaded = [sem(f"weight_loaded{s}") for s in range(SLOTS)]
    c.w_hi_ready = [sem(f"w_hi_ready{s}") for s in range(SLOTS)]
    c.w_lo_ready = [sem(f"w_lo_ready{s}") for s in range(SLOTS)]
    c.w_used = [sem(f"w_used{s}") for s in range(SLOTS)]
    c.silu_done = sem("silu_done")
    c.hidden_ready = sem("hidden_ready")
    c.hidden_hi_ready = sem("hidden_hi_ready")
    c.hidden_lo_ready = sem("hidden_lo_ready")
    c.up_kv_loaded, c.mem_loaded = sem("up_kv_loaded"), sem("mem_loaded")
    c.pe_done, c.act_done, c.dve_done, c.pool_done = (sem(f"{e}_done") for e in ("pe", "act", "dve", "pool"))
    c.params = {}
    for name in ("gain_pre", "gain_post", "small"):
        c.params[name] = sem(f"{name}_loaded")
    c.loads = c.loads_before = dict.fromkeys(c.params, 0)
    c.ev = Events(known)
    c.per_layer_sems = [*c.weight_loaded, *c.w_hi_ready, *c.w_lo_ready, *c.w_used, c.silu_done, c.hidden_ready,
                        c.hidden_hi_ready, c.hidden_lo_ready, c.up_kv_loaded, c.mem_loaded,
                        c.pe_done, c.act_done, c.dve_done, c.pool_done]
    c.setup_done = sem("setup_done")
    c.x_loaded = sem("x_loaded")
    c.stored = sem("stored")
    return c


def start_layers(c, **loads):
    c.loads_before = {name: c.loads_before[name] + DEPTH * c.loads[name] for name in c.params}
    c.loads = loads


def wait_params(c, eng, name, count):
    eng.wait_ge(c.params[name], c.layer * (16 * c.loads[name]) + 16 * (c.loads_before[name] + count))


def clear_layer(c):
    with c.nc.Block() as block:
        @block.sync
        def _(sp):
            for s in c.per_layer_sems:
                sp.sem_clear(s)



def columns(c, name, layer, first, width=COLS):
    return c.dram[name].rearrange("l (kt p) n -> l p kt n", p=P)[layer][:, :, bass.ds(first, width)]


def rows(c, name, layer, pair):
    return c.dram[name].rearrange("l (b kt p) n -> l b p kt n", kt=2, p=P)[layer][bass.ds(pair, 1)].rearrange(
        "o p kt n -> p (o kt) n")


def as_columns(t):
    return t[:].rearrange("p (kt n) -> p kt n", kt=KT)


def as_rows(t):
    return t[:].rearrange("p (kt n) -> p kt n", kt=2)


def load_weights(c, sp, slot, use, first_use, source, tile=None):
    if not first_use:
        sp.wait_ge(c.w_lo_ready[slot], use)
    if tile is None:
        tile = as_columns(c.stage[slot]) if source.shape[1] == KT else as_rows(c.stage[slot])
    sp.dma_start(tile, source).then_inc(c.weight_loaded[slot], 16)


def split_hi(c, act, slot, use, first_use, size=BLOCK):
    act.wait_ge(c.weight_loaded[slot], 16 * use + 16)
    if not first_use:
        act.wait_ge(c.w_used[slot], use)
    act.activation(c.w_hi[slot][:, 0:size], c.stage[slot][:, 0:size], ACT.Copy).then_inc(c.w_hi_ready[slot], 1)


def split_lo(c, dve, slot, use, size=BLOCK):
    dve.wait_ge(c.w_hi_ready[slot], use + 1)
    dve.tensor_tensor(c.w_lo[slot][:, 0:size], c.stage[slot][:, 0:size], c.w_hi[slot][:, 0:size].bitcast(F32),
                      ALU.subtract).then_inc(c.w_lo_ready[slot], 1)


def hi(c, act, n, size=BLOCK):
    split_hi(c, act, n % SLOTS, n // SLOTS, n < SLOTS, size)


def lo(c, dve, n, size=BLOCK):
    split_lo(c, dve, n % SLOTS, n // SLOTS, size)



def features_by_tokens(pe, out, w_hi, w_lo, a_hi, a_lo, kts=KT, late=None):
    for f in range(2):
        cols = slice(f * P, (f + 1) * P)
        for kt in range(kts):
            if late and f == 0 and kt == kts // 2:
                pe.wait_ge(*late)
            pe.matmul(out[:, f, :], w_hi[:, kt, cols], a_hi[:, kt, :], start=(kt == 0), stop=False)
            pe.matmul(out[:, f, :], w_hi[:, kt, cols], a_lo[:, kt, :], start=False, stop=False)
            last = pe.matmul(out[:, f, :], w_lo[:, kt, cols], a_hi[:, kt, :], start=False, stop=(kt == kts - 1))
    return last


def tokens_by_features(pe, outs, w_hi, w_lo, a_hi, a_lo, kts, start=True, stop=True, late=None):
    for t in range(len(outs)):
        if late and t == 1:
            pe.wait_ge(*late)
        toks = slice(t * P, (t + 1) * P)
        for kt in range(kts):
            pe.matmul(outs[t], a_hi[:, kt, toks], w_hi[:, kt, :], start=start and kt == 0, stop=False,
                      skip_group_check=True)
            pe.matmul(outs[t], a_hi[:, kt, toks], w_lo[:, kt, :], start=False, stop=False, skip_group_check=True)
            last = pe.matmul(outs[t], a_lo[:, kt, toks], w_hi[:, kt, :], start=False,
                             stop=stop and kt == kts - 1, skip_group_check=True)
    return last


def row_block(c, pe, w_hi, w_lo, a_hi, a_lo, start=False, last_of=None):
    for t in range(TT):
        for half in range(2):
            cols = slice(half * BANK, (half + 1) * BANK)
            last = tokens_by_features(pe, [c.psum[:, 4 + 2 * t + half, :]], w_hi[:, :, cols], w_lo[:, :, cols],
                                      a_hi[:, :, t * P:(t + 1) * P], a_lo[:, :, t * P:(t + 1) * P], 2, start,
                                      last_of is not None)
        if last_of is not None and t == 0:
            last.then_inc(c.pe_done, c.ev.one("pe", f"{last_of}.acc0"))
    return last


def wait_weights(c, pe, n):
    pe.wait_ge(c.w_lo_ready[n % SLOTS], n // SLOTS + 1)



def rms_factors(c, pool, tag, cols, width, eps, quarter=1.0):
    ev = c.ev
    n = cols.stop - cols.start
    pool.tensor_scalar(c.rstd[:, cols], c.ss[:, cols], quarter / width, quarter * eps, ALU.mult, ALU.add)\
        .then_inc(c.pool_done, ev.one("pool", f"{tag}.meansq"))
    pool.wait_ge(c.pool_done, ev.at(f"{tag}.meansq"))
    pool.tensor_tensor(c.rstd[:, cols], c.rstd[:, cols], c.half_power[:, 0:n], ALU.pow)\
        .then_inc(c.pool_done, ev.one("pool", f"{tag}.rstd"))


def transpose_split(c, block, tag, source, tiles, after_pe, banks, dst_hi=None, dst_lo=None,
                    by_columns=False):
    ev = c.ev
    dst_hi = c.aT_hi if dst_hi is None else dst_hi
    dst_lo = c.aT_lo if dst_lo is None else dst_lo
    groups = [(t, k, min(4, tiles - k)) for t in range(TT) for k in range(0, tiles, 4)]
    if by_columns:
        groups.sort(key=lambda group: group[1])

    @block.tensor
    def _(pe):
        for i, (t, k, m) in enumerate(groups):
            for name in after_pe[i]:
                pe.wait_ge(*ev.when(c, name))
            if i >= len(banks):
                pe.wait_ge(c.dve_done, ev.at(f"{tag}.lo{i - len(banks)}"))
            for j in range(m):
                last = pe.transpose(c.psum[:, banks[i % len(banks)], j * P:(j + 1) * P],
                                    source[:, t, (k + j) * P:(k + j + 1) * P], c.ident[:])
            last.then_inc(c.pe_done, ev.one("pe", f"{tag}.turned{i}"))

    def places(i):
        t, k, m = groups[i]
        src = c.psum[:, banks[i % len(banks)], 0:m * P].rearrange("p (k t) -> p k t", k=m)
        return src, slice(k, k + m), slice(t * P, (t + 1) * P)

    @block.scalar
    def _(act):
        for i in range(len(groups)):
            src, ks, ts = places(i)
            act.wait_ge(c.pe_done, ev.at(f"{tag}.turned{i}"))
            act.activation(dst_hi[:, ks, ts], src, ACT.Copy).then_inc(c.act_done, ev.one("act", f"{tag}.hi{i}"))

    @block.vector
    def _(dve):
        for i in range(len(groups)):
            src, ks, ts = places(i)
            dve.wait_ge(c.act_done, ev.at(f"{tag}.hi{i}"))
            dve.tensor_tensor(dst_lo[:, ks, ts], src, dst_hi[:, ks, ts].bitcast(F32), ALU.subtract)\
                .then_inc(c.dve_done, ev.one("dve", f"{tag}.lo{i}"))
    return f"{tag}.lo{len(groups) - 1}"


def keep_warm(c, pe, bank, count):
    for _ in range(count):
        pe.matmul(c.psum[:, bank, :], c.zeros[:, 0:P], c.zeros[:], start=True, stop=True)


def pre_norm(c, block, tag, x_ready, gain_count, x=None, gain=None, dst=None, banks=(0, 1, 2, 3),
             split_between=(), warm=0, warm_after=()):
    ev = c.ev
    x = c.x if x is None else x
    which, gain = ("gain_pre", c.gain_pre) if gain is None else gain
    dst = (c.aT_hi, c.aT_lo) if dst is None else dst
    xn = c.xn

    @block.scalar
    def _(act):
        for t in range(TT):
            for name in x_ready[t]:
                act.wait_ge(*ev.when(c, name))
            if ev.last("act"):
                act.wait_ge(c.act_done, ev.last("act"))
            act.activation(c.squares[:], x[:, t, :], ACT.Square, accum_out=c.ss[:, t:t + 1])\
                .then_inc(c.act_done, ev.one("act", f"{tag}.ss{t}"))

    @block.gpsimd
    def _(pool):
        for t in range(TT):
            pool.wait_ge(c.act_done, ev.at(f"{tag}.ss{t}"))
            rms_factors(c, pool, f"{tag}.{t}", slice(t, t + 1), D, RMS_EPS)

    @block.vector
    def _(dve):
        wait_params(c, dve, which, gain_count)
        for t in range(TT):
            for name in x_ready[t]:
                dve.wait_ge(*ev.when(c, name))
            dve.wait_ge(c.pool_done, ev.at(f"{tag}.{t}.rstd"))
            for half in range(2):
                cs = slice(half * BANK, (half + 1) * BANK)
                dve.scalar_tensor_tensor(xn[:, t, cs], x[:, t, cs], c.rstd[:, t:t + 1], gain[:, cs],
                                         ALU.mult, ALU.mult)\
                    .then_inc(c.dve_done, ev.one("dve", f"{tag}.xn{t}.{half}"))

    for n in split_between:
        split_next(c, block, n)

    @block.tensor
    def _(pe):
        for name in warm_after:
            pe.wait_ge(*ev.when(c, name))
        keep_warm(c, pe, banks[-1], warm)

    return transpose_split(c, block, tag, xn, KT, [[f"{tag}.xn{t}.{half}"] for t in range(TT) for half in range(2)],
                           banks, *dst)


def post_norm(c, block, tag, uses, gain_count, half, slot=2):
    ev = c.ev

    def acc(t):
        return c.psum[:, 4 + 2 * t:6 + 2 * t, :].rearrange("p b n -> p (b n)")

    @block.scalar
    def _(act):
        for t in range(TT):
            if t == 0:
                act.wait_ge(c.pe_done, ev.at(f"{tag}.acc0"))
            else:
                act.wait_ge(c.w_used[slot], uses)
            if ev.last("act"):
                act.wait_ge(c.act_done, ev.last("act"))
            act.activation(c.squares[:], acc(t), ACT.Square, accum_out=c.ss[:, t:t + 1])\
                .then_inc(c.act_done, ev.one("act", f"{tag}.post_ss{t}"))

    @block.gpsimd
    def _(pool):
        for t in range(TT):
            pool.wait_ge(c.act_done, ev.at(f"{tag}.post_ss{t}"))
            rms_factors(c, pool, f"{tag}.post{t}", slice(t, t + 1), D, RMS_EPS, 4.0 if half else 1.0)

    @block.vector
    def _(dve):
        wait_params(c, dve, "gain_post", gain_count)
        for t in range(TT):
            dve.wait_ge(c.act_done, ev.at(f"{tag}.post_ss{t}"))
            dve.tensor_tensor(c.xn[:, t, :], acc(t), c.gain_post[:], ALU.mult)\
                .then_inc(c.dve_done, ev.one("dve", f"{tag}.step{t}"))
            dve.wait_ge(c.dve_done, ev.at(f"{tag}.step{t}"))
            dve.wait_ge(c.pool_done, ev.at(f"{tag}.post{t}.rstd"))
            dve.scalar_tensor_tensor(c.x[:, t, :], c.xn[:, t, :], c.rstd[:, t:t + 1], c.x[:, t, :],
                                     ALU.mult, ALU.add).then_inc(c.dve_done, ev.one("dve", f"{tag}.x{t}"))


def add_to_x(c, block, tag, uses, slot=2):
    ev = c.ev

    @block.vector
    def _(dve):
        for t in range(TT):
            if t == 0:
                dve.wait_ge(c.pe_done, ev.at(f"{tag}.acc0"))
            else:
                dve.wait_ge(c.w_used[slot], uses)
            acc = c.psum[:, 4 + 2 * t:6 + 2 * t, :].rearrange("p b n -> p (b n)")
            dve.tensor_tensor(c.x[:, t, :], c.x[:, t, :], acc, ALU.add)\
                .then_inc(c.dve_done, ev.one("dve", f"{tag}.x{t}"))


def split_next(c, block, n):
    @block.scalar
    def _(act):
        hi(c, act, n)

    @block.vector
    def _(dve):
        lo(c, dve, n)


def ffn(c, block, tag, w1, w2, layer, use0, hidden0, last_stage, acc_free):
    nc, ev = c.nc, c.ev
    first = use0 == 0
    with ExitStack() as tiles:
        def sb(name, shape, dt=F32):
            return tiles.enter_context(nc.sbuf_tensor(f"{tag}_{name}", shape, dt))
        silu = sb("silu", [P, 2, SEQ])
        hidden = sb("hidden", [P, 2, SEQ])
        h_hi = [sb(f"h_hi{p}", [P, 2, SEQ], F32R) for p in range(2)]
        h_lo = [sb(f"h_lo{p}", [P, 2, SEQ], F32R) for p in range(2)]

    def bank(p, which):
        return c.psum[:, 2 * p + which, :].rearrange("p (f t) -> p f t", f=2)

    pairs = (FF_STEPS - 3) // 2

    @block.sync
    def _(sp):
        def up(j, first_use=False):
            load_weights(c, sp, 0, use0 + j, first_use, columns(c, w1, layer, COLS * j))
            load_weights(c, sp, 1, use0 + j, first_use, columns(c, w1, layer, COLS * j + D_FF))

        def down(j, first_use=False):
            load_weights(c, sp, 2, use0 + j, first_use, rows(c, w2, layer, j))
        up(0, first)
        down(0, first)
        up(1)
        with sp.Fori(0, FF_STEPS - 2) as i:
            up(i + 2)
            down(i + 1)
        down(FF_STEPS - 1)

    @block.scalar
    def _(act):
        def step(j, p, split_down, split_up, j_is_first=False):
            if split_up:
                split_hi(c, act, 0, use0 + j + 1, False)
            act.wait_ge(c.w_used[0], use0 + j + 1)
            if not j_is_first:
                act.wait_ge(c.hidden_ready, hidden0 + j)
            act.activation(silu[:], bank(p, 0), ACT.Silu).then_inc(c.silu_done, 1)
            if split_up:
                split_hi(c, act, 1, use0 + j + 1, False)
            act.wait_ge(c.hidden_ready, hidden0 + j + 1)
            act.activation(h_hi[p][:], hidden[:], ACT.Copy).then_inc(c.hidden_hi_ready, 1)
            if split_down:
                split_hi(c, act, 2, use0 + j, False)
        if first:
            for n in range(SLOTS):
                split_hi(c, act, n, 0, True)
        step(0, 0, False, True, True)
        with act.Fori(0, pairs) as i:
            step(2 * i + 1, 1, True, True)
            step(2 * i + 2, 0, True, True)
        step(FF_STEPS - 2, 1, True, True)
        j = FF_STEPS - 1
        act.wait_ge(c.w_used[0], use0 + j + 1)
        act.wait_ge(c.hidden_ready, hidden0 + j)
        act.activation(silu[:], bank(0, 0), ACT.Silu).then_inc(c.silu_done, 1)
        split_hi(c, act, 2, use0 + j, False)
        act.wait_ge(c.hidden_ready, hidden0 + j + 1)
        act.activation(h_hi[0][:], hidden[:], ACT.Copy).then_inc(c.hidden_hi_ready, 1)
        if not last_stage:
            split_hi(c, act, 0, use0 + j + 1, False)
            split_hi(c, act, 1, use0 + j + 1, False)

    @block.vector
    def _(dve):
        def step(j, p, split_down, split_up, j_is_first=False):
            if split_up:
                split_lo(c, dve, 0, use0 + j + 1)
            dve.wait_ge(c.silu_done, hidden0 + j + 1)
            if not j_is_first:
                dve.wait_ge(c.hidden_lo_ready, hidden0 + j)
            dve.wait_ge(c.w_used[1], use0 + j + 1)
            dve.tensor_tensor(hidden[:], silu[:], bank(p, 1), ALU.mult).then_inc(c.hidden_ready, 1)
            if split_up:
                split_lo(c, dve, 1, use0 + j + 1)
            dve.wait_ge(c.hidden_hi_ready, hidden0 + j + 1)
            dve.tensor_tensor(h_lo[p][:], hidden[:], h_hi[p][:].bitcast(F32), ALU.subtract)\
               .then_inc(c.hidden_lo_ready, 1)
            if split_down:
                split_lo(c, dve, 2, use0 + j)
        if first:
            for n in range(SLOTS):
                split_lo(c, dve, n, 0)
        step(0, 0, False, True, True)
        with dve.Fori(0, pairs) as i:
            step(2 * i + 1, 1, True, True)
            step(2 * i + 2, 0, True, True)
        step(FF_STEPS - 2, 1, True, True)
        j = FF_STEPS - 1
        split_lo(c, dve, 2, use0 + j)
        dve.wait_ge(c.silu_done, hidden0 + j + 1)
        dve.wait_ge(c.hidden_lo_ready, hidden0 + j)
        dve.wait_ge(c.w_used[1], use0 + j + 1)
        dve.tensor_tensor(hidden[:], silu[:], bank(0, 1), ALU.mult).then_inc(c.hidden_ready, 1)
        dve.wait_ge(c.hidden_hi_ready, hidden0 + j + 1)
        dve.tensor_tensor(h_lo[0][:], hidden[:], h_hi[0][:].bitcast(F32), ALU.subtract)\
            .then_inc(c.hidden_lo_ready, 1)
        if not last_stage:
            split_lo(c, dve, 0, use0 + j + 1)
            split_lo(c, dve, 1, use0 + j + 1)

    @block.tensor
    def _(pe):
        def up(j, p, reused=True, late=None):
            if reused:
                pe.wait_ge(c.hidden_lo_ready, hidden0 + j - 1)
            for slot in range(2):
                project(j, p, slot, late if slot == 0 else None)

        def project(j, p, slot, late=None):
            pe.wait_ge(c.w_lo_ready[slot], use0 + j + 1)
            features_by_tokens(pe, bank(p, slot), as_columns(c.w_hi[slot]), as_columns(c.w_lo[slot]),
                               c.aT_hi, c.aT_lo, late=late).then_inc(c.w_used[slot], 1)

        def down(j, p, last_of=None):
            pe.wait_ge(c.hidden_lo_ready, hidden0 + j + 1)
            pe.wait_ge(c.w_lo_ready[2], use0 + j + 1)
            row_block(c, pe, as_rows(c.w_hi[2]), as_rows(c.w_lo[2]), h_hi[p], h_lo[p], False, last_of)\
                .then_inc(c.w_used[2], 1)

        for name in acc_free:
            pe.wait_ge(*ev.when(c, name))
        for b in range(4):
            pe.matmul(c.psum[:, 4 + b, :], c.zeros[:, 0:P], c.zeros[:], start=True, stop=False,
                      skip_group_check=True)
        pe.wait_ge(c.dve_done, ev.at(f"{tag}.lo2"))
        up(0, 0, False, (c.dve_done, ev.at(f"{tag}.lo3")))
        up(1, 1, False)
        down(0, 0)
        with pe.Fori(0, (FF_STEPS - 3) // 2) as i:
            up(2 * i + 2, 0)
            down(2 * i + 1, 1)
            up(2 * i + 3, 1)
            down(2 * i + 2, 0)
        j = FF_STEPS - 1
        pe.wait_ge(c.hidden_lo_ready, hidden0 + j - 1)
        project(j, 0, 0)
        down(j - 1, 1)
        project(j, 0, 1)
        down(j, 0, tag)



HEADS = 16
KV_HEADS = 2
HEAD_DIM = 64
GROUPS = 8
MASKED = -1e30
MIX1_BLOCKS = 21 + 12


def load_gain(c, pool, which, source, after):
    for name in after:
        pool.wait_ge(*c.ev.when(c, name))
    tile = c.gain_pre if which == "gain_pre" else c.gain_post
    pool.dma_start(tile[:], source.partition_broadcast(P)).then_inc(c.params[which], 16)


def first_block_layer(c, layer, masks):
    nc, ev = c.nc, c.ev
    ev.new_layer("first")
    c.layer = layer
    with nc.Block() as block:
        @block.gpsimd
        def _(pool):
            load_gain(c, pool, "gain_pre", c.dram["ffn1_pre_g"][layer], [])
            load_gain(c, pool, "gain_post", c.dram["ffn1_post_g"][layer], [])
        pre_norm(c, block, "f1", [[], []], 1, warm=START_WARM)

        @block.gpsimd
        def _(pool):
            load_gain(c, pool, "gain_pre", c.dram["mix_pre_g"][layer], ["f1.xn1.1"])
        ffn(c, block, "f1", "ffn1_w1", "ffn1_w2", layer, 0, 0, False, [])
        post_norm(c, block, "f1", FF_STEPS, 1, True)
        pre_norm(c, block, "mix", [["f1.x0"], ["f1.x1"]], 2, warm=WARM)

        @block.gpsimd
        def _(pool):
            load_gain(c, pool, "gain_post", c.dram["mix_post_g"][layer], ["f1.step1"])
        split_next(c, block, SLOTS * FF_STEPS + 2)

        @block.gpsimd
        def _(pool):
            load_gain(c, pool, "gain_pre", c.dram["ffn2_pre_g"][layer], ["mix.xn1.1"])
        mixer_one(c, block, layer, SLOTS * FF_STEPS, masks)
        post_norm(c, block, "mix", FF_STEPS + MIX1_BLOCKS // SLOTS, 2, False)
        pre_norm(c, block, "f2", [["mix.x0"], ["mix.x1"]], 3, warm=WARM)

        @block.gpsimd
        def _(pool):
            load_gain(c, pool, "gain_post", c.dram["ffn2_post_g"][layer], ["mix.step1"])
        split_next(c, block, SLOTS * FF_STEPS + MIX1_BLOCKS + 2)
        ffn(c, block, "f2", "ffn2_w1", "ffn2_w2", layer, FF_STEPS + MIX1_BLOCKS // SLOTS, FF_STEPS, True,
            ["mix.step1"])
        post_norm(c, block, "f2", 2 * FF_STEPS + MIX1_BLOCKS // SLOTS, 3, True)


def mixer_one(c, block, layer, n0, masks):
    nc, ev, dram = c.nc, c.ev, c.dram
    window_mask, causal_T = masks
    with ExitStack() as tiles:
        def sb(name, shape, dt=F32):
            return tiles.enter_context(nc.sbuf_tensor(f"m_{name}", shape, dt))
        qT = sb("qT", [P, KT, SEQ])
        k_twice = [sb(f"k{g}", [P, SEQ]) for g in range(KV_HEADS)]
        vT = sb("vT", [P, SEQ])
        v = sb("v", [P, TT, P])
        uT = sb("uT", [P, GROUPS, SEQ])
        gateA = sb("gateA", [P, KT, SEQ])
        gateB = sb("gateB", [P, KT, SEQ])
        ysT_hi = sb("ysT_hi", [P, GROUPS, SEQ], F32R)
        ysT_lo = sb("ysT_lo", [P, GROUPS, SEQ], F32R)
        scores = sb("scores", [P, 2, 3 * P])
        probs = sb("probs", [P, 2, 3 * P])
        probsT = sb("probsT", [P, 2, 3 * P])
        neg_max = sb("neg_max", [P, TT, HEADS])
        row_max = sb("row_max", [P, TT, HEADS])
        row_sum = sb("row_sum", [P, TT, HEADS])
        sinks = sb("sinks", [P, HEADS])
        stats = sb("stats", [P, TT, 2, 6])
        mean_var = sb("mean_var", [P, TT, 2])
        sgu_wT = sb("sgu_wT", [P, GROUPS, P])
        sgu_b = sb("sgu_b", [P, GROUPS, P])
    vt = c.xn
    merged = qT
    sgu_w = gateB
    ln_g = gateA[:].rearrange("p k t -> p (k t)")[:, 0:D]
    ln_b = gateA[:].rearrange("p k t -> p (k t)")[:, D:2 * D]
    sgu_w = gateB[:].rearrange("p k t -> p (k t)")[:, 0:GROUPS * P].rearrange("p (g s) -> p g s", g=GROUPS)
    Q0, KV, V0, U0, GA0, GB0, SB0, AB0, WO0 = 0, 4, 5, 9, 13, 17, 21, 25, 29
    first_col = {}
    for i in range(4):
        first_col[Q0 + i] = COLS * i
        first_col[V0 + i] = 2304 + COLS * i
        first_col[U0 + i] = 1280 + COLS * i
        first_col[GA0 + i] = 3328 + COLS * i
        first_col[GB0 + i] = 4352 + COLS * i
    first_col[KV] = 1024

    def bank(b):
        return c.psum[:, b, :]

    def two(b):
        return c.psum[:, b, :].rearrange("p (f t) -> p f t", f=2)

    @block.gpsimd
    def _(pool):
        pool.wait_ge(c.dve_done, ev.at("f1.x1"))
        small = c.params["small"]
        pool.dma_start(sinks[:], dram["attn_sinks"][layer].partition_broadcast(P)).then_inc(small, 16)
        pool.dma_start(ln_g, dram["sgu_ln_g"][layer].partition_broadcast(P)).then_inc(small, 16)
        pool.dma_start(ln_b, dram["sgu_ln_b"][layer].partition_broadcast(P)).then_inc(small, 16)
        pool.dma_start(sgu_b[:], dram["sgu_b"][layer].partition_broadcast(P)).then_inc(small, 16)
        pool.dma_start(sgu_w, dram["sgu_w"].rearrange("l g t s -> l t g s")[layer]).then_inc(small, 16)

    @block.sync
    def _(sp):
        for i in range(21):
            load_weights(c, sp, (n0 + i) % SLOTS, (n0 + i) // SLOTS, False, columns(c, "w_in", layer, first_col[i]))
        for base, name in ((SB0, "w_sgu_branch"), (AB0, "w_attn_branch")):
            for i in range(4):
                n = n0 + base + i
                load_weights(c, sp, n % SLOTS, n // SLOTS, False, columns(c, name, layer, COLS * i))
        for i in range(4):
            n = n0 + WO0 + i
            load_weights(c, sp, n % SLOTS, n // SLOTS, False, rows(c, "w_out", layer, i))

    def scores_bank(h):
        return c.psum[:, 2 + h % 2, 0:3 * P]

    def probsT_bank(h):
        return c.psum[:, 4 + h % 2, 0:3 * P]

    def out_bank(q):
        return c.psum[:, 6 + q % 2, :].rearrange("p (t h e) -> p t h e", t=TT, h=4)

    @block.tensor
    def _(pe):
        pe.wait_ge(c.dve_done, ev.at("mix.lo2"))

        def project(i):
            n = n0 + i
            if i >= 2:
                pe.wait_ge(c.act_done, ev.at(f"blk{i - 2}.out"))
            wait_weights(c, pe, n)
            w_hi, w_lo = as_columns(c.w_hi[n % SLOTS]), as_columns(c.w_lo[n % SLOTS])
            a_hi, a_lo = c.aT_hi, c.aT_lo
            if V0 <= i < U0:
                last = tokens_by_features(pe, [two(i % 2)[:, t, :] for t in range(TT)], w_hi, w_lo, a_hi, a_lo, KT)
            else:
                last = features_by_tokens(pe, two(i % 2), w_hi, w_lo, a_hi, a_lo,
                                          late=None if i else (c.dve_done, ev.at("mix.lo3")))
            last.then_inc(c.w_used[n % SLOTS], 1)

        def attend(step):
            for h in range(2 * step, 2 * step + 2):
                if 0 <= h < HEADS:
                    hp = slice((h % 2) * HEAD_DIM, (h % 2 + 1) * HEAD_DIM)
                    if h >= 2:
                        pe.wait_ge(c.dve_done, ev.at(f"masked{h - 2}"))
                    else:
                        pe.wait_ge(c.dve_done, ev.at(f"blk{KV}.k"))
                        pe.wait_ge(c.act_done, ev.at(f"blk{KV}.v"))
                        pe.wait_ge(c.dve_done, ev.at("v.out"))
                    s = scores_bank(h)
                    k = k_twice[h * KV_HEADS // HEADS]
                    pe.matmul(s[:, 0:P], qT[hp, h // 2, 0:P], k[hp, 0:P], start=True, stop=True)
                    pe.matmul(s[:, P:3 * P], qT[hp, h // 2, P:2 * P], k[hp, :], start=True, stop=True)\
                        .then_inc(c.pe_done, ev.one("pe", f"scores{h}"))
            for h in range(2 * step - 2, 2 * step):
                if 0 <= h < HEADS:
                    pe.wait_ge(c.act_done, ev.at(f"probs{h}"))
                    pe.wait_ge(*ev.when(c, f"probsT{h - 2}" if h >= 2 else "sgu.u3"))
                    for j in range(3):
                        last = pe.transpose(probsT_bank(h)[:, j * P:(j + 1) * P], probs[:, h % 2, j * P:(j + 1) * P],
                                            c.ident[:])
                    last.then_inc(c.pe_done, ev.one("pe", f"turned{h}"))
            for h in range(2 * step - 4, 2 * step - 2):
                if 0 <= h < HEADS:
                    pe.wait_ge(c.act_done, ev.at(f"probsT{h}"))
                    q, kv = h // 4, h * KV_HEADS // HEADS
                    if h % 4 == 0:
                        pe.wait_ge(c.dve_done, ev.at(f"y{q - 2}" if q >= 2 else "sgu.u3"))
                    e = slice(kv * HEAD_DIM, (kv + 1) * HEAD_DIM)
                    y = out_bank(q)
                    pT = probsT[:, h % 2, :]
                    pe.matmul(y[:, 0, h % 4, :], pT[:, 0:P], v[:, 0, e], start=True, stop=True)
                    pe.matmul(y[:, 1, h % 4, :], pT[:, P:2 * P], v[:, 0, e], start=True, stop=False)
                    pe.matmul(y[:, 1, h % 4, :], pT[:, 2 * P:3 * P], v[:, 1, e], start=False, stop=True)\
                        .then_inc(c.pe_done, ev.one("pe", f"weighted{h}"))

        for i in range(21):
            project(i)
            if i == KV:
                wait_params(c, pe, "small", 5)
                pe.wait_ge(c.dve_done, ev.at("f1.step1"))
                for g in range(GROUPS):
                    last = pe.transpose(c.psum[:, 4 + g // 4, (g % 4) * P:(g % 4 + 1) * P], sgu_w[:, g, :], c.ident[:])
                last.then_inc(c.pe_done, ev.one("pe", "sgu_w.turned"))
            if i == KV + 1:
                pe.wait_ge(c.act_done, ev.at(f"blk{KV}.v"))
                for t in range(TT):
                    last = pe.transpose(c.psum[:, 2, t * P:(t + 1) * P], vT[:, t * P:(t + 1) * P], c.ident[:])
                last.then_inc(c.pe_done, ev.one("pe", "v.turned"))
            if i >= U0 + 3:
                if i == U0 + 3:
                    pe.wait_ge(c.dve_done, ev.at("sgu.vn1"))
                    pe.wait_ge(c.dve_done, ev.at("sgu_wT"))
                    for t in range(TT):
                        for g in range(GROUPS):
                            last = pe.matmul(c.psum[:, 4 + 2 * t + g // 4, (g % 4) * P:(g % 4 + 1) * P],
                                             vt[:, t, g * P:(g + 1) * P], sgu_wT[:, g, :], start=True, stop=True)
                        last.then_inc(c.pe_done, ev.one("pe", f"sgu.s{t}"))
                attend(i - U0 - 3)
        attend(9)

    @block.scalar
    def _(act):
        def evacuate(i):
            n = n0 + i
            act.wait_ge(c.w_used[n % SLOTS], n // SLOTS + 1)
            src = two(i % 2)
            if i < KV:
                act.activation(qT[:, 2 * i:2 * i + 2, :], src, ACT.Copy)\
                    .then_inc(c.act_done, ev.one("act", f"blk{i}.out"))
            elif i == KV:
                act.wait_ge(c.dve_done, ev.at(f"blk{i}.k"))
                act.activation(vT[:], src[:, 1, :], ACT.Copy).then_inc(c.act_done, ev.one("act", f"blk{i}.v"))
                act.activation(k_twice[1][0:64, :], src[64:128, 0, :], ACT.Copy)\
                    .then_inc(c.act_done, ev.one("act", f"blk{i}.out"))
            elif i < U0:
                j = i - V0
                act.activation(vt[:, :, COLS * j:COLS * (j + 1)], src, ACT.Gelu)\
                    .then_inc(c.act_done, ev.one("act", f"blk{i}.out"))
            elif i < GA0:
                j = i - U0
                act.activation(uT[:, 2 * j:2 * j + 2, :], src, ACT.Gelu)\
                    .then_inc(c.act_done, ev.one("act", f"blk{i}.out"))
            elif i < GB0:
                j = i - GA0
                act.wait_ge(c.dve_done, ev.at("sgu.vn1"))
                act.activation(gateA[:, 2 * j:2 * j + 2, :], src, ACT.Tanh, scale=0.5)\
                    .then_inc(c.act_done, ev.one("act", f"blk{i}.out"))
            else:
                j = i - GB0
                act.activation(gateB[:, 2 * j:2 * j + 2, :], src, ACT.Tanh, scale=0.5)\
                    .then_inc(c.act_done, ev.one("act", f"blk{i}.out"))

        def attend(step):
            for h in range(2 * step, 2 * step + 2):
                if 0 <= h < HEADS:
                    act.wait_ge(c.dve_done, ev.at(f"neg_max{h}"))
                    if h >= 2:
                        act.wait_ge(c.pe_done, ev.at(f"turned{h - 2}"))
                    for t, ks in ((0, slice(0, P)), (1, slice(P, 3 * P))):
                        last = act.activation(probs[:, h % 2, ks], scores[:, h % 2, ks], ACT.Exp,
                                              bias=neg_max[:, t, h:h + 1], accum_out=row_sum[:, t, h:h + 1])
                    last.then_inc(c.act_done, ev.one("act", f"probs{h}"))
            for h in range(2 * step - 2, 2 * step):
                if 0 <= h < HEADS:
                    act.wait_ge(c.pe_done, ev.at(f"turned{h}"))
                    if h >= 2:
                        act.wait_ge(c.pe_done, ev.at(f"weighted{h - 2}"))
                    act.activation(probsT[:, h % 2, :], probsT_bank(h), ACT.Copy)\
                        .then_inc(c.act_done, ev.one("act", f"probsT{h}"))
            if step >= 3 and step % 2 == 1:
                q = (step - 3) // 2
                act.wait_ge(c.dve_done, ev.at(f"sink{q}"))
                hs = slice(4 * q, 4 * q + 4)
                act.activation(neg_max[:, :, hs], neg_max[:, :, hs], ACT.Exp)\
                    .then_inc(c.act_done, ev.one("act", f"sink_exp{q}"))

        for i in range(21):
            evacuate(i)
            hi(c, act, n0 + i + SLOTS)
            if i == GA0:
                for b in range(2):
                    gs = slice(4 * b, 4 * b + 4)
                    act.wait_ge(c.dve_done, ev.at(f"sgu.u{2 + b}"))
                    act.activation(ysT_hi[:, gs, :], uT[:, gs, :], ACT.Copy)\
                        .then_inc(c.act_done, ev.one("act", f"ysT_hi{b}"))
            if i >= U0 + 3:
                attend(i - U0 - 3)
        attend(9)

    @block.vector
    def _(dve):

        def attend(step):
            for h in range(2 * step, 2 * step + 2):
                if 0 <= h < HEADS:
                    dve.wait_ge(c.pe_done, ev.at(f"scores{h}"))
                    if h >= 2:
                        dve.wait_ge(c.act_done, ev.at(f"probs{h - 2}"))
                    s = scores[:, h % 2, :]
                    dve.scalar_tensor_tensor(s, scores_bank(h), HEAD_DIM ** -0.5, window_mask[:],
                                             ALU.mult, ALU.add).then_inc(c.dve_done, ev.one("dve", f"masked{h}"))
                    dve.wait_ge(c.dve_done, ev.at(f"masked{h}"))
                    dve.tensor_reduce(row_max[:, 0, h:h + 1], s[:, 0:P], AX_X, ALU.max)
                    dve.tensor_reduce(row_max[:, 1, h:h + 1], s[:, P:3 * P], AX_X, ALU.max)\
                        .then_inc(c.dve_done, ev.one("dve", f"row_max{h}"))
                    dve.wait_ge(c.dve_done, ev.at(f"row_max{h}"))
                    dve.tensor_scalar(neg_max[:, :, h:h + 1], row_max[:, :, h:h + 1],
                                      sinks[:, h:h + 1], -1.0, ALU.max, ALU.mult)\
                        .then_inc(c.dve_done, ev.one("dve", f"neg_max{h}"))
            if step >= 3 and step % 2 == 1:
                q = (step - 3) // 2
                hs = slice(4 * q, 4 * q + 4)
                dve.wait_ge(c.act_done, ev.at(f"probs{4 * q + 3}"))
                dve.tensor_tensor(neg_max[:, :, hs], neg_max[:, :, hs],
                                  sinks[:, hs].unsqueeze(1).broadcast_to([P, TT, 4]), ALU.add)\
                    .then_inc(c.dve_done, ev.one("dve", f"sink{q}"))
                dve.wait_ge(c.act_done, ev.at(f"sink_exp{q}"))
                dve.tensor_tensor(row_sum[:, :, hs], row_sum[:, :, hs], neg_max[:, :, hs], ALU.add)\
                    .then_inc(c.dve_done, ev.one("dve", f"den{q}"))
                dve.wait_ge(c.dve_done, ev.at(f"den{q}"))
                dve.reciprocal(row_sum[:, :, hs], row_sum[:, :, hs]).then_inc(c.dve_done, ev.one("dve", f"rden{q}"))
                dve.wait_ge(c.dve_done, ev.at(f"rden{q}"))
                dve.wait_ge(c.pe_done, ev.at(f"weighted{4 * q + 3}"))
                dve.wait_ge(c.pe_done, ev.at("sgu.s1"))
                y = vt[:, :, 4 * q * HEAD_DIM:4 * (q + 1) * HEAD_DIM].rearrange("p t (h e) -> p t h e", h=4)
                dve.tensor_tensor(y, out_bank(q), row_sum[:, :, hs].unsqueeze(3).broadcast_to(
                    [P, TT, 4, HEAD_DIM]), ALU.mult).then_inc(c.dve_done, ev.one("dve", f"y{q}"))

        for i in range(21):
            if i == KV:
                n = n0 + i
                dve.wait_ge(c.w_used[n % SLOTS], n // SLOTS + 1)
                src = two(i % 2)
                dve.tensor_copy(k_twice[0][0:64, :], src[0:64, 0, :])
                dve.tensor_copy(k_twice[0][64:128, :], src[0:64, 0, :])
                dve.tensor_copy(k_twice[1][64:128, :], src[64:128, 0, :])\
                    .then_inc(c.dve_done, ev.one("dve", f"blk{i}.k"))
            lo(c, dve, n0 + i + SLOTS)
            if i == KV:
                dve.wait_ge(c.pe_done, ev.at("sgu_w.turned"))
                for b in range(2):
                    gs = slice(4 * b, 4 * b + 4)
                    last = dve.tensor_tensor(sgu_wT[:, gs, :], bank(4 + b).rearrange("p (g t) -> p g t", g=4),
                                             causal_T[:].unsqueeze(1).broadcast_to([P, 4, P]), ALU.mult)
                last.then_inc(c.dve_done, ev.one("dve", "sgu_wT"))
            if i == GA0:
                for b in range(2):
                    gs = slice(4 * b, 4 * b + 4)
                    dve.wait_ge(c.act_done, ev.at(f"ysT_hi{b}"))
                    dve.tensor_tensor(ysT_lo[:, gs, :], uT[:, gs, :], ysT_hi[:, gs, :].bitcast(F32),
                                      ALU.subtract).then_inc(c.dve_done, ev.one("dve", f"ysT_lo{b}"))
            if i == KV + 2:
                dve.wait_ge(c.pe_done, ev.at("v.turned"))
                dve.tensor_copy(v[:].rearrange("p t e -> p (t e)"), c.psum[:, 2, 0:TT * P])\
                    .then_inc(c.dve_done, ev.one("dve", "v.out"))
            if i == U0:
                dve.wait_ge(c.act_done, ev.at(f"blk{U0 - 1}.out"))
                for t in range(TT):
                    for half in range(2):
                        last = dve.bn_stats(stats[:, t, half, :], vt[:, t, half * BANK:(half + 1) * BANK])
                last.then_inc(c.dve_done, ev.one("dve", "sgu.stats"))
                dve.wait_ge(c.dve_done, ev.at("sgu.stats"))
                for t in range(TT):
                    last = dve.bn_aggr(mean_var[:, t, :], stats[:, t, :, :].rearrange("p a s -> p (a s)"))
                last.then_inc(c.dve_done, ev.one("dve", "sgu.mean_var"))
            if i == U0 + 1:
                for t in range(TT):
                    dve.wait_ge(c.pool_done, ev.at("sgu.rstd"))
                    dve.tensor_scalar(vt[:, t, :], vt[:, t, :], mean_var[:, t, 0:1],
                                      c.rstd[:, 4 + t:5 + t], ALU.subtract, ALU.mult)\
                        .then_inc(c.dve_done, ev.one("dve", f"sgu.xc{t}"))
                    dve.wait_ge(c.dve_done, ev.at(f"sgu.xc{t}"))
                    wait_params(c, dve, "small", 5)
                    dve.tensor_tensor(vt[:, t, :], vt[:, t, :], ln_g, ALU.mult)\
                        .then_inc(c.dve_done, ev.one("dve", f"sgu.xg{t}"))
                    dve.wait_ge(c.dve_done, ev.at(f"sgu.xg{t}"))
                    dve.tensor_tensor(vt[:, t, :], vt[:, t, :], ln_b, ALU.add)\
                        .then_inc(c.dve_done, ev.one("dve", f"sgu.vn{t}"))
            if i == U0 + 3:
                dve.wait_ge(c.act_done, ev.at(f"blk{U0 + 3}.out"))
                for t in range(TT):
                    dve.wait_ge(c.pe_done, ev.at(f"sgu.s{t}"))
                    for b in range(2):
                        gs, ts = slice(4 * b, 4 * b + 4), slice(t * P, (t + 1) * P)
                        s = bank(4 + 2 * t + b).rearrange("p (g t) -> p g t", g=4)
                        dve.tensor_tensor(s, s, sgu_b[:, gs, :], ALU.add)\
                            .then_inc(c.dve_done, ev.one("dve", f"sgu.b{2 * t + b}"))
                        dve.wait_ge(c.dve_done, ev.at(f"sgu.b{2 * t + b}"))
                        dve.tensor_tensor(uT[:, gs, ts], uT[:, gs, ts], s, ALU.mult)\
                            .then_inc(c.dve_done, ev.one("dve", f"sgu.u{2 * t + b}"))
            if i >= U0 + 3:
                attend(i - U0 - 3)
        attend(9)

    @block.gpsimd
    def _(pool):
        pool.wait_ge(c.dve_done, ev.at("sgu.mean_var"))
        pool.tensor_scalar(c.rstd[:, 4:4 + TT], mean_var[:, :, 1], LN_EPS, None, ALU.add)\
            .then_inc(c.pool_done, ev.one("pool", "sgu.var"))
        pool.wait_ge(c.pool_done, ev.at("sgu.var"))
        pool.tensor_tensor(c.rstd[:, 4:4 + TT], c.rstd[:, 4:4 + TT], c.half_power[:, 0:TT], ALU.pow)\
            .then_inc(c.pool_done, ev.one("pool", "sgu.rstd"))
        for gate, base, name in ((gateA, GA0, "ga"), (gateB, GB0, "gb")):
            for j in range(4):
                ks = slice(2 * j, 2 * j + 2)
                pool.wait_ge(c.act_done, ev.at(f"blk{base + j}.out"))
                pool.tensor_scalar(gate[:, ks, :], gate[:, ks, :], 0.5, 0.5, ALU.mult, ALU.add)\
                    .then_inc(c.pool_done, ev.one("pool", f"{name}{j}"))

    def branch(blocks, a_hi, a_lo, ready):
        @block.tensor
        def _(pe):
            pe.wait_ge(c.dve_done, ev.at(ready))
            for i in blocks:
                n = n0 + i
                pe.wait_ge(*ev.when(c, f"blk{i - 2}.out"))
                wait_weights(c, pe, n)
                features_by_tokens(pe, two(i % 2), as_columns(c.w_hi[n % SLOTS]), as_columns(c.w_lo[n % SLOTS]),
                                   a_hi, a_lo).then_inc(c.w_used[n % SLOTS], 1)

    def gated_branch(blocks):
        branch(blocks, ysT_hi, ysT_lo, "ysT_lo1")

        @block.scalar
        def _(act):
            for i in blocks:
                hi(c, act, n0 + i + SLOTS)

        @block.vector
        def _(dve):
            for i in blocks:
                n, j = n0 + i, i - SB0
                ks = slice(2 * j, 2 * j + 2)
                dve.wait_ge(c.w_used[n % SLOTS], n // SLOTS + 1)
                dve.wait_ge(c.pool_done, ev.at(f"gb{j}"))
                dve.tensor_tensor(merged[:, ks, :], two(i % 2), gateB[:, ks, :], ALU.mult)\
                    .then_inc(c.dve_done, ev.one("dve", f"blk{i}.out"))
                lo(c, dve, n + SLOTS)

    gated_branch(range(SB0, AB0 - 1))
    transpose_split(c, block, "ya", vt, KT, [["y3"]] * 4, [2, 3, 4, 5])
    gated_branch(range(AB0 - 1, AB0))
    branch(range(AB0, WO0), c.aT_hi, c.aT_lo, "ya.lo3")

    @block.tensor
    def _(pe):
        for i in range(4):
            n = n0 + WO0 + i
            pe.wait_ge(c.dve_done, ev.at(f"merged_lo{i}"))
            wait_weights(c, pe, n)
            row_block(c, pe, as_rows(c.w_hi[n % SLOTS]), as_rows(c.w_lo[n % SLOTS]), ysT_hi[:, 2 * i:2 * i + 2, :],
                      ysT_lo[:, 2 * i:2 * i + 2, :], i == 0, "mix" if i == 3 else None).then_inc(c.w_used[n % SLOTS], 1)

    @block.scalar
    def _(act):
        for i in range(AB0, WO0 + 4):
            if i < WO0 + 3:
                hi(c, act, n0 + i + SLOTS)
            if i < WO0:
                j = i - AB0
                ks = slice(2 * j, 2 * j + 2)
                act.wait_ge(c.dve_done, ev.at(f"merged{j}"))
                act.activation(ysT_hi[:, ks, :], merged[:, ks, :], ACT.Copy)\
                    .then_inc(c.act_done, ev.one("act", f"merged_hi{j}"))

    @block.vector
    def _(dve):
        for i in range(AB0, WO0 + 4):
            n, j = n0 + i, i - AB0
            if i < WO0:
                ks = slice(2 * j, 2 * j + 2)
                dve.wait_ge(c.w_used[n % SLOTS], n // SLOTS + 1)
                dve.wait_ge(c.pool_done, ev.at(f"ga{j}"))
                dve.tensor_tensor(gateA[:, ks, :], two(i % 2), gateA[:, ks, :], ALU.mult)\
                    .then_inc(c.dve_done, ev.one("dve", f"blk{i}.out"))
                dve.wait_ge(c.dve_done, ev.at(f"blk{i}.out"))
                dve.tensor_tensor(merged[:, ks, :], merged[:, ks, :], gateA[:, ks, :], ALU.add)\
                    .then_inc(c.dve_done, ev.one("dve", f"merged{j}"))
            if i < WO0 + 3:
                lo(c, dve, n + SLOTS)
            if i < WO0:
                dve.wait_ge(c.act_done, ev.at(f"merged_hi{j}"))
                dve.tensor_tensor(ysT_lo[:, ks, :], merged[:, ks, :],
                                  ysT_hi[:, ks, :].bitcast(F32), ALU.subtract)\
                    .then_inc(c.dve_done, ev.one("dve", f"merged_lo{j}"))



GROUP = 256
CONF_TAPS = 31
SHORT_TAPS = 3
HG_HEADS = 4
HG_D = 64
MLA_HEADS = 4
NOPE, ROPE = 64, 32
QK = NOPE + ROPE
ROPE_BASE = 10000.0
XA_HEADS = 4
XA_D = 64
LEVELS = [128, 64, 32, 16, 8, 4, 2, 1]
DIAGONAL = len(LEVELS)
HG_CHUNK = 64
TINY = 2.0 ** -60

KV0, HQ, ZF, ZB, KV1, CA, CG, CQ, CKV, HV, UP, HG, SC, SX, SB, WO = range(16)
XQ, XO = WO + 4, WO + 5
FFN_USE = 7
SMALL = 13


class Second:
    pass


def second_tiles(c, ctx):
    s = Second()

    def sb(name, shape, dt=F32):
        return ctx.enter_context(c.nc.sbuf_tensor(f"s_{name}", shape, dt))

    s.cos = sb("cos", [P, TT, ROPE // 2])
    s.sin = sb("sin", [P, TT, ROPE // 2])
    s.lower = sb("lower", [P, DEPTH, HG_HEADS])
    s.block_mask = sb("block_mask", [P, len(LEVELS) - 1, P], I32)
    s.again = sb("again", [P, HG_HEADS * SEQ], BF16)
    return s


def second_setup(c, s):
    nc, dram = c.nc, c.dram
    half = ROPE // 2
    with ExitStack() as tiles:
        def sb(name, shape, dt=F32):
            return tiles.enter_context(nc.sbuf_tensor(f"t_{name}", shape, dt))
        pos_i, pos = sb("pos_i", [P, TT], I32), sb("pos", [P, TT])
        inv = sb("inv", [P, half])
        ang, turns = sb("ang", [P, TT, half]), sb("turns", [P, TT, half])
        shifted, over = sb("shifted", [P, TT, half]), sb("over", [P, TT, half])
        gamma = sb("gamma", [P, DEPTH, HG_HEADS])
        top, total = sb("top", [P, HG_HEADS]), sb("total", [P, HG_HEADS])
        t_index, s_xor_t, shift = sb("t_index", [P, P], I32), sb("s_xor_t", [P, P], I32), sb("shift", [P, P], I32)
        p_index = sb("p_index", [P, P], I32)
        loaded = tiles.enter_context(nc.semaphore("setup_loaded"))
        made = tiles.enter_context(nc.semaphore("setup_made"))
        d = tiles.enter_context(nc.semaphore("setup_dve"))
        a = tiles.enter_context(nc.semaphore("setup_act"))
        with nc.Block() as block:
            @block.sync
            def _(sp):
                with nc.allow_non_contiguous_dma(reason="1 KB of positions and 4 KB of gammas"):
                    sp.dma_start(pos_i[:], dram["positions_2"].rearrange("o (t p) -> p (o t)", p=P))\
                        .then_inc(loaded, 16)
                    for direction in range(2):
                        ps = slice(direction * HG_D, (direction + 1) * HG_D)
                        sp.dma_start(gamma[ps], dram["h_gamma_2"][direction].rearrange("l (h d) -> d l h", d=HG_D))\
                            .then_inc(loaded, 16)
                sp.wait_ge(loaded, 48)

            @block.gpsimd
            def _(pool):
                pool.iota(t_index[:], pattern=[[1, P]], base=0, channel_multiplier=0)
                pool.iota(p_index[:], pattern=[[0, P]], base=0, channel_multiplier=1)
                for j in range(half):
                    last = pool.memset(inv[:, j:j + 1], float(np.float32(ROPE_BASE) ** np.float32(-2 * j / ROPE)))
                last.then_inc(made, 1)

            @block.vector
            def _(dve):
                count = [0]

                def link(instruction):
                    count[0] += 1
                    instruction.then_inc(d, 1)
                    dve.wait_ge(d, count[0])

                dve.wait_ge(made, 1)
                dve.wait_ge(loaded, 48)
                link(dve.tensor_tensor(s_xor_t[:], p_index[:], t_index[:], ALU.bitwise_xor))
                for i, h in enumerate(LEVELS[1:]):
                    link(dve.tensor_scalar(shift[:], s_xor_t[:], h.bit_length() - 1, None, ALU.logical_shift_right))
                    link(dve.tensor_scalar(s.block_mask[:, i, :], shift[:], 1, None, ALU.is_equal))
                link(dve.tensor_copy(pos[:], pos_i[:]))
                link(dve.tensor_tensor(ang[:], pos[:].unsqueeze(2).broadcast_to([P, TT, half]),
                                       inv[:].unsqueeze(1).broadcast_to([P, TT, half]), ALU.mult))
                link(dve.tensor_scalar(turns[:], ang[:], float(1 / (2 * np.pi)), None, ALU.mult))
                link(dve.tensor_scalar(turns[:], turns[:], 1.5 * 2.0 ** 23, None, ALU.add))
                link(dve.tensor_scalar(turns[:], turns[:], 1.5 * 2.0 ** 23, None, ALU.subtract))
                rest, full = 2 * np.pi, 2 * np.pi
                parts = []
                for bits in (6, 17):
                    part = np.floor(rest * 2.0 ** bits) / 2.0 ** bits
                    parts.append(part)
                    rest -= part
                parts.append(rest)
                for part in parts:
                    link(dve.scalar_tensor_tensor(ang[:], turns[:], -float(part), ang[:], ALU.mult, ALU.add))
                pi = float(np.nextafter(np.float32(np.pi), np.float32(0)))
                link(dve.tensor_scalar(shifted[:], ang[:], float(np.pi / 2), None, ALU.add))
                link(dve.tensor_scalar(over[:], shifted[:], pi, -float(full), ALU.is_gt, ALU.mult))
                link(dve.tensor_tensor(shifted[:], shifted[:], over[:], ALU.add))
                link(dve.tensor_scalar(shifted[:], shifted[:], pi, -pi, ALU.min, ALU.max))
                link(dve.tensor_scalar(ang[:], ang[:], pi, -pi, ALU.min, ALU.max))
                link(dve.tensor_copy(top[:], gamma[:, 0, :]))
                for l in range(1, DEPTH):
                    link(dve.tensor_tensor(top[:], top[:], gamma[:, l, :], ALU.max))
                link(dve.tensor_tensor(gamma[:], gamma[:], top[:].unsqueeze(1).broadcast_to([P, DEPTH, HG_HEADS]),
                                       ALU.subtract))
                dve.wait_ge(a, 3)
                link(dve.tensor_copy(total[:], gamma[:, 0, :]))
                for l in range(1, DEPTH):
                    link(dve.tensor_tensor(total[:], total[:], gamma[:, l, :], ALU.add))
                link(dve.reciprocal(total[:], total[:]))
                link(dve.tensor_tensor(gamma[:], gamma[:], total[:].unsqueeze(1).broadcast_to([P, DEPTH, HG_HEADS]),
                                       ALU.mult))
                link(dve.tensor_copy(top[:], gamma[:, 0, :]))
                for l in range(DEPTH):
                    if l:
                        link(dve.tensor_tensor(top[:], top[:], gamma[:, l, :], ALU.add))
                    link(dve.tensor_tensor(s.lower[:, l, :], top[:], gamma[:, 0, :], ALU.subtract))

            before = 1 + 2 * len(LEVELS[1:]) + 5 + 3 + 5

            @block.scalar
            def _(act):
                act.wait_ge(d, before)
                act.activation(s.sin[:], ang[:], ACT.Sin).then_inc(a, 1)
                act.activation(s.cos[:], shifted[:], ACT.Sin).then_inc(a, 1)
                act.wait_ge(d, before + DEPTH + 1)
                act.activation(gamma[:], gamma[:], ACT.Exp).then_inc(a, 1)


def second_block_layer(c, s, layer):
    nc, ev, dram = c.nc, c.ev, c.dram
    ev.new_layer("second")
    c.layer = layer
    with ExitStack() as tiles:
        def sb(name, shape, dt=F32):
            return tiles.enter_context(nc.sbuf_tensor(f"u_{name}", shape, dt))

        low_hi, low_lo = sb("low_hi", [P, 3, SEQ], F32R), sb("low_lo", [P, 3, SEQ], F32R)
        kv_mem = sb("kv_mem", [P, TT, 2 * XA_HEADS * XA_D])
        q2, lf, kk = (sb(n, [P, HG_HEADS, SEQ]) for n in ("q2", "lf", "kk"))
        GH = sb("GH", [P, 2, HG_HEADS, SEQ])
        hv, hg = sb("hv", [P, TT, GROUP]), sb("hg", [P, TT, GROUP])
        qk = sb("qk", [P, 2, TT * MLA_HEADS, QK])
        kv_up = sb("kv_up", [P, TT, 2 * GROUP])
        conf, conf_out = sb("conf", [P, 2, SEQ + CONF_TAPS - 1]), sb("conf_out", [P, 2, SEQ])
        short, short_out = sb("short", [P, 2, SEQ + SHORT_TAPS - 1]), sb("short_out", [P, 2, SEQ])
        row_max, row_sum = sb("row_max", [P, 2 * TT, 4]), sb("row_sum", [P, 2 * TT, 4])
        taps_rows, taps = sb("taps_rows", [36, GROUP]), sb("taps", [P, 2, 36])
        bc = {name: sb(name, [P, n]) for name, n in (("qa_g", GROUP), ("kva_g", P), ("qn_g", QK), ("kn_g", QK),
                                                     ("ln_g", GROUP), ("ln_b", GROUP), ("onorm_g", GROUP),
                                                     ("xqn_g", XA_D), ("xkn_g", XA_D))}
        sq_sum, factor = sb("sq_sum", [P, 16]), sb("factor", [P, 16])
        lower = sb("lower_now", [P, HG_HEADS])
        stats, mean_var = sb("stats", [P, TT, 6]), sb("mean_var", [P, TT, 2])
        with ExitStack() as early:
            def sb_early(name, shape, dt=F32):
                return early.enter_context(nc.sbuf_tensor(f"u_{name}", shape, dt))
            bT_hi, bT_lo = sb_early("bT_hi", [P, KT, SEQ], F32R), sb_early("bT_lo", [P, KT, SEQ], F32R)
        near, far = (sb(n, [P, HG_HEADS * TT, P]) for n in ("near", "far"))
        Q = [sb(f"Q{i}", [P, HG_HEADS, SEQ]) for i in range(2)]
        K = [sb(f"K{i}", [P, HG_HEADS, SEQ]) for i in range(2)]

    G, H = GH[:, 0], GH[:, 1]
    mem = GH.rearrange("p t h n -> p t (h n)")
    probs, probsT = lf[:, 0:2, :], lf[:, 2:4, :]
    cat = c.xn
    cqkv = c.xn[:, 0, :].rearrange("p (t n) -> p t n", t=TT)
    scratch = c.xn[:, 1, :]
    f, clamp = (t[:] for t in K)
    mla_T = (Q[0], K[0])
    mem_T = (G, H)
    squares = Q[1][:].rearrange("p h t -> p (h t)")
    CKV_AT = COLS - P - ROPE
    UP_Q = 2 * MLA_HEADS * QK
    first_col = {KV0: 0, KV1: 256, HQ: 512, ZF: 768, ZB: 1024, HV: 1280, HG: 1536, CA: 0, CG: 256, SB: 1792,
                 SC: 2048, SX: 2304, CQ: 2560, CKV: 2976 - COLS}
    by_tokens = (KV0, KV1, CQ, CKV, HV, HG)

    def two(b):
        return c.psum[:, b, :].rearrange("p (f t) -> p f t", f=2)

    def load(sp, n, source):
        load_weights(c, sp, n % SLOTS, n // SLOTS, n < SLOTS, source)

    def used(eng, n):
        eng.wait_ge(c.w_used[n % SLOTS], n // SLOTS + 1)


    def rms_sum(dve, tag, view, sq, n, dims):
        dve.tensor_tensor(sq, view, view, ALU.mult).then_inc(c.dve_done, ev.one("dve", f"{tag}.sq"))
        dve.wait_ge(c.dve_done, ev.at(f"{tag}.sq"))
        dve.tensor_reduce(sq_sum[:, 0:n].rearrange(dims[0], **dims[1]), sq, AX_X, ALU.add)\
            .then_inc(c.dve_done, ev.one("dve", f"{tag}.sum"))

    def rms_power(pool, tag, n, width):
        pool.wait_ge(c.dve_done, ev.at(f"{tag}.sum"))
        pool.tensor_scalar(factor[:, 0:n], sq_sum[:, 0:n], 1.0 / width, RMS_EPS, ALU.mult,
                           ALU.add).then_inc(c.pool_done, ev.one("pool", f"{tag}.meansq"))
        pool.wait_ge(c.pool_done, ev.at(f"{tag}.meansq"))
        pool.tensor_tensor(factor[:, 0:n], factor[:, 0:n], c.half_power[:, 0:n], ALU.pow)\
            .then_inc(c.pool_done, ev.one("pool", f"{tag}.factor"))


    def halves(tile, direction, h):
        part = tile[direction * HG_D:(direction + 1) * HG_D].rearrange("p h t -> p (h t)")
        return part.rearrange("p (b two t) -> p b two t", two=2, t=h)[:, :, 1 - direction, :]

    def other_halves(tile, direction, h):
        part = tile[direction * HG_D:(direction + 1) * HG_D].rearrange("p h t -> p (h t)")
        return part.rearrange("p (b two t) -> p b two t", two=2, t=h)[:, :, direction, :]

    def head_side(tile, direction, side):
        return tile[direction * HG_D:(direction + 1) * HG_D, side:side + 3:2, :]

    def gates_dve(dve):
        dve.wait_ge(c.act_done, ev.at(f"blk{ZB}.out"))
        dve.wait_ge(c.dve_done, ev.at("lower"))
        lower_b = lower[:].unsqueeze(2).broadcast_to([P, HG_HEADS, SEQ])
        dve.tensor_tensor(clamp, kk[:], lower_b, ALU.mult).then_inc(c.dve_done, ev.one("dve", "hg.lower"))
        dve.wait_ge(c.dve_done, ev.at("hg.lower"))
        dve.tensor_tensor(f, f, clamp, ALU.add).then_inc(c.dve_done, ev.one("dve", "hg.f"))
        dve.wait_ge(c.dve_done, ev.at("hg.f"))
        dve.tensor_tensor(kk[:], kk[:], clamp, ALU.subtract).then_inc(c.dve_done, ev.one("dve", "hg.k"))
        dve.wait_ge(c.dve_done, ev.at("hg.k"))
        dve.tensor_scalar(lf[:], f, TINY, None, ALU.max).then_inc(c.dve_done, ev.one("dve", "hg.big"))
        dve.tensor_scalar(clamp, f, 1 / TINY, 1.0, ALU.mult, ALU.min).then_inc(c.dve_done, ev.one("dve", "hg.small"))
        dve.wait_ge(c.act_done, ev.at("hg.ln"))
        dve.tensor_tensor(lf[:], lf[:], clamp, ALU.add).then_inc(c.dve_done, ev.one("dve", "lf"))

    def gates_act(act):
        act.wait_ge(c.dve_done, ev.at("hg.small"))
        act.activation(lf[:], lf[:], ACT.Ln)
        act.activation(clamp, clamp, ACT.Ln).then_inc(c.act_done, ev.one("act", "hg.ln"))

    def again_pool(pool, h):
        starts = s.again[:].rearrange("p (b t) -> p b t", t=h)[:, :, 0:1]
        pool.memset(starts, 0.0).then_inc(c.pool_done, ev.one("pool", f"again{h}"))

    def sums_dve(dve):
        flat = lf[:].rearrange("p h t -> p (h t)")
        for tile, h in ((G, SEQ), (H, HG_CHUNK)):
            dve.wait_ge(c.dve_done, ev.at("lf"))
            dve.wait_ge(c.pool_done, ev.at(f"again{h}"))
            dve.tensor_tensor_scan(tile.rearrange("p h t -> p (h t)"), s.again[:], flat, 0.0, ALU.mult, ALU.add)\
                .then_inc(c.dve_done, ev.one("dve", f"prefix{h}"))

    def sums_pool(pool, h):
        tile = G if h == SEQ else H
        back = slice(HG_D, P)
        pool.wait_ge(c.dve_done, ev.at(f"prefix{h}"))
        pool.wait_ge(c.pool_done, ev.last("pool"))
        pool.tensor_tensor(tile[back], tile[back], lf[back], ALU.subtract)\
            .then_inc(c.pool_done, ev.one("pool", f"sums{h}"))
        pool.wait_ge(c.pool_done, ev.last("pool"))

    def border_dve(dve, j):
        p, h = j % 2, LEVELS[j]
        tile = (G if h >= HG_CHUNK else H).rearrange("p h t -> p (h t)").rearrange("p (b t) -> p b t", t=2 * h)
        dve.wait_ge(c.pool_done, ev.at(f"sums{SEQ if h >= HG_CHUNK else HG_CHUNK}"))
        if j >= 2:
            dve.wait_ge(c.pe_done, ev.at(f"level{j - 2}.product"))
        dve.tensor_tensor(K[p][:].rearrange("p h t -> p (h t)").rearrange("p (b t) -> p b t", t=2 * h), tile,
                          tile[:, :, h - 1:h].broadcast_to([P, HG_HEADS * SEQ // (2 * h), 2 * h]), ALU.subtract)\
            .then_inc(c.dve_done, ev.one("dve", f"border{j}"))

    def exp_act(act, j):
        p, h = j % 2, LEVELS[j]
        act.wait_ge(c.dve_done, ev.at(f"border{j}"))
        both = K[p][:].rearrange("p h t -> p (h t)").rearrange("p (b two t) -> p b two t", two=2, t=h)
        for side, sign in ((0, -1.0), (1, 1.0)):
            last = act.activation(both[:, :, side, :], both[:, :, side, :], ACT.Exp, scale=sign)
        last.then_inc(c.act_done, ev.one("act", f"exp{j}"))

    def scale_pool(pool, j):
        p, h = j % 2, LEVELS[j]
        if j >= 2:
            pool.wait_ge(c.pe_done, ev.at(f"level{j - 2}.product"))
        else:
            pool.wait_ge(c.act_done, ev.at(f"blk{KV1}.out"))
        pool.wait_ge(c.pool_done, ev.last("pool"))
        for direction in range(2):
            pool.memset(other_halves(Q[p], direction, h), 0.0)
        pool.wait_ge(c.act_done, ev.at(f"exp{j}"))
        for direction in range(2):
            pool.tensor_tensor(halves(Q[p], direction, h), halves(K[p], direction, h), halves(q2, direction, h),
                               ALU.mult)
        for direction in range(2):
            keys = other_halves(K[p], direction, h)
            last = pool.tensor_tensor(keys, keys, other_halves(kk, direction, h), ALU.mult)
        last.then_inc(c.pool_done, ev.one("pool", f"scaled{j}"))
        pool.wait_ge(c.pool_done, ev.last("pool"))

    def product_pe(pe, j):
        p, h = j % 2, LEVELS[j] if j != DIAGONAL else 0
        if j == DIAGONAL:
            pe.wait_ge(c.dve_done, ev.at("hg.k"))
            pe.wait_ge(c.act_done, ev.at(f"blk{HQ}.out"))
        else:
            pe.wait_ge(c.pool_done, ev.at(f"scaled{j}"))
            pe.wait_ge(c.dve_done, ev.at(f"level{j - 1 if j else DIAGONAL}"))
        Kj, Qj = (K[p], Q[p]) if h else (kk, q2)
        for head in range(HG_HEADS):
            for t in range(TT):
                i, tq = 2 * head + t, (1 - t if h == P else t)
                last = pe.matmul(c.psum[:, 2 + i // 4, (i % 4) * P:(i % 4 + 1) * P],
                                 Kj[:, head, t * P:(t + 1) * P], Qj[:, head, tq * P:(tq + 1) * P],
                                 start=True, stop=True)
        last.then_inc(c.pe_done, ev.one("pe", f"level{j}.product"))

    def keep_dve(dve, j):
        product = c.psum[:, 2:4, :].rearrange("p b (i t) -> p (b i) t", t=P)
        dve.wait_ge(c.pe_done, ev.at(f"level{j}.product"))
        if j == DIAGONAL:
            ins = dve.tensor_copy(near[:], product)
        elif j == 0:
            ins = dve.tensor_copy(far[:], product)
        else:
            dve.wait_ge(c.dve_done, ev.at(f"level{j - 1 if j > 1 else DIAGONAL}"))
            ins = dve.copy_predicated(near[:], s.block_mask[:, j - 1:j, :].broadcast_to([P, HG_HEADS * TT, P]),
                                      product)
        ins.then_inc(c.dve_done, ev.one("dve", f"level{j}"))

    def weigh_pe(pe):
        pe.wait_ge(c.dve_done, ev.at(f"level{len(LEVELS) - 1}"))
        pe.wait_ge(c.act_done, ev.at(f"blk{HV}.out"))
        out = c.psum[:, 2, :].rearrange("p (t n) -> p t n", t=TT)
        for head in range(HG_HEADS):
            e = slice(head * HG_D, (head + 1) * HG_D)
            for t in range(TT):
                pe.matmul(out[:, t, e], near[:, 2 * head + t, :], hv[:, t, e], start=True, stop=False)
                last = pe.matmul(out[:, t, e], far[:, 2 * head + 1 - t, :], hv[:, 1 - t, e], start=False, stop=True)
        last.then_inc(c.pe_done, ev.one("pe", "hg.o"))

    by_head = ("p (t h) -> p t h", dict(t=TT))
    mem_heads = kv_mem[:].rearrange("p t (h e) -> p t h e", h=XA_HEADS)
    xq = conf_out[:].rearrange("p t (h e) -> p t h e", h=XA_HEADS)

    def cat_part(group):
        return cat[:, :, group * GROUP:(group + 1) * GROUP]

    def heads_of(view):
        return view.rearrange("p t (h e) -> p t h e", e=HG_D)

    def head_norm_dve(dve, tag, view, gain, after):
        sq = squares[:, 0:TT * GROUP].rearrange("p (t h e) -> p t h e", t=TT, e=HG_D)
        for name in after:
            dve.wait_ge(*ev.when(c, name))
        rms_sum(dve, tag, view, sq, 8, by_head)
        dve.wait_ge(c.pool_done, ev.at(f"{tag}.factor"))
        fb = factor[:, 0:8].rearrange("p (t h) -> p t h", t=TT).unsqueeze(3).broadcast_to([P, TT, 4, HG_D])
        dve.tensor_tensor(view, view, fb, ALU.mult).then_inc(c.dve_done, ev.one("dve", f"{tag}.scaled"))
        dve.wait_ge(c.dve_done, ev.at(f"{tag}.scaled"))
        gb = bc[gain][:].unsqueeze(1).unsqueeze(1).broadcast_to([P, TT, 4, HG_D])
        dve.tensor_tensor(view, view, gb, ALU.mult).then_inc(c.dve_done, ev.one("dve", f"{tag}.normed"))

    def hg_sum_dve(dve):
        o = heads_of(cat_part(1))
        sq = squares[:, 0:TT * GROUP].rearrange("p (t h e) -> p t h e", t=TT, e=HG_D)
        dve.wait_ge(c.act_done, ev.at("hg.copied"))
        dve.wait_ge(c.pe_done, ev.at(f"level{len(LEVELS) - 1}.product"))
        rms_sum(dve, "hgn", o, sq, 8, by_head)

    def hg_norm_dve(dve):
        o = heads_of(cat_part(1))
        dve.wait_ge(c.pool_done, ev.at("hgn.factor"))
        fb = factor[:, 0:8].rearrange("p (t h) -> p t h", t=TT).unsqueeze(3).broadcast_to([P, TT, HG_HEADS, HG_D])
        dve.tensor_tensor(o, o, fb, ALU.mult).then_inc(c.dve_done, ev.one("dve", "hgn.scaled"))
        dve.wait_ge(c.dve_done, ev.at("hgn.scaled"))
        dve.tensor_tensor(cat_part(1), cat_part(1), bc["onorm_g"][:].unsqueeze(1).broadcast_to(
            [P, TT, GROUP]), ALU.mult).then_inc(c.dve_done, ev.one("dve", "hgn.gained"))
        dve.wait_ge(c.dve_done, ev.at("hgn.gained"))
        dve.tensor_tensor(cat_part(1), cat_part(1), hg[:], ALU.mult).then_inc(c.dve_done, ev.one("dve", "cat1"))


    def low_act(act):
        act.wait_ge(c.act_done, ev.at(f"blk{CKV}.out"))
        for n in range(4):
            t, at, width = n % 2, COLS * (n // 2), (COLS, P)[n // 2]
            if n:
                act.wait_ge(c.act_done, ev.at(f"low.ss{n - 1}"))
            act.activation(scratch[:, 0:width], cqkv[:, t, at:at + width], ACT.Square,
                           accum_out=c.ss[:, 8 + n:9 + n]).then_inc(c.act_done, ev.one("act", f"low.ss{n}"))

    def low_pool(pool):
        pool.wait_ge(c.act_done, ev.at("low.ss3"))
        rms_factors(c, pool, "lowq", slice(8, 10), GROUP, RMS_EPS)
        rms_factors(c, pool, "lowkv", slice(10, 12), P, RMS_EPS)

    def low_dve(dve):
        dve.wait_ge(c.pool_done, ev.at("lowkv.rstd"))
        wait_params(c, dve, "small", SMALL)
        for n in range(4):
            t, at, width = n % 2, COLS * (n // 2), (COLS, P)[n // 2]
            v = cqkv[:, t, at:at + width]
            dve.scalar_tensor_tensor(v, v, c.rstd[:, 8 + n:9 + n], bc[("qa_g", "kva_g")[n // 2]][:],
                                     ALU.mult, ALU.mult).then_inc(c.dve_done, ev.one("dve", f"low.n{n}"))

    def low_pe(pe):
        pe.wait_ge(c.dve_done, ev.at("low.n3"))
        pe.wait_ge(c.dve_done, ev.at("taps.out"))
        for t in range(TT):
            for k in range(3):
                last = pe.transpose(c.psum[:, 6 + t, k * P:(k + 1) * P], cqkv[:, t, k * P:(k + 1) * P], c.ident[:])
            last.then_inc(c.pe_done, ev.one("pe", f"low.turned{t}"))

    def low_split(eng, name, t):
        src = c.psum[:, 6 + t, 0:3 * P].rearrange("p (k t) -> p k t", k=3)
        ts = slice(t * P, (t + 1) * P)
        if name == "act":
            eng.wait_ge(c.pe_done, ev.at(f"low.turned{t}"))
            eng.activation(low_hi[:, :, ts], src, ACT.Copy).then_inc(c.act_done, ev.one("act", f"low.hi{t}"))
        else:
            eng.wait_ge(c.act_done, ev.at(f"low.hi{t}"))
            eng.tensor_tensor(low_lo[:, :, ts], src, low_hi[:, :, ts].bitcast(F32), ALU.subtract)\
                .then_inc(c.dve_done, ev.one("dve", f"low.lo{t}"))

    def up_pe(pe):
        slot = UP % SLOTS
        pe.wait_ge(c.act_done, ev.at(f"blk{UP - 1}.out"))
        pe.wait_ge(c.dve_done, ev.at("low.lo1"))
        q_hi, q_lo = (w[slot][:, 0:UP_Q].rearrange("p (kt n) -> p kt n", kt=2) for w in (c.w_hi, c.w_lo))
        k_hi, k_lo = (w[slot][:, UP_Q:UP_Q + 512].rearrange("p (kt n) -> p kt n", kt=1) for w in (c.w_hi, c.w_lo))
        tokens_by_features(pe, [c.psum[:, t, 0:MLA_HEADS * QK] for t in range(TT)], q_hi, q_lo, low_hi, low_lo, 2)
        tokens_by_features(pe, [c.psum[:, 6 + t, :] for t in range(TT)], k_hi, k_lo, low_hi[:, 2:3, :],
                           low_lo[:, 2:3, :], 1).then_inc(c.w_used[slot], 1)

    def keys_pool(pool):
        pool.wait_ge(c.act_done, ev.at(f"blk{UP}.out"))
        pool.wait_ge(c.act_done, ev.at(f"blk{CKV}.out"))
        for t in range(TT):
            hs = slice(t * MLA_HEADS, (t + 1) * MLA_HEADS)
            pool.tensor_copy(qk[:, 1, hs, 0:NOPE],
                             kv_up[:, t, :].rearrange("p (h n) -> p h n", h=MLA_HEADS)[:, :, 0:NOPE])
            last = pool.tensor_copy(qk[:, 1, hs, NOPE:QK], cqkv[:, t, COLS + P:COLS + P + ROPE].unsqueeze(1)
                                    .broadcast_to([P, MLA_HEADS, ROPE]))
        last.then_inc(c.pool_done, ev.one("pool", "keys"))

    def qk_sums_dve(dve):
        dve.wait_ge(c.pool_done, ev.at("keys"))
        dve.wait_ge(c.pe_done, ev.at("low.turned1"))
        for w in range(2):
            if w:
                dve.wait_ge(c.dve_done, ev.at("qk0.sum"))
            sq = scratch[:, 0:8 * QK].rearrange("p (n e) -> p n e", e=QK)
            dve.tensor_tensor(sq, qk[:, w, :, :], qk[:, w, :, :], ALU.mult)\
                .then_inc(c.dve_done, ev.one("dve", f"qk{w}.sq"))
            dve.wait_ge(c.dve_done, ev.at(f"qk{w}.sq"))
            dve.tensor_reduce(sq_sum[:, 8 * w:8 * w + 8].unsqueeze(2), sq, AX_X, ALU.add)\
                .then_inc(c.dve_done, ev.one("dve", f"qk{w}.sum"))

    def qk_scale_dve(dve):
        dve.wait_ge(c.pool_done, ev.at("qk.factor"))
        for w in range(2):
            v = qk[:, w, :, :]
            dve.tensor_tensor(v, v, factor[:, 8 * w:8 * w + 8].unsqueeze(2).broadcast_to([P, 8, QK]), ALU.mult)\
                .then_inc(c.dve_done, ev.one("dve", f"qk{w}.scaled"))
        for w in range(2):
            v = qk[:, w, :, :]
            dve.wait_ge(c.dve_done, ev.at(f"qk{w}.scaled"))
            dve.tensor_tensor(v, v, bc[("qn_g", "kn_g")[w]][:].unsqueeze(1).broadcast_to([P, 8, QK]), ALU.mult)\
                .then_inc(c.dve_done, ev.one("dve", f"qk{w}.normed"))

    def qk_power_pool(pool):
        pool.wait_ge(c.dve_done, ev.at("qk1.sum"))
        pool.tensor_scalar(factor[:], sq_sum[:], 1.0 / QK, RMS_EPS, ALU.mult, ALU.add)\
            .then_inc(c.pool_done, ev.one("pool", "qk.meansq"))
        pool.wait_ge(c.pool_done, ev.at("qk.meansq"))
        pool.tensor_tensor(factor[:], factor[:], c.half_power[:], ALU.pow)\
            .then_inc(c.pool_done, ev.one("pool", "qk.factor"))

    def rope_pool(pool, w):
        n = ROPE // 2
        v = qk[:, w, :, :].rearrange("p (t h) e -> p t h e", t=TT)
        x1, x2 = v[:, :, :, NOPE:NOPE + n], v[:, :, :, NOPE + n:QK]
        cos, sin = (t[:].unsqueeze(2).broadcast_to([P, TT, MLA_HEADS, n]) for t in (s.cos, s.sin))
        tmp = [scratch[:, i * 128:(i + 1) * 128].rearrange("p (t h e) -> p t h e", t=TT, h=MLA_HEADS)
               for i in range(4)]
        pool.wait_ge(c.dve_done, ev.at(f"qk{w}.normed"))
        pool.wait_ge(c.dve_done, ev.at("qk1.sum"))
        if w:
            pool.wait_ge(c.pool_done, ev.at("rotated0"))
        for i, (x, cs) in enumerate(((x1, cos), (x2, sin), (x2, cos), (x1, sin))):
            pool.tensor_tensor(tmp[i], x, cs, ALU.mult).then_inc(c.pool_done, ev.one("pool", f"rope{w}.{i}"))
        pool.wait_ge(c.pool_done, ev.at(f"rope{w}.3"))
        pool.tensor_tensor(x1, tmp[0], tmp[1], ALU.subtract)
        pool.tensor_tensor(x2, tmp[2], tmp[3], ALU.add).then_inc(c.pool_done, ev.one("pool", f"rotated{w}"))

    def turn_heads_pe(pe, tag, view, width, after, banks):
        for name in after:
            pe.wait_ge(*ev.when(c, name))
        for g in range(2):
            for j in range(2):
                for t in range(TT):
                    at = (2 * j + t) * P
                    last = pe.transpose(c.psum[0:width, banks[g], at:at + P], view(t, 2 * g + j), c.ident[:])
            last.then_inc(c.pe_done, ev.one("pe", f"{tag}.turned{g}"))

    def turn_heads_out(eng, tag, dst, width, banks, g, after=()):
        eng.wait_ge(c.pe_done, ev.at(f"{tag}.turned{g}"))
        for name in after:
            eng.wait_ge(*ev.when(c, name))
        eng.activation(dst[0:width, 2 * g:2 * g + 2, :].rearrange("p h t -> p (h t)"),
                       c.psum[0:width, banks[g], :], ACT.Copy).then_inc(c.act_done, ev.one("act", f"{tag}.T{g}"))

    def attention(tag, qT, kT, width, value, out, ready, pe_too=None, act_too=None, dve_too=None):
        scale = width ** -0.5

        @block.tensor
        def _(pe):
            for name in ready:
                pe.wait_ge(*ev.when(c, name))
            for step in range(XA_HEADS + 2):
                h = step
                if h < XA_HEADS:
                    if h >= 2:
                        pe.wait_ge(c.act_done, ev.at(f"{tag}.p{h - 2}"))
                    for t in range(TT):
                        last = pe.matmul(two(4 + h % 2)[:, t, :], qT[0:width, h, t * P:(t + 1) * P],
                                         kT[0:width, h, :], start=True, stop=True)
                    last.then_inc(c.pe_done, ev.one("pe", f"{tag}.s{h}"))
                if tag == "xa" or step >= 2:
                    keep_warm(c, pe, 3, HEAD_WARM)
                h = step - 1
                if 0 <= h < XA_HEADS:
                    pe.wait_ge(c.act_done, ev.at(f"{tag}.p{h}"))
                    if h:
                        pe.wait_ge(c.dve_done, ev.at(f"{tag}.pT{h - 1}"))
                    for k in range(TT):
                        for t in range(TT):
                            at = (2 * k + t) * P
                            last = pe.transpose(c.psum[:, 6, at:at + P], probs[:, t, k * P:(k + 1) * P], c.ident[:])
                    last.then_inc(c.pe_done, ev.one("pe", f"{tag}.turned{h}"))
                h = step - 2
                if 0 <= h < XA_HEADS:
                    pe.wait_ge(c.dve_done, ev.at(f"{tag}.pT{h}"))
                    for t in range(TT):
                        for k in range(TT):
                            last = pe.matmul(two(7)[:, t, h * HG_D:(h + 1) * HG_D],
                                             probsT[:, k, t * P:(t + 1) * P], value(h, k),
                                             start=(k == 0), stop=(k == TT - 1))
                    last.then_inc(c.pe_done, ev.one("pe", f"{tag}.o{h}"))
                if pe_too:
                    pe_too(pe, step)

        @block.scalar
        def _(act):
            for h in range(XA_HEADS):
                act.wait_ge(c.dve_done, ev.at(f"{tag}.neg{h}"))
                if h:
                    act.wait_ge(c.pe_done, ev.at(f"{tag}.turned{h - 1}"))
                for t in range(TT):
                    last = act.activation(probs[:, t, :], two(4 + h % 2)[:, t, :], ACT.Exp, scale=scale,
                                          bias=row_max[:, t, h:h + 1], accum_out=row_sum[:, t, h:h + 1])
                last.then_inc(c.act_done, ev.one("act", f"{tag}.p{h}"))
                if act_too:
                    act_too(act, h)

        @block.vector
        def _(dve):
            for h in range(XA_HEADS + 1):
                if h < XA_HEADS:
                    dve.wait_ge(c.pe_done, ev.at(f"{tag}.s{h}"))
                    m = row_max[:, 0:TT, h:h + 1]
                    dve.tensor_reduce(m, two(4 + h % 2), AX_X, ALU.max)\
                        .then_inc(c.dve_done, ev.one("dve", f"{tag}.max{h}"))
                    dve.wait_ge(c.dve_done, ev.at(f"{tag}.max{h}"))
                    dve.tensor_scalar(m, m, -scale, None, ALU.mult)\
                        .then_inc(c.dve_done, ev.one("dve", f"{tag}.neg{h}"))
                    if dve_too:
                        dve_too(dve, h)
                if h:
                    dve.wait_ge(c.pe_done, ev.at(f"{tag}.turned{h - 1}"))
                    if h > 1:
                        dve.wait_ge(c.pe_done, ev.at(f"{tag}.o{h - 2}"))
                    dve.tensor_copy(probsT.rearrange("p k t -> p (k t)"), c.psum[:, 6, :])\
                        .then_inc(c.dve_done, ev.one("dve", f"{tag}.pT{h - 1}"))
            dve.wait_ge(c.act_done, ev.at(f"{tag}.p{XA_HEADS - 1}"))
            dve.reciprocal(row_sum[:, 0:TT, :], row_sum[:, 0:TT, :]).then_inc(c.dve_done, ev.one("dve", f"{tag}.rden"))
            dve.wait_ge(c.dve_done, ev.at(f"{tag}.rden"))
            dve.wait_ge(c.pe_done, ev.at(f"{tag}.o{XA_HEADS - 1}"))
            dve.tensor_tensor(heads_of(out), heads_of(two(7)),
                              row_sum[:, 0:TT, :].unsqueeze(3).broadcast_to([P, TT, XA_HEADS, HG_D]), ALU.mult)\
                .then_inc(c.dve_done, ev.one("dve", f"{tag}.out"))


    def conv_dve(dve, tag, padded, out, tap0, count, part):
        for k in part:
            for ct in range(2):
                src, w = padded[:, ct, k:k + SEQ], taps[:, ct, tap0 + k:tap0 + k + 1]
                if k == 0:
                    bias = taps[:, ct, tap0 + count:tap0 + count + 1]
                    ins = dve.tensor_scalar(out[:, ct, :], src, w, bias, ALU.mult, ALU.add)
                else:
                    dve.wait_ge(c.dve_done, ev.at(f"{tag}.{k - 1}.{ct}"))
                    ins = dve.scalar_tensor_tensor(out[:, ct, :], src, w, out[:, ct, :], ALU.mult, ALU.add)
                ins.then_inc(c.dve_done, ev.one("dve", f"{tag}.{k}.{ct}"))

    def turn_tiles_pe(pe, tag, source, b, after):
        for name in after:
            pe.wait_ge(*ev.when(c, name))
        for t in range(TT):
            for ct in range(2):
                last = pe.transpose(c.psum[:, b, (2 * t + ct) * P:(2 * t + ct + 1) * P],
                                    source[:, ct, t * P:(t + 1) * P], c.ident[:])
        last.then_inc(c.pe_done, ev.one("pe", f"{tag}.turned"))

    def conf_stats_dve(dve):
        dve.wait_ge(c.pe_done, ev.at("conf.turned"))
        for t in range(TT):
            last = dve.bn_stats(stats[:, t, :], two(1)[:, t, :])
        last.then_inc(c.dve_done, ev.one("dve", "conf.stats"))
        dve.wait_ge(c.dve_done, ev.at("conf.stats"))
        for t in range(TT):
            last = dve.bn_aggr(mean_var[:, t, :], stats[:, t, :])
        last.then_inc(c.dve_done, ev.one("dve", "conf.mean_var"))

    def conf_norm_dve(dve):
        dve.wait_ge(c.pool_done, ev.at("conf.rstd"))
        dve.wait_ge(c.pool_done, ev.at("rotated1"))
        for t in range(TT):
            dve.tensor_scalar(cat_part(0)[:, t, :], two(1)[:, t, :], mean_var[:, t, 0:1],
                              c.rstd[:, 4 + t:5 + t], ALU.subtract, ALU.mult)\
                .then_inc(c.dve_done, ev.one("dve", f"conf.n{t}"))
        dve.wait_ge(c.dve_done, ev.at("conf.n1"))
        dve.tensor_tensor(cat_part(0), cat_part(0), bc["ln_g"][:].unsqueeze(1).broadcast_to(
            [P, TT, GROUP]), ALU.mult).then_inc(c.dve_done, ev.one("dve", "conf.g"))
        dve.wait_ge(c.dve_done, ev.at("conf.g"))
        dve.tensor_tensor(cat_part(0), cat_part(0), bc["ln_b"][:].unsqueeze(1).broadcast_to(
            [P, TT, GROUP]), ALU.add).then_inc(c.dve_done, ev.one("dve", "conf.b"))

    def conf_pool(pool):
        pool.wait_ge(c.dve_done, ev.at("conf.mean_var"))
        pool.tensor_scalar(c.rstd[:, 4:4 + TT], mean_var[:, :, 1], RMS_EPS, None, ALU.add)\
            .then_inc(c.pool_done, ev.one("pool", "conf.var"))
        pool.wait_ge(c.pool_done, ev.at("conf.var"))
        pool.tensor_tensor(c.rstd[:, 4:4 + TT], c.rstd[:, 4:4 + TT], c.half_power[:, 0:TT],
                           ALU.pow).then_inc(c.pool_done, ev.one("pool", "conf.rstd"))

    with nc.Block() as block:
        @block.gpsimd
        def _(pool):
            load_gain(c, pool, "gain_post", dram["g_mem_2"][layer], [])
            load_gain(c, pool, "gain_pre", dram["g_mix_2"][layer], [])

        @block.sync
        def _(sp):
            sp.dma_start(mem, dram["mem_2"].rearrange("o (t p) n -> p (o t) n", p=P)).then_inc(c.mem_loaded, 16)
            for i in range(WO):
                slot = i % SLOTS
                if i == UP:
                    load_weights(c, sp, slot, i // SLOTS, False, dram["m_wuq_2"].rearrange(
                        "l (kt p) n -> l p kt n", p=P)[layer], c.stage[slot][:, 0:UP_Q].rearrange(
                        "p (kt n) -> p kt n", kt=2))
                    sp.dma_start(c.stage[slot][:, UP_Q:UP_Q + 512], dram["m_wukv_2"][layer])\
                      .then_inc(c.up_kv_loaded, 16)
                else:
                    load(sp, i, columns(c, "x_wkv_2" if i in (KV0, KV1) else "w_in_2", layer, first_col[i]))
            for i in range(4):
                load(sp, WO + i, rows(c, "w_out_2", layer, i))
            load(sp, XQ, columns(c, "x_wq_2", layer, 0))
            load(sp, XO, rows(c, "x_wo_2", layer, 0))

        @block.scalar
        def _(act):
            act.wait_ge(c.mem_loaded, 16)

        @block.vector
        def _(dve):
            dve.wait_ge(c.mem_loaded, 16)

        pre_norm(c, block, "mem", [[], []], 1, mem, ("gain_post", c.gain_post), (bT_hi, bT_lo),
                 split_between=[KV0], warm=START_WARM)

        TAPS = -(-CONF_TAPS // (WO - CG))

        def part_of_block(i):
            return UP_Q + 512 if i == UP else BLOCK

        def project(pe, i):
            if i == HQ:
                pe.wait_ge(c.dve_done, ev.at("mix.lo2"))
            if i >= 2:
                pe.wait_ge(c.act_done, ev.at(f"blk{i - 2}.out"))
            if i == UP + 1:
                pe.wait_ge(c.act_done, ev.at(f"blk{UP}.out"))
            wait_weights(c, pe, i)
            w_hi, w_lo = as_columns(c.w_hi[i % SLOTS]), as_columns(c.w_lo[i % SLOTS])
            a = (bT_hi, bT_lo) if i in (KV0, KV1) else (c.aT_hi, c.aT_lo)
            if i == UP:
                up_pe(pe)
            elif i in by_tokens:
                late = (c.dve_done, ev.at("mem.lo3")) if i == KV0 else None
                tokens_by_features(pe, [two(i % 2)[:, t, :] for t in range(TT)], w_hi, w_lo, *a, KT, late=late)\
                    .then_inc(c.w_used[i % SLOTS], 1)
            else:
                late = (c.dve_done, ev.at("mix.lo3")) if i == HQ else None
                features_by_tokens(pe, two(i % 2), w_hi, w_lo, *a, late=late).then_inc(c.w_used[i % SLOTS], 1)

        @block.tensor
        def _(pe):
            pe.wait_ge(c.dve_done, ev.at("mem.lo1"))
            project(pe, KV0)

        pre_norm(c, block, "mix", [["mem.turned1"], ["mem.turned3"]], 1, banks=(2, 3, 4, 5), split_between=[HQ])
        split_next(c, block, ZF)

        @block.tensor
        def _(pe):
            for i in range(KV0 + 1, WO):
                project(pe, i)
                if i == ZB:
                    pe.wait_ge(c.dve_done, ev.at("lower"))
                    for ct in range(2):
                        last = pe.transpose(c.psum[:, 6, ct * 36:(ct + 1) * 36], taps_rows[:, ct * P:(ct + 1) * P],
                                            c.ident[0:36, 0:36])
                    last.then_inc(c.pe_done, ev.one("pe", "taps.turned"))
                if i == HV:
                    low_pe(pe)
                if i >= CA + 1:
                    product_pe(pe, i - CA - 2 if i > CA + 1 else DIAGONAL)
                if i == SX:
                    turn_heads_pe(pe, "q", lambda t, h: qk[:, 0, t * MLA_HEADS + h, :], QK,
                                  ["rotated0", f"blk{UP}.out"], (6, 7))
                if i == SB:
                    turn_heads_pe(pe, "k", lambda t, h: qk[:, 1, t * MLA_HEADS + h, :], QK, ["rotated1", "q.T1"],
                                  (6, 7))

        @block.scalar
        def _(act):
            for i in range(WO):
                used(act, i)
                src = two(i % 2)
                if i in (KV0, KV1):
                    half = slice(first_col[i], first_col[i] + COLS)
                    ins = act.activation(kv_mem[:, :, half], src, ACT.Copy)
                elif i == HQ:
                    for side in range(2):
                        for direction in range(2):
                            ins = act.activation(head_side(q2, direction, side),
                                                 src[side * HG_D:(side + 1) * HG_D, :, :], ACT.Copy)
                elif i in (ZF, ZB):
                    for side in range(2):
                        for tile, sign in ((f, 1.0), (kk, -1.0)):
                            ins = act.activation(head_side(tile, i - ZF, side),
                                                 src[side * HG_D:(side + 1) * HG_D, :, :], ACT.Sigmoid, scale=sign)
                elif i == CQ:
                    act.wait_ge(c.pe_done, ev.at("mix.turned3"))
                    ins = act.activation(cqkv[:, :, 0:COLS], src, ACT.Copy)
                elif i == CKV:
                    ins = act.activation(cqkv[:, :, COLS:COLS + P + ROPE], src[:, :, CKV_AT:COLS], ACT.Copy)
                elif i == HV:
                    ins = act.activation(hv[:], src, ACT.Copy)
                elif i == HG:
                    ins = act.activation(hg[:], src, ACT.Silu)
                elif i == UP:
                    for t in range(TT):
                        act.activation(qk[:, 0, t * MLA_HEADS:(t + 1) * MLA_HEADS, :], c.psum[:, t, 0:MLA_HEADS * QK]
                                       .rearrange("p (h e) -> p h e", h=MLA_HEADS), ACT.Copy)
                        ins = act.activation(kv_up[:, t, :], c.psum[:, 6 + t, :], ACT.Copy)
                elif i == CA:
                    ins = act.activation(conf_out[:], src, ACT.Copy)
                elif i == CG:
                    act.wait_ge(c.pool_done, ev.at("padding"))
                    ins = act.activation(conf[:, :, 15:15 + SEQ], src, ACT.Sigmoid)
                elif i == SC:
                    ins = act.activation(short_out[:], src, ACT.Copy)
                elif i == SX:
                    ins = act.activation(short[:, :, 1:1 + SEQ], src, ACT.Copy)
                if i != SB:
                    ins.then_inc(c.act_done, ev.one("act", f"blk{i}.out"))
                if i + SLOTS == UP:
                    act.wait_ge(c.up_kv_loaded, 16)
                hi(c, act, i + SLOTS, part_of_block(i + SLOTS))
                if i == ZB:
                    gates_act(act)
                if i == CKV:
                    low_act(act)
                if i == HV:
                    for t in range(TT):
                        low_split(act, "act", t)
                if 0 <= i - CA < len(LEVELS):
                    exp_act(act, i - CA)
                if i == SB:
                    for g in range(2):
                        turn_heads_out(act, "q", mla_T[0], QK, (6, 7), g, [f"level{len(LEVELS) - 2}.product"])
                    for g in range(2):
                        turn_heads_out(act, "k", mla_T[1], QK, (6, 7), g)

        @block.vector
        def _(dve):
            for i in range(WO):
                lo(c, dve, i + SLOTS, part_of_block(i + SLOTS))
                j = i - CA
                if i == ZF:
                    wait_params(c, dve, "small", SMALL)
                    dve.tensor_copy(lower[:], s.lower[:, bass.ds(layer, 1), :].rearrange("p o h -> p (o h)"))\
                        .then_inc(c.dve_done, ev.one("dve", "lower"))
                if i == KV1:
                    dve.wait_ge(c.pe_done, ev.at("taps.turned"))
                    dve.tensor_copy(taps[:].rearrange("p c k -> p (c k)"), c.psum[:, 6, 0:72])\
                        .then_inc(c.dve_done, ev.one("dve", "taps.out"))
                if i == ZB:
                    gates_dve(dve)
                    sums_dve(dve)
                if 0 <= j < len(LEVELS):
                    border_dve(dve, j)
                if j >= 1:
                    keep_dve(dve, j - 2 if j > 1 else DIAGONAL)
                if i == CKV:
                    low_dve(dve)
                if i == HV:
                    for t in range(TT):
                        low_split(dve, "dve", t)
                if i == UP + 1:
                    qk_sums_dve(dve)
                if i == UP + 2:
                    qk_scale_dve(dve)
                if i == CG:
                    dve.wait_ge(c.act_done, ev.at(f"blk{CG}.out"))
                    dve.tensor_tensor(conf[:, :, 15:15 + SEQ], conf[:, :, 15:15 + SEQ],
                                      conf_out[:], ALU.mult).then_inc(c.dve_done, ev.one("dve", "conf.h"))
                if i >= CG:
                    first = TAPS * (i - CG)
                    if i == CG:
                        dve.wait_ge(c.dve_done, ev.at("conf.h"))
                        dve.wait_ge(c.dve_done, ev.at("taps.out"))
                    conv_dve(dve, "conf", conf, conf_out, 0, CONF_TAPS, range(first, min(first + TAPS, CONF_TAPS)))
                if i == SX:
                    dve.wait_ge(c.act_done, ev.at(f"blk{SX}.out"))
                    dve.tensor_tensor(short[:, :, 1:1 + SEQ], short[:, :, 1:1 + SEQ],
                                      short_out[:], ALU.mult).then_inc(c.dve_done, ev.one("dve", "short.h"))
                    dve.wait_ge(c.dve_done, ev.at("short.h"))
                    conv_dve(dve, "short", short, short_out, 32, SHORT_TAPS, range(SHORT_TAPS))
                if i == SB:
                    used(dve, SB)
                    dve.wait_ge(c.dve_done, ev.at(f"short.{SHORT_TAPS - 1}.0"))
                    dve.wait_ge(c.dve_done, ev.at(f"short.{SHORT_TAPS - 1}.1"))
                    dve.tensor_tensor(short_out[:], short_out[:], two(SB % 2), ALU.mult)\
                        .then_inc(c.dve_done, ev.one("dve", "short.y"))

        @block.gpsimd
        def _(pool):
            load_gain(c, pool, "gain_post", dram["g_branch_2"][layer], ["mem.xn1.1"])
            load_gain(c, pool, "gain_pre", dram["g_xq_2"][layer], ["mix.xn1.1"])
            pool.memset(conf[:], 0.0)
            pool.memset(short[:], 0.0).then_inc(c.pool_done, ev.one("pool", "padding"))
            small = c.params["small"]
            for name, source in (("qa_g", "m_qa_g_2"), ("kva_g", "m_kva_g_2"), ("qn_g", "m_qn_g_2"),
                                 ("kn_g", "m_kn_g_2"), ("ln_g", "a_ln_g_2"), ("ln_b", "a_ln_b_2"),
                                 ("onorm_g", "h_onorm_g_2"), ("xqn_g", "x_qn_g_2"), ("xkn_g", "x_kn_g_2")):
                pool.dma_start(bc[name][:], dram[source][layer].partition_broadcast(P)).then_inc(small, 16)
            pool.dma_start(taps_rows[0:31, :], dram["a_dw_w_2"][layer]).then_inc(small, 16)
            pool.dma_start(taps_rows[31:32, :], dram["a_dw_b_2"][layer].unsqueeze(0)).then_inc(small, 16)
            pool.dma_start(taps_rows[32:35, :], dram["c_dw_w_2"][layer]).then_inc(small, 16)
            pool.dma_start(taps_rows[35:36, :], dram["c_dw_b_2"][layer].unsqueeze(0)).then_inc(small, 16)
            pool.memset(s.again[:], 1.0).then_inc(c.pool_done, ev.one("pool", "ones"))
            pool.wait_ge(c.pool_done, ev.at("ones"))
            again_pool(pool, SEQ)
            pool.wait_ge(c.dve_done, ev.at(f"prefix{SEQ}"))
            again_pool(pool, HG_CHUNK)
            sums_pool(pool, SEQ)
            sums_pool(pool, HG_CHUNK)
            for j in range(len(LEVELS)):
                scale_pool(pool, j)
                if j == CKV - CA - 1:
                    low_pool(pool)
                if j == UP - CA:
                    keys_pool(pool)
                if j == UP + 1 - CA:
                    qk_power_pool(pool)
                if j == UP + 2 - CA:
                    rope_pool(pool, 0)
                    rope_pool(pool, 1)
            conf_pool(pool)
            rms_power(pool, "hgn", 8, HG_D)

        def mla_pe_too(pe, step):
            if step == 0:
                turn_tiles_pe(pe, "conf", conf_out, 1, [f"conf.{CONF_TAPS - 1}.{ct}" for ct in range(2)])
                turn_tiles_pe(pe, "short", short_out, 0, ["short.y"])
            elif step == 1:
                weigh_pe(pe)

        def mla_act_too(act, h):
            if h == 0:
                act.wait_ge(c.pe_done, ev.at("short.turned"))
                act.activation(cat_part(2), two(0), ACT.Copy).then_inc(c.act_done, ev.one("act", "cat2"))
            elif h == 1:
                act.wait_ge(c.pe_done, ev.at("hg.o"))
                act.activation(cat_part(1), two(2), ACT.Copy).then_inc(c.act_done, ev.one("act", "hg.copied"))
            elif h == MLA_HEADS - 1:
                act.wait_ge(c.dve_done, ev.at("conf.b"))
                act.activation(cat_part(0), cat_part(0), ACT.Silu).then_inc(c.act_done, ev.one("act", "cat0"))

        def mla_dve_too(dve, h):
            (conf_stats_dve, conf_norm_dve, hg_sum_dve, hg_norm_dve)[h](dve)

        attention("mla", mla_T[0], mla_T[1], QK,
                  lambda h, k: kv_up[:, k, 2 * NOPE * h + NOPE:2 * NOPE * (h + 1)], cat_part(3),
                  ["q.T1", "k.T1", "rotated1"], mla_pe_too, mla_act_too, mla_dve_too)

        def group(t, g):
            return cat[:, t, g * GROUP:(g + 1) * GROUP]

        @block.scalar
        def _(act):
            for name, gs in (("three", range(3)), ("mla", range(3, 4))):
                act.wait_ge(c.act_done, ev.last("act"))
                act.wait_ge(c.dve_done, ev.at("cat1" if name == "three" else "mla.out"))
                for g in gs:
                    for t in range(TT):
                        n = 2 * g + t
                        if n % 4 == 0 and n:
                            act.wait_ge(c.act_done, ev.last("act"))
                        act.activation(c.squares[:, n % 4 * GROUP:(n % 4 + 1) * GROUP], group(t, g), ACT.Square,
                                       accum_out=c.ss[:, n:n + 1]).then_inc(c.act_done, ev.one("act", f"group_ss{n}"))

        @block.gpsimd
        def _(pool):
            for name, ns in (("three", slice(0, 6)), ("mla", slice(6, 8))):
                pool.wait_ge(c.act_done, ev.at(f"group_ss{ns.stop - 1}"))
                rms_factors(c, pool, f"group.{name}", ns, GROUP, RMS_EPS)

        @block.vector
        def _(dve):
            wait_params(c, dve, "gain_post", 2)
            for g in range(4):
                dve.wait_ge(c.pool_done, ev.at("group.mla.rstd" if g == 3 else "group.three.rstd"))
                for t in range(TT):
                    dve.scalar_tensor_tensor(group(t, g), group(t, g), c.rstd[:, 2 * g + t:2 * g + t + 1],
                                             c.gain_post[:, g * GROUP:(g + 1) * GROUP], ALU.mult, ALU.mult)\
                        .then_inc(c.dve_done, ev.one("dve", f"cat.n{2 * g + t}"))

        @block.tensor
        def _(pe):
            keep_warm(c, pe, 3, WARM)

        transpose_split(c, block, "cat", cat, KT, [["cat.n2", "hg.copied", "short.y"], ["cat.n3"], ["cat.n6"],
                                                   ["cat.n7"]], [0, 1, 2, 3], by_columns=True)

        @block.tensor
        def _(pe):
            pe.wait_ge(c.dve_done, ev.at("mla.out"))
            pe.wait_ge(c.dve_done, ev.at("cat.lo1"))
            for i in range(4):
                n = WO + i
                if i == 2:
                    pe.wait_ge(c.dve_done, ev.at("cat.lo3"))
                wait_weights(c, pe, n)
                row_block(c, pe, as_rows(c.w_hi[n % SLOTS]), as_rows(c.w_lo[n % SLOTS]),
                          c.aT_hi[:, 2 * i:2 * i + 2, :], c.aT_lo[:, 2 * i:2 * i + 2, :], i == 0,
                          "wo" if i == 3 else None)\
                    .then_inc(c.w_used[n % SLOTS], 1)

        @block.scalar
        def _(act):
            for n in range(WO, XQ - 1):
                hi(c, act, n + SLOTS)

        @block.vector
        def _(dve):
            for n in range(WO, XQ - 1):
                lo(c, dve, n + SLOTS)
                if n == WO:
                    head_norm_dve(dve, "xk", mem_heads[:, :, :, 0:XA_D], "xkn_g", [f"blk{KV1}.out", "cat1"])

        @block.gpsimd
        def _(pool):
            rms_power(pool, "xk", 8, XA_D)
        add_to_x(c, block, "wo", WO // SLOTS + 2, 0)

        @block.tensor
        def _(pe):
            turn_heads_pe(pe, "xk", lambda t, h: mem_heads[:, t, h, :], 2 * XA_D, ["xk.normed", "cat.lo3"], (2, 3))

        @block.scalar
        def _(act):
            for g in range(2):
                turn_heads_out(act, "xk", mem_T[1], XA_D, (2, 3), g)
        pre_norm(c, block, "xq", [["wo.x0"], ["wo.x1", "xk.T1"]], 2, warm=WARM // 2, warm_after=["xk.T1"])
        split_next(c, block, XQ - 1 + SLOTS)

        @block.gpsimd
        def _(pool):
            load_gain(c, pool, "gain_pre", dram["g_ffn_2"][layer], ["xq.xn1.1"])
            rms_power(pool, "xqh", 8, XA_D)

        @block.tensor
        def _(pe):
            pe.wait_ge(c.dve_done, ev.at("xq.lo1"))
            wait_weights(c, pe, XQ)
            slot = XQ % SLOTS
            tokens_by_features(pe, [two(0)[:, t, :] for t in range(TT)], as_columns(c.w_hi[slot]),
                               as_columns(c.w_lo[slot]), c.aT_hi, c.aT_lo, KT, late=(c.dve_done, ev.at("xq.lo3")))\
                .then_inc(c.w_used[slot], 1)
            turn_tiles_pe(pe, "xq_h", conf_out, 2, ["xqh.normed"])

        @block.scalar
        def _(act):
            used(act, XQ)
            act.activation(conf_out[:], two(0), ACT.Copy).then_inc(c.act_done, ev.one("act", "xq.out"))
            hi(c, act, XQ + SLOTS)
            act.wait_ge(c.pe_done, ev.at("xq_h.turned"))
            for side in range(2):
                last = act.activation(mem_T[0][0:XA_D, side:side + 3:2, :], two(2)[side * XA_D:(side + 1) * XA_D],
                                      ACT.Copy)
            last.then_inc(c.act_done, ev.one("act", "xq_h.T"))

        @block.vector
        def _(dve):
            head_norm_dve(dve, "xqh", xq, "xqn_g", ["xq.out"])
            lo(c, dve, XQ + SLOTS)
        attention("xa", mem_T[0], mem_T[1], XA_D,
                  lambda h, k: kv_mem[:, k, 2 * XA_D * h + XA_D:2 * XA_D * (h + 1)], short_out[:],
                  ["xq_h.T", "xk.T1", "wo.x1"])
        transpose_split(c, block, "xo", short_out, 2, [["xa.out"], ["xa.out"]], [2, 3], low_hi, low_lo)

        @block.tensor
        def _(pe):
            pe.wait_ge(c.dve_done, ev.at("xo.lo1"))
            wait_weights(c, pe, XO)
            slot = XO % SLOTS
            row_block(c, pe, as_rows(c.w_hi[slot]), as_rows(c.w_lo[slot]), low_hi[:, 0:2, :], low_lo[:, 0:2, :],
                      True, "xo_x").then_inc(c.w_used[slot], 1)

        add_to_x(c, block, "xo_x", XO // SLOTS + 1, XO % SLOTS)

        pre_norm(c, block, "ffn", [["xo_x.x0"], ["xo_x.x1"]], 3, warm=WARM // 2)
        split_next(c, block, XO + SLOTS)
        ffn(c, block, "ffn", "f_w13_2", "f_w2_2", layer, FFN_USE, 0, True, ["xo_x.x1"])
        add_to_x(c, block, "ffn", FFN_USE + FF_STEPS)


def constants(c, block, window_mask, causal_T):
    @block.gpsimd
    def _(pool):
        done = c.setup_done
        pool.memset(c.ident[:], 0.0)
        pool.memset(c.zeros[:], 0.0)
        pool.memset(c.half_power[:], -0.5)
        pool.memset(window_mask[:], 0.0)
        pool.memset(causal_T[:], 1.0).then_inc(done, 1)
        pool.wait_ge(done, 1)
        pool.affine_select(out=c.ident[:], in_=c.ident[:], compare_op=ALU.not_equal, fill=1.0, base=0,
                           pattern=[[-1, P]], channel_multiplier=1)
        for part, base, step, sign in ((0, 0, -1, 1), (1, -1, 1, -1), (2, 0, -1, 1)):
            own = window_mask[:, part * P:(part + 1) * P]
            pool.affine_select(out=own, in_=own, compare_op=ALU.is_ge, fill=MASKED, base=base,
                               pattern=[[step, P]], channel_multiplier=sign)
        pool.affine_select(out=causal_T[:], in_=causal_T[:], compare_op=ALU.is_ge, fill=0.0, base=0,
                           pattern=[[1, P]], channel_multiplier=-1).then_inc(done, 1)
        pool.wait_ge(done, 2)


def program(nc, dram, out, known):
    with ExitStack() as ctx:
        c = allocate(nc, ctx, dram, known)
        token_major = dram["x"].rearrange("o (t p) n -> p (o t) n", p=P)
        with ExitStack() as first:
            window_mask = first.enter_context(nc.sbuf_tensor("window_mask", [P, 3 * P], F32))
            causal_T = first.enter_context(nc.sbuf_tensor("causal_T", [P, P], F32))
            with nc.Block() as block:
                @block.sync
                def _(sp):
                    sp.dma_start(c.x[:], token_major).then_inc(c.x_loaded, 16)
                    sp.wait_ge(c.x_loaded, 16)
                constants(c, block, window_mask, causal_T)
            start_layers(c, gain_pre=3, gain_post=3, small=5)
            with nc.Fori(0, DEPTH) as layer:
                first_block_layer(c, layer, (window_mask, causal_T))
                clear_layer(c)
        with ExitStack() as second:
            s = second_tiles(c, second)
            second_setup(c, s)
            start_layers(c, gain_pre=3, gain_post=2, small=SMALL)
            with nc.Fori(0, DEPTH) as layer:
                second_block_layer(c, s, layer)
                clear_layer(c)
        with nc.Block() as block:
            @block.sync
            def _(sp):
                sp.dma_start(out.rearrange("o (t p) n -> p (o t) n", p=P), c.x[:]).then_inc(c.stored, 16)
                sp.wait_ge(c.stored, 16)
        return c.ev.table


_SHAPE = (1, SEQ, D)


def kernel(**inputs):
    from concourse.bacc import Bacc
    from concourse.bass_utils import run_bass_kernel_spmd

    inputs = {name: np.ascontiguousarray(a) for name, a in inputs.items()}

    def build(known):
        nc = Bacc("TRN2", target_bir_lowering=False, num_devices=1)
        dram = {name: nc.dram_tensor(f"in_{name}", a.shape, mybir.dt.from_np(a.dtype), kind="ExternalInput").ap()
                for name, a in inputs.items()}
        out = nc.dram_tensor("y", _SHAPE, F32, kind="ExternalOutput").ap()
        return nc, program(nc, dram, out, known)

    _, counts = build(None)
    nc, _ = build(counts)
    result = run_bass_kernel_spmd(nc, [{f"in_{name}": a for name, a in inputs.items()}], core_ids=[0])
    return result.results[0]["y"]
```
